# Optimizing a Trainium2 kernel written in Bass

```python
import math
import jax, jax.numpy as jnp
from jax import lax
import numpy as np

D_MODEL = 1024
BATCH = 1
SEQ = 1024
DEPTH = 1

HEAD_DIM = 64
N_MIX_GROUPS = 4
GROUP_WIDTH = D_MODEL // N_MIX_GROUPS
HEADS_PER_GROUP = GROUP_WIDTH // HEAD_DIM
D_MIX = GROUP_WIDTH * N_MIX_GROUPS
CHUNK = 64
Q_BLOCK = 128
CONV_W = 4
LRU_C = 8.0
MEM_LEN = 256
MEM_HEADS = 4
MEM_HEAD_DIM = 64
MEM_WIDTH = MEM_HEADS * MEM_HEAD_DIM
N_EXPERT_GROUPS = 4
EXPERTS_PER_GROUP = 8
N_EXPERTS = N_EXPERT_GROUPS * EXPERTS_PER_GROUP
TOP_K_IN_GROUP = 2
D_EXPERT = 256
EPS = 1e-6

COL_SIZES = (
    GROUP_WIDTH, GROUP_WIDTH, GROUP_WIDTH, GROUP_WIDTH,
    GROUP_WIDTH, GROUP_WIDTH, GROUP_WIDTH, HEADS_PER_GROUP,
    GROUP_WIDTH, GROUP_WIDTH,
    GROUP_WIDTH, GROUP_WIDTH, GROUP_WIDTH, HEADS_PER_GROUP, HEADS_PER_GROUP, GROUP_WIDTH,
)
N_IN = sum(COL_SIZES)

kernel_name = "hybrid_parallel_hgrn2_fox_rglru_gdn_hmoe"

F32 = jnp.float32

def _rmsnorm(x, g):
    xf = x.astype(F32)
    y = xf * lax.rsqrt(jnp.mean(xf * xf, axis=-1, keepdims=True) + EPS)
    return (y * g.astype(F32)).astype(x.dtype)

def _head_rms(x):
    return x * lax.rsqrt(jnp.mean(x * x, axis=-1, keepdims=True) + EPS)

def _l2norm(x):
    return x * lax.rsqrt(jnp.sum(x * x, axis=-1, keepdims=True) + EPS)

def _heads(t):
    b, s, w = t.shape
    return t.astype(F32).reshape(b, s, w // HEAD_DIM, HEAD_DIM)

def _causal_dwconv(x, w):
    c = x.shape[-1]
    return lax.conv_general_dilated(x, w[:, None, :], window_strides=(1,), padding=[(w.shape[0] - 1, 0)],
                                    dimension_numbers=('NWC', 'WIO', 'NWC'), feature_group_count=c)

def _to_chunks(t):
    b, s, h, d = t.shape
    return t.reshape(b, s // CHUNK, CHUNK, h, d).transpose(1, 0, 3, 2, 4)

def _from_chunks(t):
    n, b, h, c, d = t.shape
    return t.transpose(1, 0, 3, 2, 4).reshape(b, n * c, h, d)

def hgrn2_group(q, f_logit, i, g, lb):
    b, s, w = q.shape
    q = jax.nn.silu(_heads(q))
    fl = _heads(f_logit)
    lb = lb.astype(F32).reshape(HEADS_PER_GROUP, HEAD_DIM)
    log_f = jnp.logaddexp(jnp.log(lb), jnp.log1p(-lb) + jax.nn.log_sigmoid(fl))
    k = (1.0 - lb) * jax.nn.sigmoid(-fl)
    v = _heads(i)
    qc, kc, vc, lc = _to_chunks(q), _to_chunks(k), _to_chunks(v), _to_chunks(log_f)
    bc = jnp.cumsum(lc, axis=3)
    causal = jnp.tril(jnp.ones((CHUNK, CHUNK), bool))[:, :, None]

    def step(state, inp):
        qi, ki, vi, bi = inp
        diff = bi[:, :, :, None, :] - bi[:, :, None, :, :]
        decay = jnp.where(causal, jnp.exp(jnp.where(causal, diff, 0.0)), 0.0)
        scores = jnp.einsum('bhtk,bhsk,bhtsk->bhts', qi, ki, decay)
        o = jnp.einsum('bhts,bhsv->bhtv', scores, vi) + jnp.einsum('bhtk,bhkv->bhtv', qi * jnp.exp(bi), state)
        b_last = bi[:, :, -1:, :]
        state = jnp.exp(b_last[:, :, 0, :, None]) * state + jnp.einsum('bhsk,bhsv->bhkv', ki * jnp.exp(b_last - bi), vi)
        return state, o

    s0 = jnp.zeros((b, HEADS_PER_GROUP, HEAD_DIM, HEAD_DIM), F32)
    _, o = lax.scan(step, s0, (qc, kc, vc, bc))
    o = _from_chunks(o)
    y = _head_rms(o) * jax.nn.silu(_heads(g))
    return y.reshape(b, s, w)

def fox_group(q, k, v, f_logit, f_bias):
    b, s, w = q.shape
    q, k, v = _heads(q), _heads(k), _heads(v)
    log_f = jax.nn.log_sigmoid(f_logit.astype(F32) + f_bias.astype(F32))
    c = jnp.cumsum(log_f, axis=1).transpose(0, 2, 1)
    nb = s // Q_BLOCK
    qb = q.reshape(b, nb, Q_BLOCK, HEADS_PER_GROUP, HEAD_DIM).transpose(1, 0, 2, 3, 4)
    cb = c.reshape(b, HEADS_PER_GROUP, nb, Q_BLOCK).transpose(2, 0, 1, 3)
    qpos = jnp.arange(s).reshape(nb, Q_BLOCK)
    kpos = jnp.arange(s)
    scale = HEAD_DIM ** -0.5

    def block(args):
        qi, ci, pi = args
        sc = jnp.einsum('bqhd,bkhd->bhqk', qi, k) * scale + (ci[..., :, None] - c[:, :, None, :])
        sc = jnp.where(pi[:, None] >= kpos[None, :], sc, -jnp.inf)
        p = jax.nn.softmax(sc, axis=-1)
        return jnp.einsum('bhqk,bkhd->bqhd', p, v)

    o = lax.map(block, (qb, cb, qpos))
    o = o.transpose(1, 0, 2, 3, 4).reshape(b, s, HEADS_PER_GROUP, HEAD_DIM)
    return _head_rms(o).reshape(b, s, w)

def rglru_group(xb, gate, conv_w, conv_b, w_a, b_a, w_x, b_x, lam):
    b, s, w = xb.shape
    xc = _causal_dwconv(xb.astype(F32), conv_w.astype(F32)) + conv_b.astype(F32)
    xh = xc.reshape(b, s, HEADS_PER_GROUP, HEAD_DIM)
    r = jax.nn.sigmoid(jnp.einsum('bshi,hij->bshj', xh, w_a.astype(F32)).reshape(b, s, w) + b_a.astype(F32))
    ig = jax.nn.sigmoid(jnp.einsum('bshi,hij->bshj', xh, w_x.astype(F32)).reshape(b, s, w) + b_x.astype(F32))
    log_a = -LRU_C * r * jax.nn.softplus(-lam.astype(F32))
    a = jnp.exp(log_a)
    u = jnp.sqrt(-jnp.expm1(2.0 * log_a)) * (ig * xc)

    def combine(left, right):
        a_l, u_l = left
        a_r, u_r = right
        return a_l * a_r, a_r * u_l + u_r

    _, h = lax.associative_scan(combine, (a, u), axis=1)
    y = h * jax.nn.gelu(gate.astype(F32))
    return _head_rms(y.reshape(b, s, HEADS_PER_GROUP, HEAD_DIM)).reshape(b, s, w)

def gdn_group(q, k, v, beta_logit, a_logit, z, conv_w, a_log, dt_bias):
    b, s, w = q.shape
    qkv = jax.nn.silu(_causal_dwconv(jnp.concatenate([q, k, v], axis=-1).astype(F32), conv_w.astype(F32)))
    q, k, v = [_heads(t) for t in jnp.split(qkv, 3, axis=-1)]
    q = _l2norm(q) * HEAD_DIM ** -0.5
    k = _l2norm(k)
    beta = jax.nn.sigmoid(beta_logit.astype(F32))
    g = -jnp.exp(a_log.astype(F32)) * jax.nn.softplus(a_logit.astype(F32) + dt_bias.astype(F32))
    qc, kc, vc = _to_chunks(q), _to_chunks(k), _to_chunks(v)
    bc = _to_chunks(beta[..., None])[..., 0]
    G = jnp.cumsum(_to_chunks(g[..., None])[..., 0], axis=-1)
    incl = jnp.tril(jnp.ones((CHUNK, CHUNK), bool))
    strict = jnp.tril(jnp.ones((CHUNK, CHUNK), bool), -1)
    diff = G[..., :, None] - G[..., None, :]
    gamma = jnp.where(incl, jnp.exp(jnp.where(incl, diff, 0.0)), 0.0)
    k_beta = kc * bc[..., None]
    m = jnp.where(strict, jnp.einsum('...tk,...sk->...ts', k_beta, kc) * gamma, 0.0)
    eye = jnp.eye(CHUNK, dtype=F32)
    t_inv = lax.linalg.triangular_solve(eye + m, jnp.broadcast_to(eye, m.shape), left_side=True, lower=True)
    u = t_inv @ (vc * bc[..., None])
    wk = t_inv @ (k_beta * jnp.exp(G)[..., None])
    a_qk = jnp.einsum('...tk,...sk->...ts', qc, kc) * gamma
    q_dec = qc * jnp.exp(G)[..., None]
    k_dec = kc * jnp.exp(G[..., -1:] - G)[..., None]
    g_last = jnp.exp(G[..., -1])

    def step(state, inp):
        ui, wi, aqi, qdi, kdi, gli = inp
        v_new = ui - wi @ state
        o = qdi @ state + aqi @ v_new
        state = gli[..., None, None] * state + jnp.einsum('bhsk,bhsv->bhkv', kdi, v_new)
        return state, o

    s0 = jnp.zeros((b, HEADS_PER_GROUP, HEAD_DIM, HEAD_DIM), F32)
    _, o = lax.scan(step, s0, (u, wk, a_qk, q_dec, k_dec, g_last))
    o = _from_chunks(o)
    y = _head_rms(o) * jax.nn.silu(_heads(z))
    return y.reshape(b, s, w)

def mem_cross_attention(h, memn, w_q, w_kv, w_o):
    b, s, _ = h.shape
    q = (h @ w_q).reshape(b, s, MEM_HEADS, MEM_HEAD_DIM)
    k, v = jnp.split(memn @ w_kv, 2, axis=-1)
    k = k.reshape(b, MEM_LEN, MEM_HEADS, MEM_HEAD_DIM)
    v = v.reshape(b, MEM_LEN, MEM_HEADS, MEM_HEAD_DIM)
    sc = jnp.einsum('bshd,bmhd->bhsm', q, k).astype(F32) * MEM_HEAD_DIM ** -0.5
    p = jax.nn.softmax(sc, axis=-1).astype(v.dtype)
    o = jnp.einsum('bhsm,bmhd->bshd', p, v).reshape(b, s, MEM_WIDTH)
    return o @ w_o

def hier_moe(h, w_rg, b_rg, w_re, b_re, w_gu, w_dn):
    b, s, d = h.shape
    ht = h.reshape(-1, d)
    t = ht.shape[0]
    grp_prob = jax.nn.softmax((ht @ w_rg + b_rg).astype(F32), axis=-1)
    p_grp, g_sel = lax.top_k(grp_prob, 1)
    exp_logits = (ht @ w_re + b_re).astype(F32).reshape(t, N_EXPERT_GROUPS, EXPERTS_PER_GROUP)
    sel = jnp.take_along_axis(exp_logits, g_sel[:, :, None], axis=1)[:, 0]
    w_top, i_top = lax.top_k(jax.nn.softmax(sel, axis=-1), TOP_K_IN_GROUP)
    w_top = w_top / jnp.sum(w_top, axis=-1, keepdims=True)
    gates = p_grp * w_top
    idx = g_sel * EXPERTS_PER_GROUP + i_top
    combine = jnp.sum(jax.nn.one_hot(idx, N_EXPERTS, dtype=F32) * gates[..., None], axis=1).astype(h.dtype)
    out = jnp.zeros_like(ht)
    for gi in range(N_EXPERT_GROUPS):
        sl = slice(gi * EXPERTS_PER_GROUP, (gi + 1) * EXPERTS_PER_GROUP)
        gu = jnp.einsum('td,edf->tef', ht, w_gu[sl])
        g_act, up = jnp.split(gu, 2, axis=-1)
        act = jax.nn.silu(g_act) * up * combine[:, sl, None]
        out = out + jnp.einsum('tef,efd->td', act, w_dn[sl])
    return out.reshape(b, s, d)

def setup_inputs(seed: int = 0) -> dict:
    key = jax.random.key(seed)
    ks = jax.random.split(key, 34)
    L, H = DEPTH, HEADS_PER_GROUP

    def nrm(k, shape, scale):
        return scale * jax.random.normal(k, shape, F32)

    def gain(k, shape):
        return 1.0 + nrm(k, shape, 0.02)

    lru_u = jax.random.uniform(ks[12], (L, GROUP_WIDTH), F32, minval=0.9, maxval=0.999)
    dt = jnp.exp(jax.random.uniform(ks[15], (L, H), F32, minval=math.log(1e-3), maxval=math.log(1e-1)))
    return {
        "x": nrm(ks[0], (BATCH, SEQ, D_MODEL), 1.0),
        "mem": nrm(ks[1], (BATCH, MEM_LEN, D_MODEL), 1.0),
        "norm_mix": gain(ks[2], (L, D_MODEL)),
        "w_in": nrm(ks[3], (L, D_MODEL, N_IN), D_MODEL ** -0.5),
        "hgrn_lb": nrm(ks[4], (L, GROUP_WIDTH), 0.1),
        "fox_fb": 2.0 + nrm(ks[5], (L, H), 0.5),
        "lru_conv_w": nrm(ks[6], (L, CONV_W, GROUP_WIDTH), CONV_W ** -0.5),
        "lru_conv_b": nrm(ks[7], (L, GROUP_WIDTH), 0.01),
        "lru_wa": nrm(ks[8], (L, H, HEAD_DIM, HEAD_DIM), HEAD_DIM ** -0.5),
        "lru_ba": nrm(ks[9], (L, GROUP_WIDTH), 0.01),
        "lru_wx": nrm(ks[10], (L, H, HEAD_DIM, HEAD_DIM), HEAD_DIM ** -0.5),
        "lru_bx": nrm(ks[11], (L, GROUP_WIDTH), 0.01),
        "lru_lam": jnp.log(lru_u) - jnp.log1p(-lru_u),
        "gdn_conv_w": nrm(ks[13], (L, CONV_W, 3 * GROUP_WIDTH), CONV_W ** -0.5),
        "gdn_a_log": jnp.log(jax.random.uniform(ks[14], (L, H), F32, minval=1.0, maxval=16.0)),
        "gdn_dt_bias": dt + jnp.log(-jnp.expm1(-dt)),
        "mix_gain": gain(ks[16], (L, D_MIX)),
        "w_out": nrm(ks[17], (L, D_MIX, D_MODEL), D_MIX ** -0.5),
        "norm_mem": gain(ks[18], (L, D_MODEL)),
        "norm_memkv": gain(ks[19], (L, D_MODEL)),
        "w_mq": nrm(ks[20], (L, D_MODEL, MEM_WIDTH), D_MODEL ** -0.5),
        "w_mkv": nrm(ks[21], (L, D_MODEL, 2 * MEM_WIDTH), D_MODEL ** -0.5),
        "w_mo": nrm(ks[22], (L, MEM_WIDTH, D_MODEL), MEM_WIDTH ** -0.5),
        "norm_ffn": gain(ks[23], (L, D_MODEL)),
        "w_rg": nrm(ks[24], (L, D_MODEL, N_EXPERT_GROUPS), D_MODEL ** -0.5),
        "b_rg": nrm(ks[25], (L, N_EXPERT_GROUPS), 0.01),
        "w_re": nrm(ks[26], (L, D_MODEL, N_EXPERTS), D_MODEL ** -0.5),
        "b_re": nrm(ks[27], (L, N_EXPERTS), 0.01),
        "w_e_gu": nrm(ks[28], (L, N_EXPERTS, D_MODEL, 2 * D_EXPERT), D_MODEL ** -0.5),
        "w_e_dn": nrm(ks[29], (L, N_EXPERTS, D_EXPERT, D_MODEL), D_EXPERT ** -0.5),
        "norm_final": gain(ks[30], (D_MODEL,)),
    }

def reference(x, mem, norm_mix, w_in, hgrn_lb, fox_fb, lru_conv_w, lru_conv_b, lru_wa, lru_ba, lru_wx, lru_bx,
              lru_lam, gdn_conv_w, gdn_a_log, gdn_dt_bias, mix_gain, w_out, norm_mem, norm_memkv, w_mq, w_mkv,
              w_mo, norm_ffn, w_rg, b_rg, w_re, b_re, w_e_gu, w_e_dn, norm_final):
    lb_all = jnp.cumsum(jax.nn.softmax(hgrn_lb.astype(F32), axis=0), axis=0)
    lb_all = lb_all - lb_all[0]
    split_at = np.cumsum(COL_SIZES)[:-1].tolist()
    for l in range(DEPTH):
        h = _rmsnorm(x, norm_mix[l])
        parts = jnp.split(h @ w_in[l], split_at, axis=-1)
        (a_q, a_f, a_i, a_g, b_q, b_k, b_v, b_f, c_x, c_g, d_q, d_k, d_v, d_b, d_a, d_z) = parts
        y_a = hgrn2_group(a_q, a_f, a_i, a_g, lb_all[l])
        y_b = fox_group(b_q, b_k, b_v, b_f, fox_fb[l])
        y_c = rglru_group(c_x, c_g, lru_conv_w[l], lru_conv_b[l], lru_wa[l], lru_ba[l], lru_wx[l], lru_bx[l], lru_lam[l])
        y_d = gdn_group(d_q, d_k, d_v, d_b, d_a, d_z, gdn_conv_w[l], gdn_a_log[l], gdn_dt_bias[l])
        y = jnp.concatenate([y_a, y_b, y_c, y_d], axis=-1) * mix_gain[l].astype(F32)
        x = x + y.astype(x.dtype) @ w_out[l]
        h = _rmsnorm(x, norm_mem[l])
        memn = _rmsnorm(mem, norm_memkv[l])
        x = x + mem_cross_attention(h, memn, w_mq[l], w_mkv[l], w_mo[l])
        h = _rmsnorm(x, norm_ffn[l])
        x = x + hier_moe(h, w_rg[l], b_rg[l], w_re[l], b_re[l], w_e_gu[l], w_e_dn[l])
    return _rmsnorm(x, norm_final)


_drawn_inputs = setup_inputs


def setup_inputs(seed=0):
    import zlib

    import numpy as np

    out = dict(_drawn_inputs(seed))
    spreads = {}
    factors = {'lru_ba': 8.0,
     'lru_bx': 8.0,
     'gdn_dt_bias': 8.242,
     'norm_mem': 7.237,
     'norm_memkv': 7.016,
     'norm_ffn': 2.778,
     'b_rg': 4.864,
     'b_re': 5.663,
     'norm_final': 7.672}
    for name, (base, spread) in spreads.items():
        noise = np.random.default_rng([zlib.crc32(name.encode()), seed]).standard_normal(out[name].shape)
        drawn = base * np.exp(spread * noise) if base else spread * noise
        out[name] = __import__('jax').numpy.asarray(drawn.astype(out[name].dtype))
    for name, factor in factors.items():
        out[name] = (out[name] * factor).astype(out[name].dtype)
    return out
```

```python
import concourse.bass as bass
from concourse import mybir
from contextlib import ExitStack


def hybrid_trunk(nc, a, out, dbg=None):
    f32, i32, u32 = mybir.dt.float32, mybir.dt.int32, mybir.dt.uint32
    ALU, ACT, AX = mybir.AluOpType, mybir.ActivationFunctionType, mybir.AxisListType
    P = 128
    T, D = a["x"].shape[1], a["x"].shape[2]
    NT, KT = T // P, D // P
    GW = D // 4
    HD, NH = 64, GW // 64
    CT = GW // P
    ML = a["mem"].shape[1]
    MT_ = ML // P
    NE, FE = a["w_e_gu"].shape[1], a["w_e_dn"].shape[2]
    NG, EPG = a["w_rg"].shape[2], NE // a["w_rg"].shape[2]
    TAPS = a["lru_conv_w"].shape[1]
    LRU_C = 8.0
    EPS = 1e-6
    PAD = TAPS - 1
    TP = T + PAD
    HALF = 512
    NHALF = T // HALF
    QK_SCALE = HD ** -0.5
    LEVELS = [1, 2, 4, 8, 16, 32, 64]
    NL = len(LEVELS)

    x, mem, w_in = a["x"][0], a["mem"][0], a["w_in"][0]
    names = "aq af ai ag bq bk bv bf cx cg dq dk dv db da dz".split()
    sizes = [GW] * 7 + [NH] + [GW] * 5 + [NH, NH, GW]
    col = {n: sum(sizes[:i]) for i, n in enumerate(names)}

    ctx = ExitStack()
    with ctx:
        def sb(name, shape, dt=f32):
            return ctx.enter_context(nc.sbuf_tensor(name, [P] + list(shape), dt))

        ident = sb("ident", [P])
        ones = sb("ones", [P])
        triu = sb("triu", [P])
        triu_s = sb("triu_s", [P])
        tril_s = sb("tril_s", [P])
        head_ones = sb("head_ones", [P])
        levT = sb("levT", [NL + 1, P])
        lev1 = sb("lev1", [P])
        negmask = sb("negmask", [P])
        prow = sb("prow", [P])
        pcol = sb("pcol", [80])
        negp = sb("negp", [8])
        fox_b = sb("fox_b", [1])
        alog = sb("alog", [NH])
        dtb = sb("dtb", [NH])
        lru_w = sb("lru_w", [2 * CT, P])
        PC = dict(mix=0, mem=8, memkv=16, ffn=24, gain=32, lconv=40, lb=48, ba=50, bx=52, lam=54,
                             gconv=56)
        ss = sb("ss", [4])
        rstd = sb("rstd", [4])
        epsc = sb("epsc", [1])

        arena = sb("arena", [46300])
        at = [0]

        def place(n):
            at[0] += n
            assert at[0] <= 46300, at[0]
            return at[0] - n

        def view(off, *shape):
            n = 1
            for s in shape:
                n *= s
            v = arena[:, off:off + n]
            if len(shape) == 1:
                return v
            if len(shape) == 2:
                return v.rearrange("p (a b) -> p a b", a=shape[0])
            return v.rearrange("p (a b c) -> p a b c", a=shape[0], b=shape[1])

        WC = 264
        o_ht = place(KT * T)
        o_w = place(2 * KT * WC)
        o_g1 = place(6 * TP)
        o_g4 = place(CT * T)
        o_g2 = place(6 * T)
        o_g3 = place(CT * T)
        o_bc = place(4 * CT * T)
        o_cx = place(CT * TP)
        o_tmp = place(7168)

        hT = view(o_ht, KT, T)
        wbuf = [view(o_w + i * KT * WC, KT, WC) for i in range(2)]
        memT = view(o_bc, KT, ML)
        d_raw = view(o_g1, 6, TP)
        d_cv = view(o_g2, 6, T)
        d_z = view(o_g3, NT, GW)
        a_q = view(o_g1, CT, T)
        a_f = view(o_g1 + CT * T, CT, T)
        a_i = view(o_g1 + 2 * CT * T, NT, GW)
        a_g = view(o_g1 + 3 * CT * T, NT, GW)
        assert 4 * CT * T <= 6 * TP + CT * T
        b_q = view(o_bc, CT, T)
        b_k = view(o_bc + CT * T, CT, T)
        b_v = view(o_bc + 2 * CT * T, NT, GW)
        c_g = view(o_bc + 3 * CT * T, CT, T)
        c_x = view(o_cx, CT, TP)
        yT = view(o_g2, KT, T)
        slot = lambda c: (c - 6) % KT
        memk = sb("memk", [CT, ML])
        memv = sb("memv", [MT_, GW])
        bf = sb("bf", [T])
        dba = sb("dba", [NT, 2 * NH])
        fidx, pidx, xor_f, tmp_mask, i_f, i_p, i_x = [view(o_bc + 4096 + i * P, P) for i in range(7)]
        iota_f, iota_p, xor_i = i_f.bitcast(i32), i_p.bitcast(i32), i_x.bitcast(i32)
        xin = [view(o_tmp + i * D, D) for i in range(2)]
        xs = [view(o_tmp + (2 + i) * D, D) for i in range(2)]
        junk = view(o_tmp + 4 * D, D)

        psum = [ctx.enter_context(nc.psum_tensor(f"bank{i}", [P, HALF], f32)) for i in range(8)]

        s = {n: ctx.enter_context(nc.semaphore(n)) for n in """
            h_E h_Ee h_act h_dve h_kt h_kts h_os x_l x_cbp x_cb x_nb x_o x_p x_tr x_pv x_pt l_sp l_gp l_ge
            l_gr l_a l_th l_dve l_act l_ssp h_o unit_e h_z h_dS h_Sv h_scr h_pm f_out x_row x_qk l_xc l_out
            h_qe l_w t_wo t_rw t_fg t_x2 t_mq t_mo t_o_r xs_r t_xn t_m_e t_rl t_r_dve t_o_e t_q_r t_q_e
            t_m_tr t_m_pv t_m_pt t_m_ot t_m_w t_m_ots t_m_mx t_m_p t_r_ge t_m_o t_m_sc t_z_ix t_r_rk ht_r
            t_init0 t_zt_d t_sc_d t_ix_ld f_c f_g0 f_g1 rstd_r f_ot0 f_ot1 x_in0 x_in1 unit_r w_ld0 w_ld1
            consts_i consts_v g_MTs g_T1 g_MTh a_chain params_in prm_in d_cvd d_sil d_ssp d_sq d_l2 d_el
            d_rs g_beta g_el g_Gv g_D g_qd g_eR g_mm g_ex g_MT g_XY g_T1s g_wk g_vn g_wks g_o g_os f_sq
            f_ss f_rs f_sil v_chain pcol_t pcol_v tr_r g_Gp g_cols g_R g_KV g_kv g_KK g_M g_AT g_upd g_vns
            g_dS g_S f_y f_tr e_wl0 e_wl1 e_wl2 e_wl3 e_ic e_g0 e_g1 e_tr e_ht e_gu e_sg e_ac e_at e_ats
            e_dn e_y e_st0 e_st1
            """.split()}
        block = ctx.enter_context(nc.Block())

        N_MEM0, N_X0 = 0, MT_

        w_mkv = a["w_mkv"][0]

        def cm(dst, rows=P):
            return lambda ct, h: dst(ct, h)

        CHUNKS = []

        def chunk(src, c0, width, pieces):
            CHUNKS.append((src, c0, width, pieces))

        chunk(w_mkv, 0, GW, [("cm", 0, P, "mem", lambda ct, h: memk[:, ct, :])] )
        chunk(w_mkv, GW, GW, [("tm", 0, GW, "mem", lambda m: memv[:, m, :])])
        chunk(w_in, col["dq"], GW, [("cm", 0, P, "x", lambda ct, h: d_raw[:, 4 + ct, PAD + h * HALF:PAD + (h + 1) * HALF])])
        chunk(w_in, col["dk"], GW, [("cm", 0, P, "x", lambda ct, h: d_raw[:, 2 + ct, PAD + h * HALF:PAD + (h + 1) * HALF])])
        chunk(w_in, col["dv"], GW, [("cm", 0, P, "x", lambda ct, h: d_raw[:, ct, PAD + h * HALF:PAD + (h + 1) * HALF])])
        chunk(w_in, col["db"], GW + 2 * NH, [("tmz", 0, GW + 2 * NH, "x", None)])
        chunk(w_in, col["aq"], GW, [("cm", 0, P, "x", lambda ct, h: a_q[:, ct, h * HALF:(h + 1) * HALF])])
        chunk(w_in, col["af"], GW, [("cm", 0, P, "x", lambda ct, h: a_f[:, ct, h * HALF:(h + 1) * HALF])])
        chunk(w_in, col["ai"], GW, [("tm", 0, GW, "x", lambda m: a_i[:, m, :])])
        chunk(w_in, col["ag"], GW, [("tm", 0, GW, "x", lambda m: a_g[:, m, :])])
        chunk(w_in, col["bq"], GW, [("cm", 0, P, "x", lambda ct, h: b_q[:, ct, h * HALF:(h + 1) * HALF])])
        chunk(w_in, col["bk"], GW, [("cm", 0, P, "x", lambda ct, h: b_k[:, ct, h * HALF:(h + 1) * HALF])])
        chunk(w_in, col["bv"], GW + NH, [("tm", 0, GW, "x", lambda m: b_v[:, m, :]),
                                         ("row", GW, NH, "x", lambda h: bf[0:NH, h * HALF:(h + 1) * HALF])])
        chunk(w_in, col["cx"], GW, [("cm", 0, P, "x", lambda ct, h: c_x[:, ct, PAD + h * HALF:PAD + (h + 1) * HALF])])
        chunk(w_in, col["cg"], GW, [("cm", 0, P, "x", lambda ct, h: c_g[:, ct, h * HALF:(h + 1) * HALF])])

        UNITS = []
        for ci, (src, c0, width, pieces) in enumerate(CHUNKS):
            wb = wbuf[ci % 2]
            for kind, b0, n, of, dst in pieces:
                act, rows = (memT, ML) if of == "mem" else (hT, T)
                if kind in ("cm", "row"):
                    for ct in range(CT if kind == "cm" else 1):
                        for h in range(max(1, rows // HALF)):
                            w = min(rows, HALF)
                            UNITS.append((ci, lambda k, wb=wb, b=b0 + ct * P, n=n: wb[:, k, b:b + n],
                                          lambda k, act=act, h=h, w=w: act[:, k, h * w:(h + 1) * w], n, w,
                                          [(slice(0, w), dst(ct, h) if kind == "cm" else dst(h))]))
                else:
                    for m in range(rows // P):
                        if kind == "tm":
                            to = [(slice(0, n), dst(m))]
                        else:
                            to = [(slice(0, 2 * NH), dba[:, m, :]), (slice(2 * NH, n), d_z[:, m, :])]
                        UNITS.append((ci, lambda k, act=act, m=m: act[:, k, m * P:(m + 1) * P],
                                      lambda k, wb=wb, b=b0, n=n: wb[:, k, b:b + n], P, n, to))
        UNITS_OF = [sum(u[0] == c for u in UNITS) for c in range(len(CHUNKS))]
        END_OF = [sum(UNITS_OF[:c + 1]) for c in range(len(CHUNKS))]
        PROJ_BANKS = [2, 3, 4]

        def bc(ap, axis, shape):
            return ap.unsqueeze(axis).to_broadcast(shape)

        def chain(eng, sem):
            n = [0]

            def link(ins):
                n[0] += 1
                ins.then_inc(sem, 1)
                eng.wait_ge(sem, n[0])
            return link

        (o_D, o_gam, o_gamT, o_M, o_MT, o_X, o_Y, o_T1, o_AT, o_eR, o_kvb) = [o_tmp + i * 512 for i in range(11)]
        H4 = lambda off: view(off, NH, P)
        gD, gam, gamT, gM, gMT, gX, gY, gT1, gAT, eR, kvb = map(H4, (o_D, o_gam, o_gamT, o_M, o_MT, o_X, o_Y, o_T1,
                                                                     o_AT, o_eR, o_kvb))
        MTh = [H4(o_tmp + 11 * 512), H4(o_tmp + 12 * 512)]
        kdec = view(o_tmp + 13 * 512, NH, HD)
        wkT = view(o_tmp + 13 * 512 + 256, CT, P)
        assert 14 * 512 <= 7168
        qd = sb("qd", [CT, P])
        vnew = sb("vnew", [NH, HD])
        gS = sb("gS", [CT, HD])
        l2sq = [view(o_tmp + i * T, T) for i in range(2)]
        l2rs = [view(o_tmp + (2 + i) * T, T) for i in range(2)]
        NHT = NT * NH
        small = sb("small", [12, NT, NH])
        beta, gg, Gc, Gl, eG, kds, gle, beG, sm_t, sm_e, nexp = [small[:, i] for i in range(11)]
        glS = sb("glS", [NT, CT])
        d_o = d_cv[:, 4:6]
        fin_sq = view(o_tmp, CT, T)
        fin_ss = sb("fin_ss", [CT * NT * 2])

        h_lf = view(o_ht, CT, T)
        h_b = view(o_ht + CT * T, CT, T)
        h_qe = view(o_ht + 2 * CT * T, CT, T)
        h_kdT = view(o_ht + 3 * CT * T, NT, GW)
        seg = view(o_w, T)
        hE = [view(o_w + T + i * HALF, HALF) for i in range(2)]
        h_o = view(o_w + 2 * T, CT, T)
        hz = [view(o_tmp + i * NL * HALF, NL, HALF) for i in range(2)]
        h_pm = [view(o_g2 + 6 * T + i * T, NL + 1, P) for i in range(2)]
        hS = view(o_g2 + 4 * T, CT, NT, HD)
        hdec = sb("hdec", [CT, NT])
        NIT = CT * NHALF
        x_cb = view(o_ht, NH, T)
        x_sc = [view(o_ht + (4 + i) * T, T) for i in range(2)]
        x_pT = [view(o_ht + (6 + i) * T, NT, P) for i in range(2)]
        x_row = view(o_w, T)
        x_one = view(o_w + T, T)
        x_l = view(o_tmp + 4 * T, T)
        x_o_ = view(o_tmp + 2 * T, CT, T)
        x_col = sb("x_col", [3, NH * NT])
        NW = NH * NT
        l_xc = view(o_ht, CT, T)
        l_g = view(o_ht + 2 * T, 2 * CT, T)
        l_a = view(o_ht + 6 * T, CT, T)
        l_th = view(o_w, CT, T)
        l_u = view(o_w + 2 * T, CT, T)
        l_h = view(o_tmp, CT, T)
        l_rs = view(o_tmp + 2 * T, CT, T)
        l_col = sb("l_col", [12])

        def block_halves(t, h):
            return t.rearrange("p (n two h) -> p n two h", two=2, h=h)

        def act_hgrn_E(act, k):
            act.wait_ge(s["h_E"], k + 1)
            nc.scalar.activation(hE[k % 2], hE[k % 2], ACT.Exp).then_inc(s["h_Ee"], 1)

        def act_tail(act, link, finish_act, evacuate, stats):
            nc.scalar.activation(a_q, a_q, ACT.Silu).then_inc(s["h_act"], 1)
            link(nc.scalar.activation(h_lf, a_f, ACT.Abs))
            link(nc.scalar.activation(h_lf, h_lf, ACT.Exp, scale=-1.0))
            nc.scalar.activation(h_lf, h_lf, ACT.Ln, bias=1.0).then_inc(s["h_act"], 1)
            act.wait_ge(s["h_dve"], 1)
            nc.scalar.activation(a_f, a_f, ACT.Exp).then_inc(s["h_act"], 1)
            act.wait_ge(s["h_dve"], 2)
            nc.scalar.activation(h_lf, h_lf, ACT.Exp).then_inc(s["h_act"], 1)
            nc.scalar.activation(h_qe, h_b, ACT.Exp).then_inc(s["h_act"], 1)
            nc.scalar.activation(hdec[:, :, :], h_b[:, :, P - 1:T:P], ACT.Exp).then_inc(s["h_act"], 1)
            for i in range(2 * CT):
                act.wait_ge(s["h_kt"], i + 1)
                c, j = i // 2, i % 2
                nc.scalar.activation(h_kdT[:, 4 * j:4 * j + 4, c * P:(c + 1) * P],
                                     psum[2 + i % 2][:, :].rearrange("p (n q) -> p n q", n=4),
                                     ACT.Copy).then_inc(s["h_kts"], 1)
            for k in range(NL):
                act_hgrn_E(act, k)
            for it in range(NIT):
                for j in range(8):
                    q = it * 8 + j
                    if it < NIT - 1 and j < NL:
                        act_hgrn_E(act, (it + 1) * NL + j)
                    if q >= 1:
                        act_hgrn_o(act, q - 1)
            act_hgrn_o(act, NIT * 8 - 1)
            finish_act(1, h_o, a_g, lambda e: e.wait_ge(s["h_os"], NIT * 8))

            link(nc.scalar.activation(x_l[0:NH, :], bf[0:NH, :], ACT.Abs, bias=fox_b[0:NH, 0:1]))
            link(nc.scalar.activation(x_l[0:NH, :], x_l[0:NH, :], ACT.Exp, scale=-1.0))
            nc.scalar.activation(x_l[0:NH, :], x_l[0:NH, :], ACT.Ln, bias=1.0).then_inc(s["x_l"], 1)
            for i in range(NH * NHALF):
                act.wait_ge(s["x_cbp"], i + 1)
                h, hf = i // NHALF, i % NHALF
                nc.scalar.activation(x_cb[:, h, hf * HALF:(hf + 1) * HALF], psum[2 + i % 2][:, :],
                                     ACT.Copy).then_inc(s["x_cb"], 1)
            tr = [0]

            def probs(w):
                n = (w % NT + 1) * P
                act.wait_ge(s["x_nb"], w + 1)
                if w >= 2:
                    act.wait_ge(s["x_o"], w - 1)
                nc.scalar.activation(x_sc[w % 2][:, 0:n], x_sc[w % 2][:, 0:n], ACT.Exp, bias=x_col[:, 0, w:w + 1],
                                     scale=QK_SCALE, accum_out=x_col[:, 1, w:w + 1]).then_inc(s["x_p"], 1)

            def probsT(w):
                blocks = w % NT + 1
                for b in range(0, blocks, 4):
                    m = min(4, blocks - b)
                    act.wait_ge(s["x_tr"], tr[0] + 1)
                    if w >= 2:
                        act.wait_ge(s["x_pv"], w - 1)
                    nc.scalar.activation(x_pT[w % 2][:, b:b + m, :],
                                         psum[4 + tr[0] % 2][:, 0:m * P].rearrange("p (b q) -> p b q", q=P),
                                         ACT.Copy).then_inc(s["x_pt"], 1)
                    tr[0] += 1

            for w in range(NW + 1):
                if w < NW:
                    probs(w)
                if w >= 1:
                    probsT(w - 1)
            finish_act(2, x_o_, None, lambda e: e.wait_ge(s["x_o"], NW))

            lam = pcol[:, PC["lam"]:PC["lam"] + CT]
            link(nc.scalar.activation(l_col[:, 0:CT], lam, ACT.Abs))
            link(nc.scalar.activation(l_col[:, 0:CT], l_col[:, 0:CT], ACT.Exp, scale=-1.0))
            nc.scalar.activation(l_col[:, 0:CT], l_col[:, 0:CT], ACT.Ln, bias=1.0).then_inc(s["l_sp"], 1)
            act.wait_ge(s["l_sp"], 2)
            for g in range(2):
                for c in range(CT):
                    for hf in range(NHALF):
                        i = (g * CT + c) * NHALF + hf
                        act.wait_ge(s["l_gp"], i + 1)
                        nc.scalar.activation(l_g[:, g * CT + c, hf * HALF:(hf + 1) * HALF], psum[i][:, :], ACT.Exp,
                                             bias=l_col[:, 6 + g * CT + c:7 + g * CT + c],
                                             scale=-1.0).then_inc(s["l_ge"], 1)
            act.wait_ge(s["l_gr"], 1)
            for c in range(CT):
                nc.scalar.activation(l_a[:, c], l_g[:, c], ACT.Exp, scale=l_col[:, 2 + c:3 + c]).then_inc(s["l_a"], 1)
            for c in range(CT):
                nc.scalar.activation(l_th[:, c], l_g[:, c], ACT.Tanh, scale=l_col[:, 4 + c:5 + c]).then_inc(s["l_th"], 1)
            act.wait_ge(s["l_dve"], 1)
            link(nc.scalar.activation(l_th, l_th, ACT.Ln))
            nc.scalar.activation(l_th, l_th, ACT.Exp, scale=0.5).then_inc(s["l_act"], 1)
            nc.scalar.activation(c_g, c_g, ACT.Gelu_apprx_tanh).then_inc(s["l_act"], 1)
            act.wait_ge(s["l_dve"], 2)
            nc.scalar.activation(l_a, l_h, ACT.Square).then_inc(s["l_act"], 1)
            for i in range(CT * NHALF):
                act.wait_ge(s["l_ssp"], i + 1)
                part = l_rs[:, i // NHALF, (i % NHALF) * HALF:(i % NHALF + 1) * HALF]
                link(nc.scalar.activation(part, psum[i][:, :], ACT.Ln, bias=epsc[:, 0:1], scale=1.0 / HD))
            nc.scalar.activation(l_rs, l_rs, ACT.Exp, scale=-0.5).then_inc(s["l_act"], 1)
            act_tail2(act, link, stats)

        def act_hgrn_o(act, q):
            act.wait_ge(s["h_o"], q + 1)
            it, j = q // 8, q % 8
            c, n, par = it // NHALF, (it % NHALF) * 4 + j // 2, j % 2
            nc.scalar.activation(h_o[:, c, n * P + par * HD:n * P + (par + 1) * HD], psum[6 + par][:, 0:HD],
                                 ACT.Copy).then_inc(s["h_os"], 1)

        def dve_tail(dve, v, link, finish_dve, scale_rows, gains):
            dve.wait_ge(s["unit_e"], len(UNITS))
            link(v.memset(seg, 1.0))
            link(v.memset(seg[:, 0:T:P], 0.0))
            dve.wait_ge(s["h_act"], 2)
            v.scalar_tensor_tensor(h_lf, a_f, 0.0, h_lf, ALU.min, ALU.subtract).then_inc(s["h_dve"], 1)
            dve.wait_ge(s["h_dve"], 1)
            for c in range(CT):
                link(v.tensor_tensor_scan(h_b[:, c], seg, h_lf[:, c], 0.0, ALU.mult, ALU.add))
            bt = h_b.rearrange("p c (n q) -> p (c n) q", q=P)
            lt = h_lf.rearrange("p c (n q) -> p (c n) q", q=P)
            v.tensor_tensor(lt, bt[:, :, P - 1:P].to_broadcast([P, CT * NT, P]), bt, ALU.subtract).then_inc(s["h_dve"], 1)
            dve.wait_ge(s["h_act"], 3)
            link(v.tensor_scalar(a_f, a_f, 1.0, None, ALU.add))
            v.reciprocal(a_f, a_f).then_inc(s["h_dve"], 1)
            dve.wait_ge(s["h_act"], 4)
            dve.wait_ge(s["h_dve"], 3)
            v.tensor_tensor(h_lf, h_lf, a_f, ALU.mult).then_inc(s["h_dve"], 1)

            def level(k):
                it, h = k // NL, LEVELS[k % NL]
                c, hf = it // NHALF, it % NHALF
                if k >= 2:
                    dve.wait_ge(s["h_z"], 2 * (k - 1))
                b = block_halves(h_b[:, c, hf * HALF:(hf + 1) * HALF], h)
                e = block_halves(hE[k % 2], h)
                mid = b[:, :, 0, h - 1:h].to_broadcast([P, HALF // (2 * h), h])
                link(v.tensor_tensor(e[:, :, 0], mid, b[:, :, 0], ALU.subtract))
                v.tensor_tensor(e[:, :, 1], b[:, :, 1], mid, ALU.subtract).then_inc(s["h_E"], 1)

            for k in range(NL):
                level(k)
            dve.wait_ge(s["h_act"], 6)
            link(v.memset(hS[:, :, 0], 0.0))
            for c in range(CT):
                dve.wait_ge(s["h_dS"], c + 1)
                for n in range(1, NT):
                    link(v.scalar_tensor_tensor(hS[:, c, n], hS[:, c, n - 1], hdec[:, c, n - 1:n],
                                                psum[4 + c][:, (n - 1) * HD:n * HD], ALU.mult, ALU.add))
            v.tensor_copy(l_col[:, 11:12], epsc[:, 0:1]).then_inc(s["h_Sv"], 1)
            for it in range(NIT):
                for j in range(8):
                    q = it * 8 + j
                    dve.wait_ge(s["h_scr"], q + 1)
                    if q >= 2:
                        dve.wait_ge(s["h_o"], q - 1)
                    for b in range(2):
                        v.tensor_tensor(h_pm[q % 2][:, 4 * b:4 * b + 4],
                                        psum[2 * (j % 2) + b][:, :].rearrange("p (l t) -> p l t", l=4),
                                        levT[:, 4 * b:4 * b + 4], ALU.mult).then_inc(s["h_pm"], 1)
                    if it < NIT - 1 and j < NL:
                        level((it + 1) * NL + j)
            finish_dve(1, h_o, a_g, 0)

            dve.wait_ge(s["f_out"], 8)
            link(v.memset(x_one[0:NH, :], 1.0))
            link(v.tensor_scalar(x_row[0:NH, :], bf[0:NH, :], fox_b[0:NH, 0:1], 0.0, ALU.add, ALU.min))
            dve.wait_ge(s["x_l"], 1)
            link(v.tensor_tensor(x_l[0:NH, :], x_row[0:NH, :], x_l[0:NH, :], ALU.subtract))
            link(v.tensor_tensor_scan(x_row[0:NH, :], x_one[0:NH, :], x_l[0:NH, :], 0.0, ALU.mult, ALU.add))
            v.tensor_scalar(x_row[0:NH, :], x_row[0:NH, :], -1.0 / QK_SCALE, None, ALU.mult).then_inc(s["x_row"], 1)
            dve.wait_ge(s["x_cb"], NH * NHALF)

            def fox_out(w):
                h, i = w // NT, w % NT
                dve.wait_ge(s["x_pv"], w + 1)
                link(v.reciprocal(x_col[:, 2, w:w + 1], x_col[:, 1, w:w + 1]))
                v.tensor_scalar(x_o_[:, h // 2, i * P + (h % 2) * HD:i * P + (h % 2 + 1) * HD],
                                psum[2 + w % 2][:, 0:HD], x_col[:, 2, w:w + 1], None, ALU.mult).then_inc(s["x_o"], 1)

            for w in range(NW):
                h, n = w // NT, (w % NT + 1) * P
                dve.wait_ge(s["x_qk"], w + 1)
                if w >= 2:
                    dve.wait_ge(s["x_tr"], fox_tr(w - 2))
                for b in range(0, n, HALF):
                    m = min(HALF, n - b)
                    link(v.tensor_tensor(x_sc[w % 2][:, b:b + m], psum[6 * (w % 2) + b // HALF][:, 0:m],
                                         x_cb[:, h, b:b + m], ALU.add))
                link(v.tensor_reduce(x_col[:, 0, w:w + 1], x_sc[w % 2][:, 0:n], AX.X, ALU.max))
                v.tensor_scalar(x_col[:, 0, w:w + 1], x_col[:, 0, w:w + 1], -QK_SCALE, None,
                                ALU.mult).then_inc(s["x_nb"], 1)
                if w >= 2:
                    fox_out(w - 2)
            fox_out(NW - 2)
            fox_out(NW - 1)
            finish_dve(2, x_o_, None, 2)

            wl = lambda t, c: pcol[:, PC["lconv"] + CT * t + c:PC["lconv"] + CT * t + c + 1]
            dve.wait_ge(s["f_out"], 12)
            dve.wait_ge(s["l_sp"], 1)
            link(v.tensor_scalar(l_col[:, 2:4], pcol[:, PC["lam"]:PC["lam"] + CT], -1.0, 0.0, ALU.mult, ALU.max))
            link(v.tensor_tensor(l_col[:, 0:2], l_col[:, 0:2], l_col[:, 2:4], ALU.add))
            link(v.tensor_scalar(l_col[:, 2:4], l_col[:, 0:2], -LRU_C, None, ALU.mult))
            link(v.tensor_scalar(l_col[:, 4:6], l_col[:, 0:2], LRU_C, None, ALU.mult))
            v.tensor_scalar(l_col[:, 6:10], pcol[:, PC["ba"]:PC["ba"] + 2 * CT], -1.0, None, ALU.mult).then_inc(s["l_sp"], 1)
            for c in range(CT):
                link(v.tensor_scalar(l_xc[:, c], c_x[:, c, 0:T], wl(0, c), pcol[:, PC["lb"] + c:PC["lb"] + c + 1],
                                     ALU.mult, ALU.add))
                for t in range(1, TAPS):
                    ins = v.scalar_tensor_tensor(l_xc[:, c], c_x[:, c, t:t + T], wl(t, c), l_xc[:, c],
                                                 ALU.mult, ALU.add)
                    ins.then_inc(s["l_xc"], 1) if t == TAPS - 1 else link(ins)
            for g in range(2):
                dve.wait_ge(s["l_ge"], 2 * CT * (g + 1))
                part = l_g[:, g * CT:(g + 1) * CT]
                link(v.tensor_scalar(part, part, 1.0, None, ALU.add))
                v.reciprocal(part, part).then_inc(s["l_gr"], 1)
            dve.wait_ge(s["l_xc"], CT)
            dve.wait_ge(s["l_gr"], 2)
            link(v.tensor_tensor(l_xc, l_xc, l_g[:, CT:2 * CT], ALU.mult))
            dve.wait_ge(s["l_a"], CT)
            link(v.tensor_tensor(l_u, l_a, l_a, ALU.mult))
            dve.wait_ge(s["l_th"], CT)
            link(v.scalar_tensor_tensor(l_th, l_u, 1.0, l_th, ALU.add, ALU.mult))
            v.tensor_scalar(l_th, l_th, 1e-18, None, ALU.max).then_inc(s["l_dve"], 1)
            dve.wait_ge(s["l_act"], 1)
            link(v.tensor_tensor(l_u, l_th, l_xc, ALU.mult))
            for c in range(CT):
                link(v.tensor_tensor_scan(l_h[:, c], l_a[:, c], l_u[:, c], 0.0, ALU.mult, ALU.add))
            dve.wait_ge(s["l_act"], 2)
            v.tensor_tensor(l_h, l_h, c_g, ALU.mult).then_inc(s["l_dve"], 1)
            dve.wait_ge(s["l_act"], 4)
            for c in range(CT):
                v.scalar_tensor_tensor(yT[:, slot(4 + c)], l_h[:, c], pcol[:, PC["gain"] + 4 + c:PC["gain"] + 5 + c],
                                       l_rs[:, c], ALU.mult, ALU.mult).then_inc(s["l_out"], 1)
            dve_tail2(dve, v, link, scale_rows, gains)

        def fox_tr(w):
            return sum((i % NT + 4) // 4 for i in range(w + 1))

        def pe_tail(pe, mm, finish_pe, transposes):
            rows = lambda h: slice(HD * (h % 2), HD * (h % 2) + HD)
            hd = lambda h: slice(h * HD, (h + 1) * HD)
            pe.wait_ge(s["h_dve"], 4)
            for i in range(2 * CT):
                if i >= 2:
                    pe.wait_ge(s["h_kts"], i - 1)
                for t in range(4):
                    n = (i % 2) * 4 + t
                    ins = nc.tensor.transpose(psum[2 + i % 2][:, t * P:(t + 1) * P],
                                              h_lf[:, i // 2, n * P:(n + 1) * P], ident[:, :])
                ins.then_inc(s["h_kt"], 1)
            pe.wait_ge(s["h_kts"], 2 * CT)
            for c in range(CT):
                for n in range(NT):
                    for par in range(2):
                        h = 2 * c + par
                        ins = mm(psum[4 + c][rows(h), hd(n)], h_kdT[:, n, hd(h)], a_i[:, n, hd(h)],
                                 start=True, stop=True)
                ins.then_inc(s["h_dS"], 1)

            def hgrn_scores(q):
                it, j = q // 8, q % 8
                c, n4, par = it // NHALF, j // 2, j % 2
                pe.wait_ge(s["h_z"], 2 * NL * (it + 1))
                if q >= 2:
                    pe.wait_ge(s["h_pm"], 2 * (q - 1))
                part = slice(n4 * P, (n4 + 1) * P)
                tok = slice((it % NHALF) * HALF + n4 * P, (it % NHALF) * HALF + (n4 + 1) * P)
                for lv in range(NL + 1):
                    bank = psum[2 * par + lv // 4][:, (lv % 4) * P:(lv % 4 + 1) * P]
                    if lv < NL:
                        ins = mm(bank, hz[it % 2][rows(par), lv, part], hz[it % 2][rows(par), lv, part],
                                 start=True, stop=True)
                    else:
                        ins = mm(bank, a_f[rows(par), c, tok], a_q[rows(par), c, tok], start=True, stop=True)
                ins.then_inc(s["h_scr"], 1)

            def hgrn_out(q):
                it, j = q // 8, q % 8
                c, n, par = it // NHALF, (it % NHALF) * 4 + j // 2, j % 2
                pe.wait_ge(s["h_pm"], 2 * q + 2)
                if q >= 2:
                    pe.wait_ge(s["h_os"], q - 1)
                bank = psum[6 + par][:, 0:HD]
                for lv in range(NL + 1):
                    mm(bank, h_pm[q % 2][:, lv], a_i[:, n, hd(2 * c + par)], start=(lv == 0), stop=False)
                mm(bank, h_qe[rows(par), c, n * P:(n + 1) * P], hS[rows(par), c, n], start=False,
                   stop=True).then_inc(s["h_o"], 1)

            pe.wait_ge(s["f_out"], 4)
            pe.wait_ge(s["h_act"], 1)
            pe.wait_ge(s["h_Sv"], 1)
            pe.wait_ge(s["h_qe"], 1)
            hgrn_scores(0)
            for q in range(NIT * 8):
                if q + 1 < NIT * 8:
                    hgrn_scores(q + 1)
                hgrn_out(q)
            finish_pe(1, h_o)

            pe.wait_ge(s["x_row"], 1)
            for i in range(NH * NHALF):
                if i >= 2:
                    pe.wait_ge(s["x_cb"], i - 1)
                h, hf = i // NHALF, i % NHALF
                mm(psum[2 + i % 2][:, :], ident[0:NH, h:h + 1].to_broadcast([NH, P]),
                   x_row[0:NH, hf * HALF:(hf + 1) * HALF], start=True, stop=True).then_inc(s["x_cbp"], 1)
            pe.wait_ge(s["x_cb"], NH * NHALF)
            pe.wait_ge(s["f_out"], 8)
            tr = [0]

            def fox_scores(w):
                h, i = w // NT, w % NT
                if w >= 2:
                    pe.wait_ge(s["x_nb"], w - 1)
                q = b_q[rows(h), h // 2, i * P:(i + 1) * P]
                for b in range(0, i * P, HALF):
                    m = min(HALF, i * P - b)
                    mm(psum[6 * (w % 2) + b // HALF][:, 0:m], q, b_k[rows(h), h // 2, b:b + m], start=True, stop=True)
                o = (i * P) % HALF
                bank = psum[6 * (w % 2) + i * P // HALF][:, o:o + P]
                mm(bank, q, b_k[rows(h), h // 2, i * P:(i + 1) * P], start=True, stop=False)
                mm(bank, ident[:, :], negmask[:, :], start=False, stop=True).then_inc(s["x_qk"], 1)

            def fox_transposes(w):
                blocks = w % NT + 1
                pe.wait_ge(s["x_p"], w + 1)
                for b in range(0, blocks, 4):
                    if tr[0] >= 2:
                        pe.wait_ge(s["x_pt"], tr[0] - 1)
                    for t in range(b, min(b + 4, blocks)):
                        ins = nc.tensor.transpose(psum[4 + tr[0] % 2][:, (t - b) * P:(t - b + 1) * P],
                                                  x_sc[w % 2][:, t * P:(t + 1) * P], ident[:, :])
                    ins.then_inc(s["x_tr"], 1)
                    tr[0] += 1

            def fox_values(w):
                h, i = w // NT, w % NT
                pe.wait_ge(s["x_pt"], fox_tr(w))
                if w >= 2:
                    pe.wait_ge(s["x_o"], w - 1)
                for t in range(i + 1):
                    ins = mm(psum[2 + w % 2][:, 0:HD], x_pT[w % 2][:, t], b_v[:, t, hd(h)], start=(t == 0),
                             stop=(t == i))
                ins.then_inc(s["x_pv"], 1)

            fox_scores(0)
            for w in range(NW + 1):
                if w + 1 < NW:
                    fox_scores(w + 1)
                if w < NW:
                    fox_transposes(w)
                if w >= 1:
                    fox_values(w - 1)
            finish_pe(2, x_o_)

            pe.wait_ge(s["l_w"], 16 * 4 * CT)
            pe.wait_ge(s["l_xc"], CT)
            for g in range(2):
                for c in range(CT):
                    for hf in range(NHALF):
                        i = (g * CT + c) * NHALF + hf
                        mm(psum[i][:, :], lru_w[:, g * CT + c, :], l_xc[:, c, hf * HALF:(hf + 1) * HALF],
                           start=True, stop=True).then_inc(s["l_gp"], 1)
            pe.wait_ge(s["l_act"], 3)
            pe.wait_ge(s["l_ge"], 4 * CT)
            for i in range(CT * NHALF):
                mm(psum[i][:, :], head_ones[:, :], l_a[:, i // NHALF, (i % NHALF) * HALF:(i % NHALF + 1) * HALF],
                   start=True, stop=True).then_inc(s["l_ssp"], 1)
            pe_tail2(pe, mm, transposes)

        def pool_tail(pool):
            pool.wait_ge(s["h_act"], 1)
            pool.wait_ge(s["h_act"], 5)
            nc.gpsimd.tensor_tensor(h_qe, h_qe, a_q, ALU.mult).then_inc(s["h_qe"], 1)
            pool.wait_ge(s["h_dve"], 3)
            for k in range(NIT * NL):
                it, lv = k // NL, k % NL
                c, hf = it // NHALF, it % NHALF
                pool.wait_ge(s["h_Ee"], k + 1)
                if it >= 2:
                    pool.wait_ge(s["h_scr"], 8 * (it - 1))
                part = slice(hf * HALF, (hf + 1) * HALF)
                e, z = block_halves(hE[k % 2], LEVELS[lv]), block_halves(hz[it % 2][:, lv], LEVELS[lv])
                kk, qq = block_halves(a_f[:, c, part], LEVELS[lv]), block_halves(a_q[:, c, part], LEVELS[lv])
                nc.gpsimd.tensor_tensor(z[:, :, 0], e[:, :, 0], kk[:, :, 0], ALU.mult).then_inc(s["h_z"], 1)
                nc.gpsimd.tensor_tensor(z[:, :, 1], e[:, :, 1], qq[:, :, 1], ALU.mult).then_inc(s["h_z"], 1)
            pool_tail2(pool)
        OE = NT * D
        wo = view(o_g1, KT, D)
        x2 = view(o_bc, NT, D)
        mq = view(o_w, KT, GW)
        mo = view(o_w + KT * GW, CT, D)
        NR = NG + NE
        wr = view(o_cx, KT, NR)
        br = view(o_cx + KT * NR, NR)
        fin_g = view(o_cx + (KT + 1) * NR, D)
        mqT = view(o_tmp, CT, T)
        m_p = [view(o_g1 + i * T, NH, ML) for i in range(2)]
        m_pT = [view(o_g1 + (2 + i) * T, NH * MT_, P) for i in range(2)]
        m_o = [view(o_g1 + 4 * T + i * GW, GW) for i in range(2)]
        m_oT = [view(o_g1 + 4 * T + (2 + i) * GW, CT, P) for i in range(2)]
        m_col = sb("m_col", [3, NT, NH])
        G2, G3 = MT_ + NT, MT_ + 2 * NT
        r0 = o_g1 + 6144 + 4
        rp = [r0]

        def rt(*shape):
            n = 1
            for d in shape:
                n *= d
            rp[0] += n
            assert rp[0] <= o_g2, rp[0]
            return view(rp[0] - n, *shape)
        TK = 2
        lg = rt(NT, NR)
        gpad, gmx, sel, smx = rt(NT, 8), rt(NT, 8), rt(NT, 8), rt(NT, 8)
        gix, six = rt(NT, 8).bitcast(u32), rt(NT, 8).bitcast(u32)
        gself, goh, pg = rt(NT), rt(NT, NG), rt(NT)
        gex = rt(NT, NG)
        eid = rt(TK, NT)
        wts = rt(TK, NT)
        rank = rt(TK, NT)
        slots = rt(TK, NT).bitcast(i32)
        tokid = rt(NT).bitcast(i32)
        io_i = rt(NE).bitcast(i32)
        io_f = rt(NE)
        totf = rt(NE)
        toti = rt(1).bitcast(i32)
        r1 = [o_g2 + 6144]
        oh = [view(r1[0] + i * NT * NE, NT, NE) for i in range(TK)]
        asum, apre, rtmp = [view(r1[0] + (TK + i) * NT * NE, NT, NE) for i in range(3)]
        gsum = view(r1[0] + 5 * NT * NE, NT * NG, EPG)
        idx_all = view(r1[0] + 6 * NT * NE, NE * (T // P)).bitcast(i32)
        EW = KT * 2 * FE + (FE // P) * D
        NB = 4
        wb_at = [o_g2, 0, EW, 2 * EW + 128]
        assert wb_at[3] >= o_g1 and wb_at[3] + EW <= r0 and EW == 6144
        w_gu = [view(o, KT, 2 * FE) for o in wb_at]
        w_dn = [view(o + KT * 2 * FE, FE // P, D) for o in wb_at]
        hg = [view(o_tmp + i * D, D) for i in range(2)]
        hgT = [view(o_tmp + (2 + i) * D, KT, P) for i in range(2)]
        ysb = [view(o_tmp + (4 + i) * D, D) for i in range(2)]
        sg = view(o_cx + (KT + 1) * NR + D, 2, FE)
        actv = view(o_tmp + 6 * D + 2 * FE, 2, FE)
        actT = [view(o_tmp + 6 * D + i * FE, FE // P, P) for i in range(2)]
        idxc = sb("idxc", [2], i32)
        PASSES = T // P
        yg = [view(i * D, D) for i in range(4)]
        slot_tok = nc.dram_tensor("slot_tok", (NE * T, 1), i32, kind="Internal").ap()
        xn_d = nc.dram_tensor("xn_d", (T, D), f32, kind="Internal").ap()
        y_d = nc.dram_tensor("y_d", (NE * T, D), f32, kind="Internal").ap()
        y_rows = y_d.rearrange("(p r e) d -> p e r d", r=P, e=NE)
        moe = ({n: s["e_" + n] for n in
                                 "wl0 wl1 wl2 wl3 ic g0 g1 tr ht gu sg ac at ats dn y st0 st1".split()})

        OVER = P

        def after(eng, sem, start, n):
            if isinstance(n, int) and n <= 0:
                return
            eng.wait_ge(sem, start + n)

        def each_expert(eng, step):
            for e in range(NB):
                step(e, e)
            with eng.Fori(1, NE // NB - 1) as i:
                for j in range(NB):
                    step(i * NB + j, j)
            for e in range(NE - NB, NE):
                step(e, e % NB)

        def gathers(e, b):
            return (e + 2 - b) * 8

        def weights(e, j):
            return (e + NB - j) * 8

        gu_d, dn_d = [t[0].rearrange("e (k p) n -> e p k n", p=P) for t in (a["w_e_gu"], a["w_e_dn"])]

        def load_expert(sp, q, e, j):
            sem = (q["wl0"], q["wl1"], q["wl2"], q["wl3"])[j]
            sp.dma_start(w_gu[j], gu_d[e]).then_inc(sem, 16)
            sp.dma_start(w_dn[j], dn_d[e]).then_inc(sem, 16)

        def sp_experts(sp, q, base, p):
            def step(e, j, more=True):
                sp.wait_ge(q["y"], 2 * base + 2 * (e + 1))
                sp.dma_start(y_rows[p, e], ysb[j % 2]).then_inc((q["st0"], q["st1"])[j % 2], 16)
                if more:
                    load_expert(sp, q, e + NB, j)
            for e in range(NB):
                step(e, e)
            with sp.Fori(1, NE // NB - 1) as i:
                for j in range(NB):
                    step(i * NB + j, j)
            for e in range(NE - NB, NE):
                step(e, e % NB, more=False)

        def pass_end(eng, q, base):
            eng.wait_ge(q["st0"], 8 * base + 8 * NE)
            eng.wait_ge(q["st1"], 8 * base + 8 * NE)

        def sp_tail(sp):
            sp.wait_ge(s["f_out"], 8)
            sp.dma_start(wo, a["w_out"][0].rearrange("(k p) n -> p k n", p=P)).then_inc(s["t_wo"], 16)
            sp.wait_ge(s["l_xc"], CT)
            sp.dma_start(wr[:, :, 0:NG], a["w_rg"][0].rearrange("(k p) n -> p k n", p=P)).then_inc(s["t_rw"], 16)
            sp.dma_start(wr[:, :, NG:NR], a["w_re"][0].rearrange("(k p) n -> p k n", p=P)).then_inc(s["t_rw"], 16)
            sp.dma_start(br[:, 0:NG], a["b_rg"][0:1, :].to_broadcast([P, NG])).then_inc(s["t_rw"], 16)
            sp.dma_start(br[:, NG:NR], a["b_re"][0:1, :].to_broadcast([P, NE])).then_inc(s["t_rw"], 16)
            sp.dma_start(fin_g, a["norm_final"].unsqueeze(0).to_broadcast([P, D])).then_inc(s["t_fg"], 16)
            sp.wait_ge(s["f_out"], 12)
            sp.wait_ge(s["l_dve"], 2)
            sp.dma_start(x2, x.rearrange("(m p) n -> p m n", p=P)).then_inc(s["t_x2"], 16)
            sp.dma_start(mq, a["w_mq"][0].rearrange("(k p) n -> p k n", p=P)).then_inc(s["t_mq"], 16)
            sp.dma_start(mo, a["w_mo"][0].rearrange("(k p) n -> p k n", p=P)).then_inc(s["t_mo"], 16)
            first = lambda e: load_expert(sp, moe, e, e)
            sp.wait_ge(s["t_o_r"], 2 * NT)
            first(0)
            for m in range(NT):
                sp.wait_ge(s["xs_r"], G3 + m + 1)
                sp.dma_start(xn_d[m * P:(m + 1) * P, :], xs[m % 2]).then_inc(s["t_xn"], 16)
                sp.wait_ge(s["t_xn"], 16 * (m + 1))
                if m == 0:
                    sp.wait_ge(s["t_m_e"], 2 * NT)
                    first(3)
            sp.wait_ge(s["t_rl"], 1)
            first(1)
            first(2)
            sp_experts(sp, moe, 0, 0)
            with overflow(sp):
                with sp.Fori(0, PASSES - 1) as p:
                    pass_end(sp, moe, p * NE)
                    for e in range(NB):
                        load_expert(sp, moe, e, e)
                    sp_experts(sp, moe, (p + 1) * NE, p + 1)
                sp.wait_ge(moe["st0"], 8 * NE * PASSES)
                sp.wait_ge(moe["st1"], 8 * NE * PASSES)
            sp_tail3(sp)

        def overflow(eng):
            eng.wait_ge(s["t_r_dve"], 4)
            most = eng.value_load(toti[0:1, 0:1], min_val=0, max_val=T)
            return eng.If(most > OVER)

        def act_experts(act, q, base):
            def step(e, j):
                b = j % 2
                act.wait_ge(q["gu"], base + (e + 1))
                after(act, q["ac"], base, e - 1)
                nc.scalar.activation(sg[:, b], psum[2 + 4 * b][:, 0:FE], ACT.Silu).then_inc(q["sg"], 1)
                act.wait_ge(q["at"], base + (e + 1))
                nc.scalar.activation(actT[b], psum[3][:, 0:FE].rearrange("p (k t) -> p k t", t=P),
                                     ACT.Copy).then_inc(q["ats"], 1)
                act.wait_ge(q["dn"], base + (e + 1))
                after(act, (q["st0"], q["st1"])[b], 8 * base, gathers(e, b) - 16)
                nc.scalar.activation(ysb[b][:, 0:HALF], psum[4][:, :], ACT.Copy).then_inc(q["y"], 1)
            each_expert(act, step)

        def act_tail2(act, link, stats):
            for m in range(NT):
                stats(G2 + m, x2[:, m], lambda e, m=m: e.wait_ge(s["t_o_e"], 2 * (m + 1)))
            for u in range(CT * NHALF):
                act.wait_ge(s["t_q_r"], u + 1)
                nc.scalar.activation(mqT[:, u % CT, (u // CT) * HALF:(u // CT + 1) * HALF], psum[2 + u % 3][:, :],
                                     ACT.Copy).then_inc(s["t_q_e"], 1)
            act.wait_ge(s["t_o_r"], 2 * NT)

            def m_out(m):
                act.wait_ge(s["t_m_tr"], 2 * (m + 1))
                if m >= 2:
                    act.wait_ge(s["t_m_pv"], m - 1)
                link(nc.scalar.activation(m_pT[m % 2][:, 0:4], psum[0][:, :].rearrange("p (a b) -> p a b", b=P),
                                          ACT.Copy))
                nc.scalar.activation(m_pT[m % 2][:, 4:8], psum[1][:, :].rearrange("p (a b) -> p a b", b=P),
                                     ACT.Copy).then_inc(s["t_m_pt"], 1)
                act.wait_ge(s["t_m_ot"], m + 1)
                if m >= 2:
                    act.wait_ge(s["t_m_w"], 2 * (m - 1))
                nc.scalar.activation(m_oT[m % 2], psum[2][:, 0:GW].rearrange("p (c t) -> p c t", c=CT),
                                     ACT.Copy).then_inc(s["t_m_ots"], 1)

            for m in range(NT):
                act.wait_ge(s["t_m_mx"], m + 1)
                if m >= 2:
                    act.wait_ge(s["t_m_tr"], 2 * (m - 1))
                for h in range(NH):
                    k = (h % 2) * 2 + h // 2
                    ins = nc.scalar.activation(m_p[m % 2][:, h], psum[5 + h % 2][:, (h // 2) * ML:(h // 2 + 1) * ML],
                                               ACT.Exp, bias=m_col[:, 0, m, k:k + 1], scale=QK_SCALE,
                                               accum_out=m_col[:, 1, m, h:h + 1])
                    ins.then_inc(s["t_m_p"], 1) if h == NH - 1 else link(ins)
                m_out(m)
            for m in range(NT):
                stats(G3 + m, x2[:, m], lambda e, m=m: e.wait_ge(s["t_m_e"], 2 * (m + 1)))
            act.wait_ge(s["t_r_dve"], 1)
            nc.scalar.activation(gex, gex, ACT.Exp).then_inc(s["t_r_ge"], 1)
            act.wait_ge(s["t_r_dve"], 2)
            nc.scalar.activation(wts[:, 1], wts[:, 1], ACT.Exp).then_inc(s["t_r_ge"], 1)
            act.wait_ge(s["t_r_dve"], 5)
            act_experts(act, moe, 0)
            with overflow(act):
                pass_end(act, moe, 0)
                with act.Fori(0, PASSES - 1) as p:
                    act_experts(act, moe, (p + 1) * NE)
                    pass_end(act, moe, (p + 1) * NE)
            act_tail3(act, link, stats)

        def dve_experts(dve, v, q, base):
            def tokens(e, b):
                for k in range(2):
                    dve.wait_ge(q["tr"], 2 * base + (2 * e + k + 1))
                    v.tensor_tensor(hgT[b][:, 4 * k:4 * k + 4], psum[k][:, :].rearrange("p (a t) -> p a t", a=4),
                                    bc(pcol[:, PC["ffn"] + 4 * k:PC["ffn"] + 4 * k + 4], 2, [P, 4, P]),
                                    ALU.mult).then_inc(q["ht"], 1)

            def step(e, j):
                b = j % 2
                dve.wait_ge(q["sg"], base + (e + 1))
                after(dve, q["at"], base, e - 1)
                v.tensor_tensor(actv[:, b], sg[:, b], psum[2 + 4 * b][:, FE:2 * FE], ALU.mult).then_inc(q["ac"], 1)
                if not (isinstance(e, int) and e >= NE - 2):
                    tokens(e + 2, b)
                dve.wait_ge(q["dn"], base + (e + 1))
                after(dve, (q["st0"], q["st1"])[b], 8 * base, gathers(e, b) - 16)
                v.tensor_copy(ysb[b][:, HALF:D], psum[5][:, :]).then_inc(q["y"], 1)
            tokens(0, 0)
            tokens(1, 1)
            each_expert(dve, step)

        def dve_tail2(dve, v, link, scale_rows, gains):
            dve.wait_ge(s["t_x2"], 16)

            def add(m, hf, bank):
                part = x2[:, m, hf * HALF:(hf + 1) * HALF]
                return v.tensor_tensor(part, part, bank[:, :], ALU.add)

            for m in range(NT + 1):
                if m < NT:
                    for hf in range(2):
                        u = 2 * m + hf
                        dve.wait_ge(s["t_o_r"], u + 1)
                        add(m, hf, psum[2 + u % 3]).then_inc(s["t_o_e"], 1)
                if m >= 1:
                    g = G2 + m - 1
                    scale_rows(g, x2[:, m - 1])
                    gains(g, PC["mem"], hT, slice((m - 1) * P, m * P))

            def m_out(m):
                dve.wait_ge(s["t_m_pv"], m + 1)
                link(v.reciprocal(m_col[:, 2, m], m_col[:, 1, m]))
                v.tensor_tensor(m_o[m % 2].rearrange("p (h d) -> p h d", d=HD),
                                psum[7][:, 0:GW].rearrange("p (h d) -> p h d", d=HD),
                                bc(m_col[:, 2, m], 2, [P, NH, HD]), ALU.mult).then_inc(s["t_m_o"], 1)
                for hf in range(2):
                    dve.wait_ge(s["t_m_w"], 2 * m + hf + 1)
                    add(m, hf, psum[3 + hf]).then_inc(s["t_m_e"], 1)

            for m in range(NT):
                dve.wait_ge(s["t_m_sc"], m + 1)
                for par in range(2):
                    link(v.tensor_reduce(m_col[:, 0, m, 2 * par:2 * par + 2],
                                         psum[5 + par][:, :].rearrange("p (h k) -> p h k", h=2), AX.X, ALU.max))
                v.tensor_scalar(m_col[:, 0, m], m_col[:, 0, m], -QK_SCALE, None, ALU.mult).then_inc(s["t_m_mx"], 1)
                m_out(m)
            for m in range(NT):
                if m >= 2:
                    dve.wait_ge(s["t_xn"], 16 * (m - 1))
                scale_rows(G3 + m, x2[:, m])
                gains(G3 + m, PC["ffn"], hT, slice(m * P, (m + 1) * P))

            dve.wait_ge(s["t_rw"], 64)
            dve.wait_ge(s["t_z_ix"], 2)
            link(v.tensor_copy(io_f, io_i))
            link(v.memset(gpad, -3e38))
            dve.wait_ge(s["t_rl"], 1)
            link(v.tensor_tensor(lg, psum[2][:, 0:NT * NR].rearrange("p (m r) -> p m r", m=NT),
                                 bc(br, 1, [P, NT, NR]), ALU.add))
            grp = lg[:, :, 0:NG]
            link(v.tensor_copy(gpad[:, :, 0:NG], grp))
            for m in range(NT):
                link(v.max(gmx[:, m], gpad[:, m]))
                link(v.max_index(gix[:, m], gmx[:, m], gpad[:, m]))
            v.tensor_tensor(gex, grp, gmx[:, :, 0:1].to_broadcast([P, NT, NG]), ALU.subtract).then_inc(s["t_r_dve"], 1)
            link(v.tensor_copy(gself, gix[:, :, 0]))
            link(v.tensor_tensor(goh, bc(io_f[:, 0:NG], 1, [P, NT, NG]), bc(gself, 2, [P, NT, NG]), ALU.is_equal))
            for m in range(NT):
                link(v.tensor_tensor(gsum[:, m * NG:(m + 1) * NG], lg[:, m, NG:NR].rearrange("p (g e) -> p g e", g=NG),
                                     bc(goh[:, m], 2, [P, NG, EPG]), ALU.mult))
            link(v.tensor_reduce(sel, gsum.rearrange("p (m g) e -> p m e g", g=NG), AX.X, ALU.add))
            for m in range(NT):
                link(v.max(smx[:, m], sel[:, m]))
                link(v.max_index(six[:, m], smx[:, m], sel[:, m]))
            v.tensor_tensor(wts[:, 1], smx[:, :, 1], smx[:, :, 0], ALU.subtract).then_inc(s["t_r_dve"], 1)
            for k in range(TK):
                link(v.tensor_copy(rank[:, k], six[:, :, k]))
                link(v.scalar_tensor_tensor(eid[:, k], gself, float(EPG), rank[:, k], ALU.mult, ALU.add))
                link(v.tensor_tensor(oh[k], bc(io_f, 1, [P, NT, NE]), bc(eid[:, k], 2, [P, NT, NE]), ALU.is_equal))
            link(v.tensor_tensor(asum, oh[0], oh[1], ALU.add))
            link(v.memset(apre[:, 0], 0.0))
            for m in range(1, NT):
                link(v.tensor_tensor(apre[:, m], apre[:, m - 1], asum[:, m - 1], ALU.add))
            v.tensor_copy(totf, apre[:, NT - 1]).then_inc(s["t_r_dve"], 1)
            dve.wait_ge(s["t_r_ge"], 2)
            link(v.tensor_reduce(pg, gex, AX.X, ALU.add))
            link(v.reciprocal(pg, pg))
            link(v.tensor_scalar(wts[:, 0], wts[:, 1], 1.0, None, ALU.add))
            link(v.reciprocal(wts[:, 0], wts[:, 0]))
            link(v.tensor_tensor(wts[:, 0], wts[:, 0], pg, ALU.mult))
            link(v.tensor_tensor(wts[:, 1], wts[:, 1], wts[:, 0], ALU.mult))
            dve.wait_ge(s["t_r_rk"], 1)
            for k in range(TK):
                link(v.tensor_tensor(rtmp, oh[k], psum[3][:, 0:NT * NE].rearrange("p (m e) -> p m e", m=NT), ALU.mult))
                link(v.tensor_reduce(rank[:, k], rtmp, AX.X, ALU.add))
                link(v.scalar_tensor_tensor(rank[:, k], rank[:, k], float(NE), eid[:, k], ALU.mult, ALU.add))
            link(v.tensor_reduce(totf[:, 0:1], psum[3][:, NT * NE:(NT + 1) * NE], AX.X, ALU.max))
            v.tensor_copy(toti[:, 0:1], totf[:, 0:1]).then_inc(s["t_r_dve"], 1)
            v.tensor_copy(slots, rank).then_inc(s["t_r_dve"], 1)
            dve_experts(dve, v, moe, 0)
            with overflow(dve):
                pass_end(dve, moe, 0)
                with dve.Fori(0, PASSES - 1) as p:
                    dve_experts(dve, v, moe, (p + 1) * NE)
                    pass_end(dve, moe, (p + 1) * NE)
            dve_tail3(dve, v, link)

        def pe_experts(pe, mm, q, base):
            def tr(e, b):
                pe.wait_ge((q["g0"], q["g1"])[b], 8 * base + gathers(e, b))
                for k in range(2):
                    after(pe, q["ht"], 2 * base, 2 * e + (k - 1))
                    for t in range(4):
                        c = (4 * k + t) * P
                        ins = nc.tensor.transpose(psum[k][:, t * P:(t + 1) * P], hg[b][:, c:c + P], ident[:, :])
                    ins.then_inc(q["tr"], 1)

            def gate_up(e, j):
                b = j % 2
                pe.wait_ge((q["wl0"], q["wl1"], q["wl2"], q["wl3"])[j], 8 * base + weights(e, j))
                pe.wait_ge(q["ht"], 2 * base + 2 * (e + 1))
                after(pe, q["ac"], base, e - 1)
                for k in range(KT):
                    ins = mm(psum[2 + 4 * b][:, :], hgT[b][:, k], w_gu[j][:, k], start=(k == 0), stop=(k == KT - 1))
                ins.then_inc(q["gu"], 1)

            def act_tr(e, j):
                b = j % 2
                pe.wait_ge(q["ac"], base + (e + 1))
                after(pe, q["ats"], base, e)
                for k in range(FE // P):
                    ins = nc.tensor.transpose(psum[3][:, k * P:(k + 1) * P], actv[:, b, k * P:(k + 1) * P], ident[:, :])
                ins.then_inc(q["at"], 1)

            def down(e, j):
                b = j % 2
                pe.wait_ge(q["ats"], base + (e + 1))
                after(pe, q["y"], 2 * base, 2 * e)
                for hf in range(2):
                    for k in range(FE // P):
                        ins = mm(psum[4 + hf][:, :], actT[b][:, k], w_dn[j][:, k, hf * HALF:(hf + 1) * HALF],
                                 start=(k == 0), stop=(k == FE // P - 1))
                ins.then_inc(q["dn"], 1)

            def step(e, j):
                first, last = (isinstance(e, int) and e == x for x in (0, NE - 1))
                gate_up(e, j)
                if not first:
                    act_tr(e - 1, (j - 1) % NB)
                if not last:
                    tr(e + 1, (j + 1) % 2)
                if not first:
                    down(e - 1, (j - 1) % NB)

            tr(0, 0)
            each_expert(pe, step)
            act_tr(NE - 1, NB - 1)
            down(NE - 1, NB - 1)

        def pe_tail2(pe, mm, transposes):
            rows = lambda h: slice(HD * (h % 2), HD * (h % 2) + HD)
            pe.wait_ge(s["l_out"], CT)
            pe.wait_ge(s["t_wo"], 16)

            for m in range(NT + 1):
                if m < NT:
                    for hf in range(2):
                        u = 2 * m + hf
                        if u >= 3:
                            pe.wait_ge(s["t_o_e"], u - 2)
                        for k in range(KT):
                            ins = mm(psum[2 + u % 3][:, :], yT[:, slot(k), m * P:(m + 1) * P],
                                     wo[:, k, hf * HALF:(hf + 1) * HALF], start=(k == 0), stop=(k == KT - 1))
                        ins.then_inc(s["t_o_r"], 1)
                if m >= 1:
                    transposes(G2 + m - 1)
            pe.wait_ge(s["t_o_e"], 2 * NT)
            pe.wait_ge(s["t_mq"], 16)
            for u in range(CT * NHALF):
                c, hf = u % CT, u // CT
                pe.wait_ge(s["ht_r"], 2 * (G2 + 4 * hf + 4))
                if u >= 3:
                    pe.wait_ge(s["t_q_e"], u - 2)
                for k in range(KT):
                    ins = mm(psum[2 + u % 3][:, :], mq[:, k, c * P:(c + 1) * P], hT[:, k, hf * HALF:(hf + 1) * HALF],
                             start=(k == 0), stop=(k == KT - 1))
                ins.then_inc(s["t_q_r"], 1)
            pe.wait_ge(s["t_q_e"], CT * NHALF)
            pe.wait_ge(s["t_mo"], 16)

            def scores(m):
                if m >= 1:
                    pe.wait_ge(s["t_m_p"], m)
                for h in range(NH):
                    ins = mm(psum[5 + h % 2][:, (h // 2) * ML:(h // 2 + 1) * ML], mqT[rows(h), h // 2, m * P:(m + 1) * P],
                             memk[rows(h), h // 2, :], start=True, stop=True)
                ins.then_inc(s["t_m_sc"], 1)

            scores(0)
            for m in range(NT):
                pe.wait_ge(s["t_m_p"], m + 1)
                if m >= 1:
                    pe.wait_ge(s["t_m_pt"], m)
                for b in range(2):
                    for t in range(4):
                        h, k = (4 * b + t) // MT_, (4 * b + t) % MT_
                        ins = nc.tensor.transpose(psum[b][:, t * P:(t + 1) * P], m_p[m % 2][:, h, k * P:(k + 1) * P],
                                                  ident[:, :])
                    ins.then_inc(s["t_m_tr"], 1)
                if m + 1 < NT:
                    scores(m + 1)
                pe.wait_ge(s["t_m_pt"], m + 1)
                if m >= 1:
                    pe.wait_ge(s["t_m_o"], m)
                for h in range(NH):
                    for k in range(MT_):
                        ins = mm(psum[7][:, h * HD:(h + 1) * HD], m_pT[m % 2][:, h * MT_ + k],
                                 memv[:, k, h * HD:(h + 1) * HD], start=(k == 0), stop=(k == MT_ - 1))
                ins.then_inc(s["t_m_pv"], 1)
                pe.wait_ge(s["t_m_o"], m + 1)
                if m >= 1:
                    pe.wait_ge(s["t_m_ots"], m)
                for c in range(CT):
                    ins = nc.tensor.transpose(psum[2][:, c * P:(c + 1) * P], m_o[m % 2][:, c * P:(c + 1) * P], ident[:, :])
                ins.then_inc(s["t_m_ot"], 1)
                pe.wait_ge(s["t_m_ots"], m + 1)
                for hf in range(2):
                    if m >= 1:
                        pe.wait_ge(s["t_m_e"], 2 * (m - 1) + hf + 1)
                    for c in range(CT):
                        ins = mm(psum[3 + hf][:, :], m_oT[m % 2][:, c], mo[:, c, hf * HALF:(hf + 1) * HALF],
                                 start=(c == 0), stop=(c == CT - 1))
                    ins.then_inc(s["t_m_w"], 1)
            for m in range(NT):
                transposes(G3 + m)
            pe.wait_ge(s["ht_r"], 2 * (G3 + NT))
            pe.wait_ge(s["t_rw"], 64)
            for m in range(NT):
                for k in range(KT):
                    ins = mm(psum[2][:, m * NR:(m + 1) * NR], hT[:, k, m * P:(m + 1) * P], wr[:, k],
                             start=(k == 0), stop=(k == KT - 1))
            ins.then_inc(s["t_rl"], 1)
            pe.wait_ge(s["t_r_dve"], 3)
            pe.wait_ge(s["t_m_e"], 2 * NT)
            flat = lambda t: t.rearrange("p m e -> p (m e)")
            mm(psum[3][:, 0:NT * NE], triu_s[:, :], flat(asum), start=True, stop=False)
            mm(psum[3][:, 0:NT * NE], ones[:, :], flat(apre), start=False, stop=True)
            tot = psum[3][:, NT * NE:(NT + 1) * NE]
            mm(tot, ones[:, :], apre[:, NT - 1], start=True, stop=False)
            mm(tot, ones[:, :], asum[:, NT - 1], start=False, stop=True).then_inc(s["t_r_rk"], 1)
            pe.wait_ge(s["t_r_dve"], 5)
            pe_experts(pe, mm, moe, 0)
            with overflow(pe):
                pass_end(pe, moe, 0)
                with pe.Fori(0, PASSES - 1) as p:
                    pe_experts(pe, mm, moe, (p + 1) * NE)
                    pass_end(pe, moe, (p + 1) * NE)

        def pool_experts(pool, q, base, p):
            def step(e, j):
                b = j % 2
                after(pool, q["tr"], 2 * base, 2 * (e - 1))
                after(pool, (q["g0"], q["g1"])[b], 8 * base, gathers(e, b) - 16)
                nc.gpsimd.tensor_copy(idxc[:, b:b + 1], idx_all[:, bass.ds(p * NE + e, 1)]).then_inc(q["ic"], 1)
                pool.drain()
                pool.indirect_dma_start(hg[b], None, xn_d, bass.IndirectOffsetOnAxis(ap=idxc[:, b:b + 1], axis=0)
                                        ).then_inc((q["g0"], q["g1"])[b], 16)
            each_expert(pool, step)

        def pool_tail2(pool):
            pool.wait_ge(s["t_o_r"], 2 * NT)
            nc.gpsimd.iota(tokid, [[P, NT]], base=0, channel_multiplier=1).then_inc(s["t_z_ix"], 1)
            nc.gpsimd.iota(io_i, [[1, NE]], base=0, channel_multiplier=0).then_inc(s["t_z_ix"], 1)
            nc.gpsimd.memset(idx_all, 0).then_inc(s["t_init0"], 1)
            pool.wait_ge(s["t_init0"], 1)
            pool.dma_start(slot_tok.rearrange("(r q) o -> r (q o)", r=P), idx_all).then_inc(s["t_zt_d"], 16)
            pool.wait_ge(s["t_zt_d"], 16)
            pool.wait_ge(s["t_z_ix"], 2)
            pool.wait_ge(s["t_r_dve"], 5)
            for k in range(TK):
                for m in range(NT):
                    pool.indirect_dma_start(slot_tok, bass.IndirectOffsetOnAxis(ap=slots[:, k, m:m + 1], axis=0),
                                            tokid[:, m:m + 1], None).then_inc(s["t_sc_d"], 16)
            pool.wait_ge(s["t_sc_d"], 16 * TK * NT)
            pool.dma_start(idx_all.rearrange("r (p e) -> r p e", e=NE),
                           slot_tok.rearrange("(p r e) o -> r p (e o)", r=P, e=NE)).then_inc(s["t_ix_ld"], 16)
            pool.wait_ge(s["t_ix_ld"], 16)
            pool.wait_ge(s["t_xn"], 16 * NT)
            pool_experts(pool, moe, 0, 0)
            with overflow(pool):
                pass_end(pool, moe, 0)
                with pool.Fori(0, PASSES - 1) as p:
                    pool_experts(pool, moe, (p + 1) * NE, p + 1)
                    pass_end(pool, moe, (p + 1) * NE)
                gather_outputs(pool, y_d)
            with pool.Else():
                gather_outputs(pool, y_d[0:NE * P, :])

        def gather_outputs(pool, rows):
            pool.wait_ge(moe["st0"], 8 * NE)
            pool.wait_ge(moe["st1"], 8 * NE)
            for m in range(NT):
                if m >= 2:
                    pool.wait_ge(s["f_c"], m - 1)
                for k in range(TK):
                    pool.indirect_dma_start(yg[2 * (m % 2) + k], None, rows,
                                            bass.IndirectOffsetOnAxis(ap=slots[:, k, m:m + 1], axis=0)
                                            ).then_inc((s["f_g0"], s["f_g1"])[m % 2], 16)

        G4 = G3 + NT

        def dve_tail3(dve, v, link):
            dve.wait_ge(s["t_fg"], 16)
            for m in range(NT + 1):
                if m < NT:
                    dve.wait_ge((s["f_g0"], s["f_g1"])[m % 2], 32 * (m // 2 + 1))
                    for k in range(TK):
                        ins = v.scalar_tensor_tensor(x2[:, m], yg[2 * (m % 2) + k], wts[:, k, m:m + 1], x2[:, m],
                                                     ALU.mult, ALU.add)
                        link(ins) if k == 0 else ins.then_inc(s["f_c"], 1)
                if m >= 1:
                    q = m - 1
                    dve.wait_ge(s["rstd_r"], G4 + q + 1)
                    if q >= 2:
                        dve.wait_ge((s["f_ot0"], s["f_ot1"])[q % 2], 16 * (q // 2))
                    v.scalar_tensor_tensor(xs[q % 2], x2[:, q], rstd[:, (G4 + q) % 4:(G4 + q) % 4 + 1], fin_g,
                                           ALU.mult, ALU.mult).then_inc(s["xs_r"], 1)

        def act_tail3(act, link, stats):
            for m in range(NT):
                stats(G4 + m, x2[:, m], lambda e, m=m: e.wait_ge(s["f_c"], m + 1))

        def sp_tail3(sp):
            for m in range(NT):
                sp.wait_ge(s["xs_r"], G4 + m + 1)
                sp.dma_start(out[m * P:(m + 1) * P, :], xs[m % 2]).then_inc((s["f_ot0"], s["f_ot1"])[m % 2], 16)
            sp.wait_ge(s["f_ot0"], 16 * (NT // 2))
            sp.wait_ge(s["f_ot1"], 16 * (NT // 2))
        @block.sync
        def _(sp):
            def x_tile(g):
                if g >= 2:
                    sp.wait_ge(s["xs_r"], g - 1)
                src = mem[g * P:(g + 1) * P, :] if g < MT_ else x[(g - MT_) * P:(g - MT_ + 1) * P, :]
                sp.dma_start(xin[g % 2], src).then_inc(s["x_in0"] if g % 2 == 0 else s["x_in1"], 16)

            def w_chunk(c):
                if c >= 2:
                    sp.wait_ge(s["unit_r"], END_OF[c - 2])
                src, c0, width, _p = CHUNKS[c]
                sp.dma_start(wbuf[c % 2][:, :, 0:width],
                             src[:, c0:c0 + width].rearrange("(k p) n -> p k n", p=P)).then_inc(
                                 s["w_ld0"] if c % 2 == 0 else s["w_ld1"], 16)

            x_tile(0)
            x_tile(1)
            w_chunk(0)
            w_chunk(1)
            for g in range(2, MT_ + NT):
                x_tile(g)
            for c in range(2, len(CHUNKS)):
                w_chunk(c)
            sp_tail(sp)

        @block.gpsimd
        def _(pool):
            nc.gpsimd.iota(iota_f[:], [[1, P]], base=0, channel_multiplier=0).then_inc(s["consts_i"], 1)
            nc.gpsimd.iota(iota_p[:], [[0, P]], base=0, channel_multiplier=1).then_inc(s["consts_i"], 1)
            pool.wait_ge(s["consts_v"], 2)
            for g, w in enumerate((a["lru_wa"][0], a["lru_wx"][0])):
                for h in range(NH):
                    r = slice(HD * (h % 2), HD * (h % 2) + HD)
                    pool.dma_start(lru_w[r, g * CT + h // 2, r], w[h]).then_inc(s["l_w"], 16)
            k = 0
            for n in range(NT):
                for lv in range(1, NL):
                    if lv == 1:
                        pool.wait_ge(s["g_MTs"], n + 1)
                    if k >= 2:
                        pool.wait_ge(s["g_T1"], k - 1)
                    nc.gpsimd.tensor_tensor(MTh[k % 2], gMT, bc(levT[:, lv], 1, [P, NH, P]),
                                            ALU.mult).then_inc(s["g_MTh"], 1)
                    k += 1
            pool_tail(pool)

        @block.scalar
        def _(act):
            link = chain(act, s["a_chain"])
            act.dma_start(prow[0:8, :], a["norm_mix"][0].rearrange("(r c) -> r c", c=P)).then_inc(s["params_in"], 16)
            act.dma_start(prow[8:16, :], a["norm_mem"][0].rearrange("(r c) -> r c", c=P)).then_inc(s["params_in"], 16)
            act.dma_start(prow[16:24, :], a["norm_memkv"][0].rearrange("(r c) -> r c", c=P)).then_inc(s["params_in"], 16)
            act.dma_start(prow[24:32, :], a["norm_ffn"][0].rearrange("(r c) -> r c", c=P)).then_inc(s["params_in"], 16)
            act.dma_start(prow[32:40, :], a["mix_gain"][0].rearrange("(r c) -> r c", c=P)).then_inc(s["params_in"], 16)
            act.dma_start(prow[40:48, :], a["lru_conv_w"][0].rearrange("t (r c) -> (t r) c", c=P)).then_inc(s["params_in"], 16)
            for i, v in enumerate((a["lru_conv_b"], a["lru_ba"], a["lru_bx"], a["lru_lam"])):
                act.dma_start(prow[48 + 2 * i:50 + 2 * i, :],
                              v[0].rearrange("(r c) -> r c", c=P)).then_inc(s["params_in"], 16)
            act.dma_start(prow[56:80, :], a["gdn_conv_w"][0].rearrange("t (r c) -> (t r) c", c=P)).then_inc(s["params_in"], 16)
            act.dma_start(fox_b[0:NH, :], a["fox_fb"].rearrange("a h -> h a")).then_inc(s["prm_in"], 16)
            act.dma_start(alog[:, :], a["gdn_a_log"][0:1, :].to_broadcast([P, NH])).then_inc(s["prm_in"], 16)
            act.dma_start(dtb[:, :], a["gdn_dt_bias"][0:1, :].to_broadcast([P, NH])).then_inc(s["prm_in"], 16)
            act.wait_ge(s["consts_v"], 1)

            def stats(g, src, wait):
                wait(act)
                if g >= 4:
                    act.wait_ge(s["xs_r"], g - 3)
                link(nc.scalar.activation(junk, src, ACT.Square, accum_out=ss[:, g % 4:g % 4 + 1]))
                link(nc.scalar.activation(ss[:, g % 4:g % 4 + 1], ss[:, g % 4:g % 4 + 1], ACT.Ln,
                                          bias=epsc[:, 0:1], scale=1.0 / D))
                nc.scalar.activation(rstd[:, g % 4:g % 4 + 1], ss[:, g % 4:g % 4 + 1], ACT.Exp,
                                     scale=-0.5).then_inc(s["rstd_r"], 1)

            def x_wait(g):
                return lambda e: e.wait_ge(s["x_in0"] if g % 2 == 0 else s["x_in1"], 16 * (g // 2 + 1))

            def evacuate(u):
                act.wait_ge(s["unit_r"], u + 1)
                to = UNITS[u][5]
                for i, (cols, dst) in enumerate(to):
                    rows = UNITS[u][3]
                    ins = nc.scalar.activation(dst, psum[PROJ_BANKS[u % 3]][0:rows, cols], ACT.Copy)
                    if i == len(to) - 1:
                        ins.then_inc(s["unit_e"], 1)
                    else:
                        link(ins)

            for g in range(MT_):
                stats(g, xin[g % 2], x_wait(g))
            for u in range(END_OF[1]):
                evacuate(u)
            for g in range(MT_, MT_ + NT):
                stats(g, xin[g % 2], x_wait(g))
            for u in range(END_OF[1], END_OF[5]):
                evacuate(u)

            for j in range(6):
                act.wait_ge(s["d_cvd"], j + 1)
                nc.scalar.activation(d_cv[:, j], d_cv[:, j], ACT.Silu).then_inc(s["d_sil"], 1)
            for j in range(4):
                act.wait_ge(s["d_sil"], j + 3)
                if j >= 2:
                    act.wait_ge(s["d_ssp"], j - 1)
                nc.scalar.activation(l2sq[j % 2], d_cv[:, 2 + j], ACT.Square).then_inc(s["d_sq"], 1)
                for h in range(NHALF):
                    act.wait_ge(s["d_ssp"], 2 * j + h + 1)
                    if j >= 2:
                        act.wait_ge(s["d_l2"], j - 1)
                    part = l2rs[j % 2][:, h * HALF:(h + 1) * HALF]
                    nc.scalar.activation(part, psum[5 + h][:, :], ACT.Ln, bias=epsc[:, 0:1]).then_inc(s["d_el"], 1)
                    act.wait_ge(s["d_el"], 2 * j + h + 1)
                    nc.scalar.activation(part, part, ACT.Exp, scale=-0.5).then_inc(s["d_rs"], 1)

            act.wait_ge(s["prm_in"], 48)
            link(nc.scalar.activation(sm_e, dba[:, :, 0:NH], ACT.Exp, scale=-1.0))
            link(nc.scalar.activation(nexp[:, 0], alog[:, :], ACT.Exp))
            act.wait_ge(s["g_beta"], 1)
            link(nc.scalar.activation(Gc, sm_t, ACT.Abs))
            link(nc.scalar.activation(Gc, Gc, ACT.Exp, scale=-1.0))
            nc.scalar.activation(Gl, Gc, ACT.Ln, bias=1.0).then_inc(s["g_el"], 1)
            act.wait_ge(s["g_Gv"], 1)
            link(nc.scalar.activation(eG, Gc, ACT.Exp))
            link(nc.scalar.activation(kds, kds, ACT.Exp))
            nc.scalar.activation(gle, Gl, ACT.Exp).then_inc(s["g_el"], 1)

            filler = iter(range(END_OF[5], len(UNITS)))
            for n in range(NT):
                act.wait_ge(s["g_D"], n + 1)
                if n >= 1:
                    act.wait_ge(s["g_qd"], n)
                nc.scalar.activation(eR, psum[5][:, :], ACT.Exp).then_inc(s["g_eR"], 1)
                act.wait_ge(s["g_mm"], 2 * n + 2)
                nc.scalar.activation(gam, gam, ACT.Exp, scale=-1.0).then_inc(s["g_ex"], 1)
                nc.scalar.activation(gamT, gamT, ACT.Exp).then_inc(s["g_ex"], 1)
                act.wait_ge(s["g_MT"], n + 1)
                if n >= 1:
                    act.wait_ge(s["g_MTh"], (NL - 1) * n)
                nc.scalar.activation(gMT, psum[5][:, :], ACT.Copy).then_inc(s["g_MTs"], 1)
                for lv in range(1, NL):
                    k = (NL - 1) * n + lv
                    act.wait_ge(s["g_T1"], k)
                    if k >= 2:
                        act.wait_ge(s["g_XY"], k - 1)
                    nc.scalar.activation(gT1, psum[6][:, :], ACT.Copy).then_inc(s["g_T1s"], 1)
                    u = next(filler, None)
                    if u is not None:
                        evacuate(u)
                u = next(filler, None)
                if u is not None:
                    evacuate(u)
                act.wait_ge(s["g_wk"], n + 1)
                if n >= 1:
                    act.wait_ge(s["g_vn"], n)
                nc.scalar.activation(wkT, psum[6][:, 0:CT * P], ACT.Copy, scale=-1.0).then_inc(s["g_wks"], 1)
                act.wait_ge(s["g_o"], n + 1)
                for par in range(2):
                    ins = nc.scalar.activation(d_o[:, :, n * P + par * HD:n * P + (par + 1) * HD],
                                               psum[7 - par][:, 0:GW // 2].rearrange("p (c d) -> p c d", c=CT),
                                               ACT.Copy)
                    link(ins) if par == 0 else ins.then_inc(s["g_os"], 1)
            assert next(filler, None) is None

            def finish_act(f, o, gate, ready):
                ready(act)
                nc.scalar.activation(fin_sq, o, ACT.Square).then_inc(s["f_sq"], 1)
                act.wait_ge(s["f_ss"], f + 1)
                link(nc.scalar.activation(fin_ss[:, :], fin_ss[:, :], ACT.Ln, bias=epsc[:, 0:1], scale=1.0 / HD))
                nc.scalar.activation(fin_ss[:, :], fin_ss[:, :], ACT.Exp, scale=-0.5).then_inc(s["f_rs"], 1)
                if gate is not None:
                    nc.scalar.activation(gate, gate, ACT.Silu).then_inc(s["f_sil"], 1)

            finish_act(0, d_o, d_z, lambda e: e.wait_ge(s["g_os"], NT))
            act_tail(act, link, finish_act, evacuate, stats)

        @block.vector
        def _(dve):
            v = nc.vector
            link = chain(dve, s["v_chain"])
            dve.wait_ge(s["consts_i"], 2)
            link(v.memset(epsc[:, :], EPS))
            v.tensor_tensor(xor_i[:, :], iota_f[:, :], iota_p[:, :], ALU.bitwise_xor).then_inc(s["consts_v"], 1)
            link(v.tensor_copy(fidx[:, :], iota_f[:, :]))
            link(v.tensor_copy(pidx[:, :], iota_p[:, :]))
            dve.wait_ge(s["consts_v"], 1)
            link(v.tensor_copy(xor_f[:, :], xor_i[:, :]))
            link(v.tensor_tensor(ident[:, :], fidx[:, :], pidx[:, :], ALU.is_equal))
            link(v.tensor_tensor(triu[:, :], fidx[:, :], pidx[:, :], ALU.is_ge))
            link(v.tensor_tensor(triu_s[:, :], fidx[:, :], pidx[:, :], ALU.is_gt))
            link(v.tensor_tensor(tril_s[:, :], fidx[:, :], pidx[:, :], ALU.is_lt))
            link(v.tensor_scalar(negmask[:, :], triu_s[:, :], -1e30, None, ALU.mult))
            link(v.memset(ones[:, :], 1.0))
            link(v.tensor_scalar(tmp_mask[:, :], pidx[:, :], float(HD), None, ALU.is_ge))
            link(v.scalar_tensor_tensor(head_ones[:, :], fidx[:, :], float(HD), tmp_mask[:, :],
                                        ALU.is_ge, ALU.is_equal))
            for lv, h in enumerate(LEVELS):
                link(v.scalar_tensor_tensor(tmp_mask[:, :], xor_f[:, :], float(h), triu_s[:, :], ALU.is_ge, ALU.mult))
                link(v.scalar_tensor_tensor(levT[:, lv], xor_f[:, :], float(2 * h), tmp_mask[:, :],
                                            ALU.is_lt, ALU.mult))
            link(v.tensor_copy(levT[:, NL], ident[:, :]))
            link(v.scalar_tensor_tensor(lev1[:, :], xor_f[:, :], 2.0, tril_s[:, :], ALU.is_lt, ALU.mult))
            link(v.memset(d_raw[:, :, 0:PAD], 0.0))
            link(v.memset(c_x[:, :, 0:PAD], 0.0))
            link(v.memset(lru_w[:, :, :], 0.0))
            v.memset(gS[:, :, :], 0.0).then_inc(s["consts_v"], 1)
            dve.wait_ge(s["pcol_t"], 1)
            v.tensor_copy(pcol[:, :], psum[7][:, 0:80]).then_inc(s["pcol_v"], 1)
            dve.wait_ge(s["pcol_v"], 1)

            def scale_rows(g, src):
                dve.wait_ge(s["rstd_r"], g + 1)
                if g >= 2:
                    dve.wait_ge(s["tr_r"], 2 * (g - 1))
                v.tensor_scalar(xs[g % 2], src, rstd[:, g % 4:g % 4 + 1], None, ALU.mult).then_inc(s["xs_r"], 1)

            def gains(g, gain, dst, cols):
                for b in range(2):
                    dve.wait_ge(s["tr_r"], 2 * g + b + 1)
                    v.tensor_tensor(dst[:, 4 * b:4 * b + 4, cols], psum[b][:, :].rearrange("p (k t) -> p k t", k=4),
                                    bc(pcol[:, gain + 4 * b:gain + 4 * b + 4], 2, [P, 4, P]),
                                    ALU.mult).then_inc(s["ht_r"], 1)

            for lo, hi in ((0, MT_), (MT_, MT_ + NT)):
                for g in range(lo, hi + 1):
                    if g < hi:
                        scale_rows(g, xin[g % 2])
                    q = g - 1
                    if q >= lo and lo == 0:
                        gains(q, PC["memkv"], memT, slice(q * P, (q + 1) * P))
                    elif q >= lo:
                        gains(q, PC["mix"], hT, slice((q - MT_) * P, (q - MT_ + 1) * P))

            for j in range(6):
                if j % 2 == 0:
                    dve.wait_ge(s["unit_e"], END_OF[4 - j // 2])
                grp, ct = 2 - j // 2, j % 2
                w = lambda t: pcol[:, PC["gconv"] + 6 * t + 2 * grp + ct:PC["gconv"] + 6 * t + 2 * grp + ct + 1]
                link(v.tensor_scalar(d_cv[:, j], d_raw[:, j, 0:T], w(0), None, ALU.mult))
                for t in range(1, TAPS):
                    ins = v.scalar_tensor_tensor(d_cv[:, j], d_raw[:, j, t:t + T], w(t), d_cv[:, j], ALU.mult, ALU.add)
                    if t < TAPS - 1:
                        link(ins)
                    else:
                        ins.then_inc(s["d_cvd"], 1)
            for j in range(4):
                dve.wait_ge(s["d_rs"], 2 * j + 2)
                v.scalar_tensor_tensor(d_cv[:, 2 + j], d_cv[:, 2 + j], 1.0 if j < 2 else QK_SCALE, l2rs[j % 2],
                                       ALU.mult, ALU.mult).then_inc(s["d_l2"], 1)
            dve.wait_ge(s["unit_e"], END_OF[5])
            dve.wait_ge(s["prm_in"], 48)
            v.tensor_tensor(sm_t, dba[:, :, NH:2 * NH], bc(dtb[:, :], 1, [P, NT, NH]), ALU.add).then_inc(s["g_beta"], 1)
            dve.wait_ge(s["g_el"], 1)
            link(v.tensor_scalar(sm_e, sm_e, 1.0, None, ALU.add))
            link(v.reciprocal(beta, sm_e))
            link(v.scalar_tensor_tensor(sm_t, sm_t, 0.0, Gl, ALU.max, ALU.add))
            v.scalar_tensor_tensor(gg, sm_t, -1.0, bc(nexp[:, 0], 1, [P, NT, NH]), ALU.mult,
                                   ALU.mult).then_inc(s["g_beta"], 1)
            dve.wait_ge(s["g_Gp"], 1)
            gp = psum[5]
            link(v.tensor_copy(Gc, gp[:, 0:NHT].rearrange("p (n h) -> p n h", h=NH)))
            link(v.tensor_copy(Gl, gp[:, NHT:2 * NHT].rearrange("p (n h) -> p n h", h=NH)))
            v.tensor_tensor(kds, Gl, Gc, ALU.subtract).then_inc(s["g_Gv"], 1)
            dve.wait_ge(s["g_el"], 2)
            link(v.tensor_tensor(beG, beta, eG, ALU.mult))
            link(v.tensor_copy(glS[0:HD, :, :], gle[0:HD, :, 0:NH:2]))
            v.tensor_copy(glS[HD:P, :, :], gle[HD:P, :, 1:NH:2]).then_inc(s["g_cols"], 1)
            dve.wait_ge(s["g_cols"], 1)

            for n in range(NT):
                tok = slice(n * P, (n + 1) * P)
                col = lambda c, w: bc(c[:, n], 2, [P, NH, w])
                b5, b6, b7 = [psum[i][:, :].rearrange("p (h t) -> p h t", h=NH) for i in (5, 6, 7)]
                dve.wait_ge(s["g_R"], n + 1)
                v.tensor_tensor(gD, b5, col(Gc, P), ALU.subtract).then_inc(s["g_D"], 1)
                dve.wait_ge(s["g_D"], n + 1)
                v.tensor_scalar(gam, gD, 0.0, None, ALU.max).then_inc(s["g_mm"], 1)
                v.tensor_scalar(gamT, gD, 0.0, None, ALU.min).then_inc(s["g_mm"], 1)
                dve.wait_ge(s["g_KV"], n + 1)
                b0 = psum[0][:, :].rearrange("p (w h d) -> p w h d", w=2, h=NH)
                link(v.tensor_tensor(kvb[:, :, 0:HD], b0[:, 1], col(beta, HD), ALU.mult))
                link(v.tensor_tensor(kvb[:, :, HD:P], b0[:, 0], col(beG, HD), ALU.mult))
                v.tensor_tensor(kdec, b0[:, 0], col(kds, HD), ALU.mult).then_inc(s["g_kv"], 1)
                dve.wait_ge(s["g_eR"], n + 1)
                for h in range(NH):
                    r = slice(HD * (h % 2), HD * (h % 2) + HD)
                    ins = v.tensor_tensor(qd[r, h // 2], d_cv[r, 4 + h // 2, tok], eR[r, h], ALU.mult)
                    ins.then_inc(s["g_qd"], 1) if h == NH - 1 else link(ins)
                dve.wait_ge(s["g_ex"], 2 * n + 2)
                link(v.tensor_tensor(gam, gam, bc(tril_s[:, :], 1, [P, NH, P]), ALU.mult))
                link(v.tensor_tensor(gam, gam, col(beta, P), ALU.mult))
                dve.wait_ge(s["g_KK"], n + 1)
                link(v.tensor_tensor(gM[:, 0:NH:2], b6[:, 0:2], gam[:, 0:NH:2], ALU.mult))
                v.tensor_tensor(gM[:, 1:NH:2], b7[:, 0:2], gam[:, 1:NH:2], ALU.mult).then_inc(s["g_M"], 1)
                link(v.tensor_tensor(gamT, gamT, bc(triu[:, :], 1, [P, NH, P]), ALU.mult))
                link(v.tensor_tensor(gAT[:, 0:NH:2], b6[:, 2:4], gamT[:, 0:NH:2], ALU.mult))
                v.tensor_tensor(gAT[:, 1:NH:2], b7[:, 2:4], gamT[:, 1:NH:2], ALU.mult).then_inc(s["g_AT"], 1)
                dve.wait_ge(s["g_M"], n + 1)
                link(v.tensor_tensor(gX, gM, bc(lev1[:, :], 1, [P, NH, P]), ALU.mult))
                link(v.tensor_tensor(gX, bc(ident[:, :], 1, [P, NH, P]), gX, ALU.subtract))
                dve.wait_ge(s["g_MTs"], n + 1)
                link(v.tensor_tensor(gY, gMT, bc(levT[:, 0], 1, [P, NH, P]), ALU.mult))
                v.tensor_tensor(gY, bc(ident[:, :], 1, [P, NH, P]), gY, ALU.subtract).then_inc(s["g_upd"], 1)
                for lv in range(1, NL):
                    k = (NL - 1) * n + lv
                    dve.wait_ge(s["g_upd"], NL * n + lv)
                    dve.wait_ge(s["g_XY"], k)
                    if lv < NL - 1:
                        link(v.tensor_tensor(gX, gX, b7, ALU.subtract))
                    v.tensor_tensor(gY, gY, b5, ALU.subtract).then_inc(s["g_upd"], 1)
                dve.wait_ge(s["g_vn"], n + 1)
                for par in range(2):
                    ins = v.tensor_copy(vnew[:, par:NH:2, :],
                                        psum[1 - par][:, 0:GW // 2].rearrange("p (h d) -> p h d", d=HD))
                    link(ins) if par == 0 else ins.then_inc(s["g_vns"], 1)
                dve.wait_ge(s["g_dS"], n + 1)
                link(v.tensor_tensor(gS[:, :, :], gS[:, :, :], bc(glS[:, n], 2, [P, CT, HD]), ALU.mult))
                v.tensor_tensor(gS[:, :, :], gS[:, :, :], psum[5][:, 0:CT * HD].rearrange("p (c d) -> p c d", c=CT),
                                ALU.add).then_inc(s["g_S"], 1)

            def finish_dve(f, o, gate, c0):
                heads = lambda t: t.rearrange("p c (g d) -> p (c g) d", d=HD)
                dve.wait_ge(s["f_sq"], f + 1)
                v.tensor_reduce(fin_ss[:, :], heads(fin_sq), AX.X, ALU.add).then_inc(s["f_ss"], 1)
                dve.wait_ge(s["f_rs"], f + 1)
                G = NT * 2
                for c in range(CT):
                    oh = o[:, c].rearrange("p (g d) -> p g d", d=HD)
                    ins = v.tensor_tensor(oh, oh, bc(fin_ss[:, c * G:(c + 1) * G], 2, [P, G, HD]), ALU.mult)
                    if gate is None:
                        ins.then_inc(s["f_y"], 1)
                        continue
                    link(ins)
                    if c == 0:
                        dve.wait_ge(s["f_sil"], f + 1)
                    ot = o[:, c].rearrange("p (n q) -> p n q", q=P)
                    v.tensor_tensor(ot, ot, gate[:, :, c * P:(c + 1) * P], ALU.mult).then_inc(s["f_y"], 1)
                for c in range(CT):
                    for hf in range(2):
                        i = (f * CT + c) * 2 + hf
                        dve.wait_ge(s["f_tr"], i + 1)
                        v.tensor_scalar(yT[:, slot(c0 + c), hf * HALF:(hf + 1) * HALF], psum[i % 2][:, :],
                                        pcol[:, PC["gain"] + c0 + c:PC["gain"] + c0 + c + 1], None,
                                        ALU.mult).then_inc(s["f_out"], 1)

            finish_dve(0, d_o, d_z, 6)
            dve_tail(dve, v, link, finish_dve, scale_rows, gains)

        @block.tensor
        def _(pe):
            mm = nc.tensor.matmul
            pe.wait_ge(s["consts_v"], 2)
            pe.wait_ge(s["params_in"], 16 * 11)
            nc.tensor.transpose(psum[7][:, 0:80], prow[0:80, :], ident[0:80, 0:80]).then_inc(s["pcol_t"], 1)

            def transposes(g):
                pe.wait_ge(s["xs_r"], g + 1)
                for b in range(2):
                    if g >= 1:
                        pe.wait_ge(s["ht_r"], 2 * (g - 1) + b + 1)
                    for k in range(4):
                        c = (4 * b + k) * P
                        ins = nc.tensor.transpose(psum[b][:, k * P:(k + 1) * P], xs[g % 2][:, c:c + P], ident[:, :])
                    ins.then_inc(s["tr_r"], 1)

            def unit(u):
                c, lhs, rhs, rows, n, _to = UNITS[u]
                if u == 0 or UNITS[u - 1][0] != c:
                    pe.wait_ge(s["w_ld0"] if c % 2 == 0 else s["w_ld1"], 16 * (c // 2 + 1))
                if u >= 3:
                    pe.wait_ge(s["unit_e"], u - 2)
                bank = psum[PROJ_BANKS[u % 3]]
                for k in range(KT):
                    ins = mm(bank[0:rows, 0:n], lhs(k), rhs(k), start=(k == 0), stop=(k == KT - 1))
                ins.then_inc(s["unit_r"], 1)

            for g in range(MT_):
                transposes(g)
            pe.wait_ge(s["ht_r"], 2 * MT_)
            for u in range(END_OF[1]):
                unit(u)
            for g in range(MT_, MT_ + NT):
                transposes(g)
            pe.wait_ge(s["ht_r"], 2 * (MT_ + NT))
            for u in range(END_OF[1], END_OF[5]):
                unit(u)
            for j in range(4):
                pe.wait_ge(s["d_sq"], j + 1)
                for h in range(NHALF):
                    if j >= 1:
                        pe.wait_ge(s["d_el"], 2 * (j - 1) + h + 1)
                    mm(psum[5 + h][:, :], head_ones[:, :], l2sq[j % 2][:, h * HALF:(h + 1) * HALF],
                       start=True, stop=True).then_inc(s["d_ssp"], 1)
            pe.wait_ge(s["g_beta"], 2)
            pe.wait_ge(s["d_el"], 8)
            mm(psum[5][:, 0:NHT], triu[:, :], gg.rearrange("p n h -> p (n h)"), start=True, stop=True)
            mm(psum[5][:, NHT:2 * NHT], ones[:, :], gg.rearrange("p n h -> p (n h)"), start=True,
               stop=True).then_inc(s["g_Gp"], 1)
            pe.wait_ge(s["d_l2"], 4)
            pe.wait_ge(s["g_cols"], 1)

            filler = iter(range(END_OF[5], len(UNITS)))

            def fill():
                u = next(filler, None)
                if u is not None:
                    unit(u)

            for n in range(NT):
                tok = slice(n * P, (n + 1) * P)
                rows = lambda h: slice(HD * (h % 2), HD * (h % 2) + HD)
                hp = lambda h: slice(h * P, (h + 1) * P)
                hd = lambda h: slice(h * HD, (h + 1) * HD)
                if n >= 1:
                    pe.wait_ge(s["g_S"], n)
                for h in range(NH):
                    ins = mm(psum[5][:, hp(h)], gg[:, n, h:h + 1].to_broadcast([P, P]), triu[:, :],
                             start=True, stop=True)
                ins.then_inc(s["g_R"], 1)
                if n >= 1:
                    pe.wait_ge(s["g_os"], n)
                for h in range(NH):
                    bank = psum[6 + h % 2]
                    mm(bank[:, hp(h // 2)], d_cv[rows(h), 2 + h // 2, tok], d_cv[rows(h), 2 + h // 2, tok],
                       start=True, stop=True)
                    ins = mm(bank[:, hp(2 + h // 2)], d_cv[rows(h), 2 + h // 2, tok], d_cv[rows(h), 4 + h // 2, tok],
                             start=True, stop=True)
                ins.then_inc(s["g_KK"], 1)
                if n >= 1:
                    pe.wait_ge(s["g_vns"], n)
                for c in range(4):
                    j = 2 + c if c < 2 else c - 2
                    ins = nc.tensor.transpose(psum[0][:, hp(c)], d_cv[:, j, tok], ident[:, :])
                ins.then_inc(s["g_KV"], 1)
                fill()
                pe.wait_ge(s["g_M"], n + 1)
                pe.wait_ge(s["g_eR"], n + 1)
                pe.wait_ge(s["g_D"], n + 1)
                for h in range(NH):
                    ins = nc.tensor.transpose(psum[5][:, hp(h)], gM[:, h], ident[:, :])
                ins.then_inc(s["g_MT"], 1)
                pe.wait_ge(s["g_AT"], n + 1)
                for lv in range(1, NL):
                    k = (NL - 1) * n + lv
                    pe.wait_ge(s["g_MTh"], k)
                    pe.wait_ge(s["g_upd"], NL * n + lv)
                    for h in range(NH):
                        ins = mm(psum[6][:, hp(h)], MTh[(k - 1) % 2][:, h], gX[:, h], start=True, stop=True)
                    ins.then_inc(s["g_T1"], 1)
                    fill()
                    pe.wait_ge(s["g_T1s"], k)
                    if lv == 1:
                        pe.wait_ge(s["g_MTs"], n + 1)
                    if lv < NL - 1:
                        for h in range(NH):
                            mm(psum[7][:, hp(h)], gY[:, h], gT1[:, h], start=True, stop=True)
                    for h in range(NH):
                        ins = mm(psum[5][:, hp(h)], gT1[:, h], gY[:, h], start=True, stop=True)
                    ins.then_inc(s["g_XY"], 1)
                pe.wait_ge(s["g_upd"], NL * n + NL)
                pe.wait_ge(s["g_kv"], n + 1)
                for h in range(NH):
                    ins = mm(psum[6][rows(h), (h // 2) * P:(h // 2 + 1) * P], kvb[:, h, HD:P], gY[:, h],
                             start=True, stop=True)
                ins.then_inc(s["g_wk"], 1)
                pe.wait_ge(s["g_wks"], n + 1)
                pe.wait_ge(s["g_S"], n) if n >= 1 else None
                for h in range(NH):
                    bank = psum[1 - h % 2]
                    mm(bank[:, hd(h // 2)], gY[:, h], kvb[:, h, 0:HD], start=True, stop=False)
                    ins = mm(bank[:, hd(h // 2)], wkT[rows(h), h // 2], gS[rows(h), h // 2], start=False, stop=True)
                ins.then_inc(s["g_vn"], 1)
                pe.wait_ge(s["g_vns"], n + 1)
                pe.wait_ge(s["g_qd"], n + 1)
                for h in range(NH):
                    bank = psum[7 - h % 2]
                    mm(bank[:, hd(h // 2)], qd[rows(h), h // 2], gS[rows(h), h // 2], start=True, stop=False)
                    ins = mm(bank[:, hd(h // 2)], gAT[:, h], vnew[:, h], start=False, stop=True)
                ins.then_inc(s["g_o"], 1)
                for h in range(NH):
                    ins = mm(psum[5][rows(h), (h // 2) * HD:(h // 2 + 1) * HD], kdec[:, h], vnew[:, h],
                             start=True, stop=True)
                ins.then_inc(s["g_dS"], 1)
            assert next(filler, None) is None

            def finish_pe(f, o):
                pe.wait_ge(s["f_y"], CT * (f + 1))
                for c in range(CT):
                    for hf in range(2):
                        i = (f * CT + c) * 2 + hf
                        if i >= 2:
                            pe.wait_ge(s["f_out"], i - 1)
                        for t in range(4):
                            n = 4 * hf + t
                            ins = nc.tensor.transpose(psum[i % 2][:, t * P:(t + 1) * P], o[:, c, n * P:(n + 1) * P],
                                                      ident[:, :])
                        ins.then_inc(s["f_tr"], 1)

            finish_pe(0, d_o)
            pe_tail(pe, mm, finish_pe, transposes)


_INS = ["x", "mem", "norm_mix", "w_in", "hgrn_lb", "fox_fb", "lru_conv_w", "lru_conv_b", "lru_wa", "lru_ba", "lru_wx",
        "lru_bx", "lru_lam", "gdn_conv_w", "gdn_a_log", "gdn_dt_bias", "mix_gain", "w_out", "norm_mem", "norm_memkv",
        "w_mq", "w_mkv", "w_mo", "norm_ffn", "w_rg", "b_rg", "w_re", "b_re", "w_e_gu", "w_e_dn", "norm_final"]


def kernel(**inputs):
    import numpy as np
    import concourse.bacc as bacc
    from concourse.bass_utils import run_bass_kernel_spmd

    nc = bacc.Bacc("TRN2", target_bir_lowering=False, num_devices=1)
    arrays, aps = {}, {}
    for name in _INS:
        v = np.ascontiguousarray(inputs[name])
        arrays[f"in_{name}"] = v
        aps[name] = nc.dram_tensor(f"in_{name}", v.shape, mybir.dt.from_np(v.dtype), kind="ExternalInput").ap()
    T, D = inputs["x"].shape[1:]
    out = nc.dram_tensor("out_0", (T, D), mybir.dt.float32, kind="ExternalOutput").ap()
    hybrid_trunk(nc, aps, out)
    r = run_bass_kernel_spmd(nc, [arrays], core_ids=[0])
    return r.results[0]["out_0"].reshape(1, T, D)
```

```python
import concourse.bass as bass
from concourse import mybir
from contextlib import ExitStack


def hybrid_trunk(nc, a, out):
    f32, i32, u32 = mybir.dt.float32, mybir.dt.int32, mybir.dt.uint32
    ALU, ACT, AX = mybir.AluOpType, mybir.ActivationFunctionType, mybir.AxisListType
    P = 128
    T, D = a["x"].shape[1], a["x"].shape[2]
    NT, KT = T // P, D // P
    GW = D // 4
    HD, NH = 64, GW // 64
    CT = GW // P
    ML = a["mem"].shape[1]
    MT_ = ML // P
    NE, FE = a["w_e_gu"].shape[1], a["w_e_dn"].shape[2]
    NG, EPG = a["w_rg"].shape[2], NE // a["w_rg"].shape[2]
    TAPS = a["lru_conv_w"].shape[1]
    LRU_C = 8.0
    EPS = 1e-6
    PAD = TAPS - 1
    TP = T + PAD
    HALF = 512
    NHALF = T // HALF
    QK_SCALE = HD ** -0.5
    LEVELS = [1, 2, 4, 8, 16, 32, 64]
    NL = len(LEVELS)

    x, mem, w_in = a["x"][0], a["mem"][0], a["w_in"][0]
    names = "aq af ai ag bq bk bv bf cx cg dq dk dv db da dz".split()
    sizes = [GW] * 7 + [NH] + [GW] * 5 + [NH, NH, GW]
    col = {n: sum(sizes[:i]) for i, n in enumerate(names)}

    ctx = ExitStack()
    with ctx:
        def sb(name, shape, dt=f32):
            return ctx.enter_context(nc.sbuf_tensor(name, [P] + list(shape), dt))

        ident = sb("ident", [P])
        ones = sb("ones", [P])
        triu = sb("triu", [P])
        triu_s = sb("triu_s", [P])
        tril_s = sb("tril_s", [P])
        head_ones = sb("head_ones", [P])
        levT = sb("levT", [NL + 1, P])
        lev1 = sb("lev1", [P])
        negmask = sb("negmask", [P])
        prow = sb("prow", [P])
        pcol = sb("pcol", [80])
        fox_b = sb("fox_b", [1])
        alog = sb("alog", [NH])
        dtb = sb("dtb", [NH])
        lru_w = sb("lru_w", [2 * CT, P])
        PC = dict(mix=0, mem=8, memkv=16, ffn=24, gain=32, lconv=40, lb=48, ba=50, bx=52, lam=54,
                             gconv=56)
        ss = sb("ss", [4])
        rms = sb("rms", [4])
        epsc = sb("epsc", [1])

        arena = sb("arena", [46300])
        at = [0]

        def place(n):
            at[0] += n
            assert at[0] <= 46300, at[0]
            return at[0] - n

        def view(off, *shape):
            n = 1
            for s in shape:
                n *= s
            v = arena[:, off:off + n]
            if len(shape) == 1:
                return v
            if len(shape) == 2:
                return v.rearrange("p (a b) -> p a b", a=shape[0])
            return v.rearrange("p (a b c) -> p a b c", a=shape[0], b=shape[1])

        WC = 264
        o_ht = place(KT * T)
        o_w = place(2 * KT * WC)
        o_g1 = place(6 * TP)
        o_g4 = place(CT * T)
        o_g2 = place(6 * T)
        o_g3 = place(CT * T)
        o_bc = place(4 * CT * T)
        o_cx = place(CT * TP)
        o_tmp = place(7168)

        hT = view(o_ht, KT, T)
        wbuf = [view(o_w + i * KT * WC, KT, WC) for i in range(2)]
        memT = view(o_bc, KT, ML)
        d_raw = view(o_g1, 6, TP)
        d_cv = view(o_g2, 6, T)
        d_z = view(o_g3, NT, GW)
        a_q = view(o_g1, CT, T)
        a_f = view(o_g1 + CT * T, CT, T)
        a_i = view(o_g1 + 2 * CT * T, NT, GW)
        a_g = view(o_g1 + 3 * CT * T, CT, T)
        assert 4 * CT * T <= 6 * TP + CT * T
        b_q = view(o_bc, CT, T)
        b_k = view(o_bc + CT * T, CT, T)
        b_v = view(o_bc + 2 * CT * T, NT, GW)
        c_g = view(o_bc + 3 * CT * T, CT, T)
        c_x = view(o_cx, CT, TP)
        yT = view(o_g2, KT, T)
        slot = lambda c: (c - 6) % KT
        memk = sb("memk", [CT, ML])
        memv = sb("memv", [MT_, GW])
        bf = sb("bf", [T])
        bf_tm = sb("bf_tm", [NT, NH])
        dba = sb("dba", [NT, 2 * NH])
        fidx, pidx, xor_f, tmp_mask, i_f, i_p, i_x = [view(o_bc + 4096 + i * P, P) for i in range(7)]
        iota_f, iota_p, xor_i = i_f.bitcast(i32), i_p.bitcast(i32), i_x.bitcast(i32)
        xin = [view(o_tmp + i * D, D) for i in range(2)]
        xs = [view(o_tmp + (2 + i) * D, D) for i in range(2)]
        junk = view(o_tmp + 4 * D, D)

        psum = [ctx.enter_context(nc.psum_tensor(f"bank{i}", [P, HALF], f32)) for i in range(8)]

        s = {n: ctx.enter_context(nc.semaphore(n)) for n in """
            h_E h_Ee n_sq n_ss n_rms n_gate n_out h_act x_bt x_bf x_l h_dve unit_e h_z x_row l_w l_xc x_ad
            l_ge l_gp h_os l_act l_dve l_pool h_kt h_kts x_cbp x_cb x_nb x_p x_tr x_pv x_pt x_o h_o h_dS
            h_Sv h_scr h_pm x_dg x_qk f_out h_qe t_wo t_x2 t_mo t_mq t_rw t_fg t_o_r xs_r t_xn t_m_e t_rl
            t_r_dve t_o_e t_q_r t_q_e t_m_mx t_m_tr t_m_p t_m_pv t_m_pt t_m_w t_m_ots t_r_ge t_m_sc t_m_dg
            t_z_ix t_r_rk ht_r t_sl f_c f_g0 f_g1 f_g2 f_g3 f_ot0 f_ot1 x_in0 x_in1 unit_r w_ld0 w_ld1
            consts_i consts_v g_MTs g_T1 g_MTh a_chain params_in prm_in rms_r d_cvd d_sil d_ssp d_sq d_l2
            d_el l_sp g_beta g_el g_Gv g_D g_qd g_eR g_mm g_ex g_MT g_XY g_T1s g_wk g_vn g_wks g_o g_os
            f_sq f_ss f_rs f_sil v_chain pcol_t tr_r g_Gp g_cols g_R g_KV g_kv g_KK g_M g_upd g_AT g_vns
            g_dS g_S f_y f_tr e_wl0 e_wl1 e_wl2 e_wl3 e_ic e_g0 e_g1 e_tr e_ht e_gu e_sg e_ac e_at e_ats
            e_dn e_y e_st0 e_st1
            """.split()}
        block = ctx.enter_context(nc.Block())


        w_mkv = a["w_mkv"][0]

        CHUNKS = []

        def chunk(src, c0, width, pieces):
            CHUNKS.append((src, c0, width, pieces))

        chunk(w_mkv, 0, GW, [("cm", 0, P, "mem", lambda ct, h: memk[:, ct, :])] )
        chunk(w_mkv, GW, GW, [("tm", 0, GW, "mem", lambda m: memv[:, m, :])])
        chunk(w_in, col["dq"], GW, [("cm", 0, P, "x", lambda ct, h: d_raw[:, 4 + ct, PAD + h * HALF:PAD + (h + 1) * HALF])])
        chunk(w_in, col["dk"], GW, [("cm", 0, P, "x", lambda ct, h: d_raw[:, 2 + ct, PAD + h * HALF:PAD + (h + 1) * HALF])])
        chunk(w_in, col["dv"], GW, [("cm", 0, P, "x", lambda ct, h: d_raw[:, ct, PAD + h * HALF:PAD + (h + 1) * HALF])])
        chunk(w_in, col["db"], GW + 2 * NH, [("tm2", 0, GW + 2 * NH, "x", lambda m: [
            (slice(0, 2 * NH), dba[:, m, :]), (slice(2 * NH, GW + 2 * NH), d_z[:, m, :])])])
        chunk(w_in, col["aq"], GW, [("cm", 0, P, "x", lambda ct, h: a_q[:, ct, h * HALF:(h + 1) * HALF])])
        chunk(w_in, col["af"], GW, [("cm", 0, P, "x", lambda ct, h: a_f[:, ct, h * HALF:(h + 1) * HALF])])
        chunk(w_in, col["ai"], GW, [("tm", 0, GW, "x", lambda m: a_i[:, m, :])])
        chunk(w_in, col["ag"], GW, [("cm", 0, P, "x", lambda ct, h: a_g[:, ct, h * HALF:(h + 1) * HALF])])
        chunk(w_in, col["bq"], GW, [("cm", 0, P, "x", lambda ct, h: b_q[:, ct, h * HALF:(h + 1) * HALF])])
        chunk(w_in, col["bk"], GW, [("cm", 0, P, "x", lambda ct, h: b_k[:, ct, h * HALF:(h + 1) * HALF])])
        chunk(w_in, col["bv"], GW + NH, [("tm2", 0, GW + NH, "x", lambda m: [
            (slice(0, GW), b_v[:, m, :]), (slice(GW, GW + NH), bf_tm[:, m, :])])])
        chunk(w_in, col["cx"], GW, [("cm", 0, P, "x", lambda ct, h: c_x[:, ct, PAD + h * HALF:PAD + (h + 1) * HALF])])
        chunk(w_in, col["cg"], GW, [("cm", 0, P, "x", lambda ct, h: c_g[:, ct, h * HALF:(h + 1) * HALF])])

        UNITS = []
        for ci, (src, c0, width, pieces) in enumerate(CHUNKS):
            wb = wbuf[ci % 2]
            for kind, b0, n, of, dst in pieces:
                act, rows = (memT, ML) if of == "mem" else (hT, T)
                if kind == "cm":
                    for ct in range(CT):
                        for h in range(max(1, rows // HALF)):
                            w = min(rows, HALF)
                            UNITS.append((ci, lambda k, wb=wb, b=b0 + ct * P, n=n: wb[:, k, b:b + n],
                                          lambda k, act=act, h=h, w=w: act[:, k, h * w:(h + 1) * w], n, w,
                                          [(slice(0, w), dst(ct, h))]))
                else:
                    for m in range(rows // P):
                        to = [(slice(0, n), dst(m))] if kind == "tm" else dst(m)
                        UNITS.append((ci, lambda k, act=act, m=m: act[:, k, m * P:(m + 1) * P],
                                      lambda k, wb=wb, b=b0, n=n: wb[:, k, b:b + n], P, n, to))
        UNITS_OF = [sum(u[0] == c for u in UNITS) for c in range(len(CHUNKS))]
        END_OF = [sum(UNITS_OF[:c + 1]) for c in range(len(CHUNKS))]
        PROJ_BANKS = [2, 3, 4]

        SLOTS = [("head", 1024), ("decay", 3072), ("rows", 2048)]
        for lv in range(1, NL):
            SLOTS += [(("half", lv), 512), (("joined", lv), 1024)]
        SLOTS += [("new", 1024), ("out", 1024), ("state", 1536)]
        PRE = [END_OF[5] + i for i in range(4)]
        products = [(u, k) for u in range(PRE[-1] + 1, len(UNITS)) for k in range(KT)]
        FILL, at_product = {}, 0
        for n in range(NT):
            for name, columns in SLOTS:
                FILL[n, name] = []
                while columns > 0 and at_product < len(products):
                    FILL[n, name].append(products[at_product])
                    columns -= UNITS[products[at_product][0]][4]
                    at_product += 1
        assert at_product == len(products)
        assert not any(FILL[NT - 1, name] for name, _c in SLOTS)

        def bc(ap, axis, shape):
            return ap.unsqueeze(axis).to_broadcast(shape)

        def chain(eng, sem):
            n = [0]

            def link(ins):
                n[0] += 1
                ins.then_inc(sem, 1)
                eng.wait_ge(sem, n[0])
            return link

        (o_D, o_gam, o_gamT, o_M, o_MT, o_X, o_Y, o_T1, o_AT, o_eR, o_kvb) = [o_tmp + i * 512 for i in range(11)]
        H4 = lambda off: view(off, NH, P)
        gD, gam, gamT, gM, gMT, gX, gY, gT1, gAT, eR, kvb = map(H4, (o_D, o_gam, o_gamT, o_M, o_MT, o_X, o_Y, o_T1,
                                                                     o_AT, o_eR, o_kvb))
        MTh = [H4(o_tmp + 11 * 512), H4(o_tmp + 12 * 512)]
        kdec = view(o_tmp + 13 * 512, NH, HD)
        wkT = view(o_tmp + 13 * 512 + 256, CT, P)
        assert 14 * 512 <= 7168
        qd = sb("qd", [CT, P])
        vnew = sb("vnew", [NH, HD])
        gS = sb("gS", [CT, HD])
        l2sq = [view(o_tmp + i * T, T) for i in range(2)]
        L2_BANKS = [(5, 6), (0, 1)]
        l2rs = [view(o_tmp + (2 + i) * T, T) for i in range(2)]
        NHT = NT * NH
        small = sb("small", [12, NT, NH])
        beta, gg, Gc, Gl, eG, kds, gle, beG, sm_t, sm_e, nexp = [small[:, i] for i in range(11)]
        glS = sb("glS", [NT, CT])
        d_o = d_cv[:, 4:6]
        fin_sq = view(o_tmp, CT, T)
        fin_ss = sb("fin_ss", [CT * NT * 2])

        h_lf = view(o_ht, CT, T)
        h_b = view(o_ht + CT * T, CT, T)
        h_qe = view(o_ht + 2 * CT * T, CT, T)
        h_kdT = view(o_ht + 3 * CT * T, NT, GW)
        seg = view(o_w, T)
        hE = [view(o_w + T + i * HALF, HALF) for i in range(2)]
        h_o = view(o_w + 2 * T, CT, T)
        hz = [view(o_tmp + i * NL * HALF, NL, HALF) for i in range(2)]
        h_pm = [view(o_g2 + 6 * T + i * T, NL + 1, P) for i in range(2)]
        hS = view(o_g2 + 4 * T, CT, NT, HD)
        hdec = sb("hdec", [CT, NT])
        NIT = CT * NHALF
        x_cb = view(o_ht, NH, T)
        x_sc = [view(o, T) for o in (o_ht + 4 * T, o_ht + 5 * T, o_tmp + 5 * T)]
        x_dg = [view(o_tmp + 6 * T + i * P, P) for i in range(2)]
        x_pT = [view(o_ht + (6 + i) * T, NT, P) for i in range(2)]
        x_row = bf
        x_one = view(o_w + 3 * T, T)
        x_l = view(o_w + 2 * T, T)
        x_o_ = view(o_tmp + 2 * T, CT, T)
        x_col = sb("x_col", [3, NH * NT])
        NW = NH * NT
        l_xc = view(o_w + 2 * T, CT, T)
        l_r = view(o_w, CT, T)
        l_i = view(o_cx, CT, T)
        l_a = view(o_tmp, CT, T)
        l_h = l_i
        l_col = sb("l_col", [12])

        def block_halves(t, h):
            return t.rearrange("p (n two h) -> p n two h", two=2, h=h)

        def act_hgrn_E(act, k):
            act.wait_ge(s["h_E"], k + 1)
            nc.scalar.activation(hE[k % 2], hE[k % 2], ACT.Exp).then_inc(s["h_Ee"], 1)

        n_sq = [view(o, CT, T) for o in (o_tmp, o_tmp, o_w)]
        n_bank = lambda f, i: psum[(0, 0, 4)[f] + i]

        def norm_act(act, link, f, o, ready, gate=None):
            ready(act)
            nc.scalar.activation(n_sq[f], o, ACT.Square).then_inc(s["n_sq"], 1)
            for i in range(CT * NHALF):
                act.wait_ge(s["n_ss"], CT * NHALF * (f + 1))
                link(nc.scalar.activation(n_sq[f][:, i // NHALF, (i % NHALF) * HALF:(i % NHALF + 1) * HALF],
                                          n_bank(f, i)[:, :], ACT.Ln, bias=epsc[:, 0:1], scale=1.0 / HD))
            for c in range(CT):
                nc.scalar.activation(n_sq[f][:, c], n_sq[f][:, c], ACT.Exp, scale=-0.5).then_inc(s["n_rms"], 1)
            if gate is not None:
                nc.scalar.activation(gate, gate, ACT.Silu).then_inc(s["n_gate"], 1)

        def norm_pe(pe, mm, f):
            pe.wait_ge(s["n_sq"], f + 1)
            for i in range(CT * NHALF):
                mm(n_bank(f, i)[:, :], head_ones[:, :], n_sq[f][:, i // NHALF, (i % NHALF) * HALF:(i % NHALF + 1) * HALF],
                   start=True, stop=True).then_inc(s["n_ss"], 1)

        def norm_dve(dve, v, link, f, o, c0, gate=None):
            for c in range(CT):
                dve.wait_ge(s["n_rms"], CT * f + c + 1)
                ins = v.scalar_tensor_tensor(yT[:, slot(c0 + c)], o[:, c], pcol[:, PC["gain"] + c0 + c:PC["gain"] + c0 + c + 1],
                                             n_sq[f][:, c], ALU.mult, ALU.mult)
                if gate is not None:
                    link(ins)
                    dve.wait_ge(s["n_gate"], 1)
                    ins = v.tensor_tensor(yT[:, slot(c0 + c)], yT[:, slot(c0 + c)], gate[:, c], ALU.mult)
                ins.then_inc(s["n_out"], 1)

        def hgrn_prepare_act(act, link, part):
            if part == 1:
                nc.scalar.activation(a_q, a_q, ACT.Silu).then_inc(s["h_act"], 1)
                link(nc.scalar.activation(h_lf, a_f, ACT.Abs))
            elif part == 2:
                link(nc.scalar.activation(h_lf, h_lf, ACT.Exp, scale=-1.0))
                nc.scalar.activation(h_lf, h_lf, ACT.Ln, bias=1.0).then_inc(s["h_act"], 1)
            elif part == 3:
                for hf in range(NHALF):
                    act.wait_ge(s["x_bt"], hf + 1)
                    nc.scalar.activation(bf[0:NH, hf * HALF:(hf + 1) * HALF], psum[2 + hf][0:NH, :],
                                         ACT.Copy).then_inc(s["x_bf"], 1)
                act.wait_ge(s["x_bf"], NHALF)
                link(nc.scalar.activation(x_l[0:NH, :], bf[0:NH, :], ACT.Abs, bias=fox_b[0:NH, 0:1]))
                link(nc.scalar.activation(x_l[0:NH, :], x_l[0:NH, :], ACT.Exp, scale=-1.0))
                nc.scalar.activation(x_l[0:NH, :], x_l[0:NH, :], ACT.Ln, bias=1.0).then_inc(s["x_l"], 1)
            elif part == 4:
                act.wait_ge(s["h_dve"], 1)
                nc.scalar.activation(a_f, a_f, ACT.Sigmoid, scale=-1.0).then_inc(s["h_act"], 1)
            elif part == 6:
                act.wait_ge(s["h_dve"], 2)
                nc.scalar.activation(h_lf, h_lf, ACT.Exp).then_inc(s["h_act"], 1)
                nc.scalar.activation(h_qe, h_b, ACT.Exp).then_inc(s["h_act"], 1)
                nc.scalar.activation(hdec[:, :, :], h_b[:, :, P - 1:T:P], ACT.Exp).then_inc(s["h_act"], 1)

        def hgrn_prepare_dve(dve, v, link, part):
            bt = h_b.rearrange("p c (n q) -> p (c n) q", q=P)
            lt = h_lf.rearrange("p c (n q) -> p (c n) q", q=P)
            if part == 1:
                dve.wait_ge(s["unit_e"], len(UNITS))
                link(v.memset(seg, 1.0))
                link(v.memset(seg[:, 0:T:P], 0.0))
            elif part == 3:
                dve.wait_ge(s["h_act"], 2)
                v.scalar_tensor_tensor(h_lf, a_f, 0.0, h_lf, ALU.min, ALU.subtract).then_inc(s["h_dve"], 1)
            elif part == 4:
                dve.wait_ge(s["h_dve"], 1)
                for c in range(CT):
                    link(v.tensor_tensor_scan(h_b[:, c], seg, h_lf[:, c], 0.0, ALU.mult, ALU.add))
            elif part == 5:
                v.tensor_tensor(lt, bt[:, :, P - 1:P].to_broadcast([P, CT * NT, P]), bt,
                                ALU.subtract).then_inc(s["h_dve"], 1)

        def hgrn_level(dve, v, link, k):
            it, h = k // NL, LEVELS[k % NL]
            c, hf = it // NHALF, it % NHALF
            if k >= 2:
                dve.wait_ge(s["h_z"], 2 * (k - 1))
            b = block_halves(h_b[:, c, hf * HALF:(hf + 1) * HALF], h)
            e = block_halves(hE[k % 2], h)
            mid = b[:, :, 0, h - 1:h].to_broadcast([P, HALF // (2 * h), h])
            link(v.tensor_tensor(e[:, :, 0], mid, b[:, :, 0], ALU.subtract))
            v.tensor_tensor(e[:, :, 1], b[:, :, 1], mid, ALU.subtract).then_inc(s["h_E"], 1)

        def fox_logits_dve(dve, v, link):
            dve.wait_ge(s["x_l"], 1)
            link(v.memset(x_one[0:NH, :], 1.0))
            link(v.tensor_scalar(bf[0:NH, :], bf[0:NH, :], fox_b[0:NH, 0:1], 0.0, ALU.add, ALU.min))
            link(v.tensor_tensor(x_l[0:NH, :], bf[0:NH, :], x_l[0:NH, :], ALU.subtract))
            link(v.tensor_tensor_scan(x_row[0:NH, :], x_one[0:NH, :], x_l[0:NH, :], 0.0, ALU.mult, ALU.add))
            v.tensor_scalar(x_row[0:NH, :], x_row[0:NH, :], -1.0 / QK_SCALE, None, ALU.mult).then_inc(s["x_row"], 1)

        def fox_logits_pe(pe):
            pe.wait_ge(s["unit_e"], len(UNITS))
            for n in range(NT):
                ins = nc.tensor.transpose(psum[2 + n // 4][0:NH, (n % 4) * P:(n % 4 + 1) * P], bf_tm[:, n, :],
                                          ident[:, :])
                if n % 4 == 3:
                    ins.then_inc(s["x_bt"], 1)

        L_GATES = [(8 * (g + 1) + c, g, c) for g in range(2) for c in range(CT)]

        def lru_pe(pe, mm, w):
            for w0, g, c in L_GATES:
                if w != w0:
                    continue
                if c == 0 and g == 0:
                    pe.wait_ge(s["l_w"], 16 * 4 * CT)
                    pe.wait_ge(s["l_xc"], CT)
                if c == 0:
                    pe.wait_ge(s["x_ad"], w)
                for hf in range(NHALF):
                    i = (g * CT + c) * NHALF + hf
                    if c > 0:
                        pe.wait_ge(s["l_ge"], i - 1)
                    mm(psum[1 + 6 * hf][:, :], lru_w[:, g * CT + c, :], l_xc[:, c, hf * HALF:(hf + 1) * HALF],
                       start=True, stop=True).then_inc(s["l_gp"], 1)

        def lru_act(act, link, w):
            for w0, g, c in L_GATES:
                for hf in range(NHALF if w == w0 else 0):
                    i = (g * CT + c) * NHALF + hf
                    act.wait_ge(s["l_gp"], i + 1)
                    if i == 0:
                        act.wait_ge(s["h_os"], NIT * 8)
                    nc.scalar.activation((l_r, l_i)[g][:, c, hf * HALF:(hf + 1) * HALF], psum[1 + 6 * hf][:, :],
                                         ACT.Sigmoid,
                                         bias=pcol[:, PC["ba"] + g * CT + c:PC["ba"] + g * CT + c + 1]).then_inc(s["l_ge"], 1)
            if w == 12:
                act.wait_ge(s["l_ge"], CT * NHALF)
                for c in range(CT):
                    link(nc.scalar.activation(l_a[:, c], l_r[:, c], ACT.Exp, scale=l_col[:, 2 + c:3 + c]))
            elif w == 13:
                for c in range(CT):
                    ins = nc.scalar.activation(l_r[:, c], l_r[:, c], ACT.Tanh, scale=l_col[:, 4 + c:5 + c])
                    ins.then_inc(s["l_act"], 1) if c == CT - 1 else link(ins)
                nc.scalar.activation(c_g, c_g, ACT.Gelu_apprx_tanh).then_inc(s["l_act"], 1)
            elif w == 24:
                act.wait_ge(s["l_dve"], 1)
                nc.scalar.activation(l_r, l_r, ACT.Sqrt).then_inc(s["l_act"], 1)

        def lru_dve(dve, v, link, w):
            if w < 2 * CT:
                c = w // 2
                wl = lambda t: pcol[:, PC["lconv"] + CT * t + c:PC["lconv"] + CT * t + c + 1]
                for t in range(TAPS // 2 * (w % 2), TAPS // 2 * (w % 2 + 1)):
                    if t == 0:
                        ins = v.tensor_scalar(l_xc[:, c], c_x[:, c, 0:T], wl(0), pcol[:, PC["lb"] + c:PC["lb"] + c + 1],
                                              ALU.mult, ALU.add)
                    else:
                        ins = v.scalar_tensor_tensor(l_xc[:, c], c_x[:, c, t:t + T], wl(t), l_xc[:, c],
                                                     ALU.mult, ALU.add)
                    ins.then_inc(s["l_xc"], 1) if t == TAPS - 1 else link(ins)
            elif w == 22:
                dve.wait_ge(s["l_pool"], 2)
                dve.wait_ge(s["l_act"], 1)
                link(v.scalar_tensor_tensor(l_r, l_i, 1.0, l_r, ALU.add, ALU.mult))
                v.tensor_scalar(l_r, l_r, 1e-18, None, ALU.max).then_inc(s["l_dve"], 1)
            elif w == 28:
                dve.wait_ge(s["l_pool"], 3)
                for c in range(CT):
                    ins = v.tensor_tensor_scan(l_h[:, c], l_a[:, c], l_xc[:, c], 0.0, ALU.mult, ALU.add)
                    ins.then_inc(s["l_dve"], 1) if c == CT - 1 else link(ins)

        def lru_pool(pool):
            pool.wait_ge(s["l_xc"], CT)
            pool.wait_ge(s["l_ge"], 2 * CT * NHALF)
            nc.gpsimd.tensor_tensor(l_xc, l_xc, l_i, ALU.mult).then_inc(s["l_pool"], 1)
            pool.wait_ge(s["l_pool"], 1)
            pool.wait_ge(s["l_act"], 1)
            nc.gpsimd.tensor_tensor(l_i, l_a, l_a, ALU.mult).then_inc(s["l_pool"], 1)
            pool.wait_ge(s["l_act"], 3)
            nc.gpsimd.tensor_tensor(l_xc, l_xc, l_r, ALU.mult).then_inc(s["l_pool"], 1)
            pool.wait_ge(s["l_dve"], 2)
            nc.gpsimd.tensor_tensor(l_h, l_h, c_g, ALU.mult).then_inc(s["l_pool"], 1)

        def act_tail(act, link, stats):
            for i in range(2 * CT):
                act.wait_ge(s["h_kt"], i + 1)
                c, j = i // 2, i % 2
                nc.scalar.activation(h_kdT[:, 4 * j:4 * j + 4, c * P:(c + 1) * P],
                                     psum[2 + i % 2][:, :].rearrange("p (n q) -> p n q", n=4),
                                     ACT.Copy).then_inc(s["h_kts"], 1)
            for k in range(NL):
                act_hgrn_E(act, k)
            for it in range(NIT):
                for j in range(8):
                    q = it * 8 + j
                    if it < NIT - 1 and j < NL:
                        act_hgrn_E(act, (it + 1) * NL + j)
                    if q >= 1:
                        act_hgrn_o(act, q - 1)
            act_hgrn_o(act, NIT * 8 - 1)
            norm_act(act, link, 0, h_o, lambda e: e.wait_ge(s["h_os"], NIT * 8), a_g)

            for i in range(NH * NHALF):
                act.wait_ge(s["x_cbp"], i + 1)
                h, hf = i // NHALF, i % NHALF
                nc.scalar.activation(x_cb[:, h, hf * HALF:(hf + 1) * HALF], psum[4 + i % 2][:, :],
                                     ACT.Copy).then_inc(s["x_cb"], 1)
            tr = [0]

            def probs(w):
                n = (w % NT + 1) * P
                act.wait_ge(s["x_nb"], w + 1)
                nc.scalar.activation(x_sc[w % 3][:, 0:n], x_sc[w % 3][:, 0:n], ACT.Exp, bias=x_col[:, 0, w:w + 1],
                                     scale=QK_SCALE, accum_out=x_col[:, 1, w:w + 1]).then_inc(s["x_p"], 1)

            def probsT(w):
                blocks = w % NT + 1
                for b in range(0, blocks, 4):
                    m = min(4, blocks - b)
                    act.wait_ge(s["x_tr"], tr[0] + 1)
                    if w >= 2:
                        act.wait_ge(s["x_pv"], w - 1)
                    nc.scalar.activation(x_pT[w % 2][:, b:b + m, :],
                                         psum[4 + tr[0] % 2][:, 0:m * P].rearrange("p (b q) -> p b q", q=P),
                                         ACT.Copy).then_inc(s["x_pt"], 1)
                    tr[0] += 1

            for w in range(NW + 1):
                if w < NW:
                    probs(w)
                if w >= 1:
                    probsT(w - 1)
                lru_act(act, link, w)

            def fox_done(e):
                e.wait_ge(s["x_o"], NW)
                e.wait_ge(s["l_dve"], 2)
            norm_act(act, link, 1, x_o_, fox_done)

            norm_act(act, link, 2, l_h, lambda e: e.wait_ge(s["l_pool"], 4))
            act_tail2(act, link, stats)

        def act_hgrn_o(act, q):
            act.wait_ge(s["h_o"], q + 1)
            it, j = q // 8, q % 8
            c, n, par = it // NHALF, (it % NHALF) * 4 + j // 2, j % 2
            r = slice(HD * par, HD * par + HD)
            nc.scalar.activation(h_o[r, c, n * P:(n + 1) * P], psum[6 + par][r, 0:P], ACT.Copy).then_inc(s["h_os"], 1)

        def dve_tail(dve, v, link, scale_rows, gains, inverse_rms):

            for k in range(2, NL):
                hgrn_level(dve, v, link, k)
            dve.wait_ge(s["h_act"], 6)
            link(v.memset(hS[:, :, 0], 0.0))
            for c in range(CT):
                dve.wait_ge(s["h_dS"], c + 1)
                for n in range(1, NT):
                    link(v.scalar_tensor_tensor(hS[:, c, n], hS[:, c, n - 1], hdec[:, c, n - 1:n],
                                                psum[4 + c][:, (n - 1) * HD:n * HD], ALU.mult, ALU.add))
            v.tensor_copy(l_col[:, 11:12], epsc[:, 0:1]).then_inc(s["h_Sv"], 1)
            for it in range(NIT):
                for j in range(8):
                    q = it * 8 + j
                    dve.wait_ge(s["h_scr"], q + 1)
                    if q >= 2:
                        dve.wait_ge(s["h_o"], q - 1)
                    for b in range(2):
                        v.tensor_tensor(h_pm[q % 2][:, 4 * b:4 * b + 4],
                                        psum[2 * (j % 2) + b][:, :].rearrange("p (l t) -> p l t", l=4),
                                        levT[:, 4 * b:4 * b + 4], ALU.mult).then_inc(s["h_pm"], 1)
                    if it < NIT - 1 and j < NL:
                        hgrn_level(dve, v, link, (it + 1) * NL + j)
            norm_dve(dve, v, link, 0, h_o, 0, a_g)

            dve.wait_ge(s["n_out"], CT)
            dve.wait_ge(s["x_cb"], NH * NHALF)

            def fox_out(w):
                h, i = w // NT, w % NT
                dve.wait_ge(s["x_pv"], w + 1)
                r = slice(HD * (h % 2), HD * (h % 2) + HD)
                v.tensor_copy(x_o_[r, h // 2, i * P:(i + 1) * P], psum[2 + w % 2][r, 0:P]).then_inc(s["x_o"], 1)

            def fox_diagonal(w):
                dve.wait_ge(s["x_p"], w + 1)
                if w >= 2:
                    dve.wait_ge(s["x_tr"], fox_tr(w - 2))
                link(v.reciprocal(x_col[:, 2, w:w + 1], x_col[:, 1, w:w + 1]))
                v.tensor_scalar(x_dg[w % 2], ident[:, :], x_col[:, 2, w:w + 1], None, ALU.mult).then_inc(s["x_dg"], 1)

            for w in range(NW):
                h, n = w // NT, (w % NT + 1) * P
                dve.wait_ge(s["x_qk"], w + 1)
                if w >= 3:
                    dve.wait_ge(s["x_tr"], fox_tr(w - 3))
                for b in range(0, n, HALF):
                    m = min(HALF, n - b)
                    ins = v.tensor_tensor(x_sc[w % 3][:, b:b + m], psum[6 * (w % 2) + b // HALF][:, 0:m],
                                          x_cb[:, h, b:b + m], ALU.add)
                    link(ins) if b + m < n else ins.then_inc(s["x_ad"], 1)
                dve.wait_ge(s["x_ad"], w + 1)
                link(v.tensor_reduce(x_col[:, 0, w:w + 1], x_sc[w % 3][:, 0:n], AX.X, ALU.max))
                v.tensor_scalar(x_col[:, 0, w:w + 1], x_col[:, 0, w:w + 1], -QK_SCALE, None,
                                ALU.mult).then_inc(s["x_nb"], 1)
                if w >= 1:
                    fox_diagonal(w - 1)
                if w >= 2:
                    fox_out(w - 2)
                lru_dve(dve, v, link, w)
            fox_diagonal(NW - 1)
            fox_out(NW - 2)
            fox_out(NW - 1)
            norm_dve(dve, v, link, 1, x_o_, 2)

            norm_dve(dve, v, link, 2, l_h, 4)
            dve_tail2(dve, v, link, scale_rows, gains, inverse_rms)

        def fox_tr(w):
            return sum((i % NT + 4) // 4 for i in range(w + 1))

        def hgrn_states_pe(pe, mm):
            rows = lambda h: slice(HD * (h % 2), HD * (h % 2) + HD)
            hd = lambda h: slice(h * HD, (h + 1) * HD)
            pe.wait_ge(s["x_bf"], NHALF)
            pe.wait_ge(s["h_dve"], 3)
            for i in range(2 * CT):
                if i >= 2:
                    pe.wait_ge(s["h_kts"], i - 1)
                for t in range(4):
                    n = (i % 2) * 4 + t
                    ins = nc.tensor.transpose(psum[2 + i % 2][:, t * P:(t + 1) * P],
                                              h_lf[:, i // 2, n * P:(n + 1) * P], ident[:, :])
                ins.then_inc(s["h_kt"], 1)
            pe.wait_ge(s["h_kts"], 2 * CT)
            for c in range(CT):
                for n in range(NT):
                    for par in range(2):
                        h = 2 * c + par
                        ins = mm(psum[4 + c][rows(h), hd(n)], h_kdT[:, n, hd(h)], a_i[:, n, hd(h)],
                                 start=True, stop=True)
                ins.then_inc(s["h_dS"], 1)

        def pe_tail(pe, mm, transposes):
            rows = lambda h: slice(HD * (h % 2), HD * (h % 2) + HD)
            hd = lambda h: slice(h * HD, (h + 1) * HD)
            def hgrn_scores(q):
                it, j = q // 8, q % 8
                c, n4, par = it // NHALF, j // 2, j % 2
                pe.wait_ge(s["h_z"], 2 * NL * (it + 1))
                if q >= 2:
                    pe.wait_ge(s["h_pm"], 2 * (q - 1))
                part = slice(n4 * P, (n4 + 1) * P)
                tok = slice((it % NHALF) * HALF + n4 * P, (it % NHALF) * HALF + (n4 + 1) * P)
                for lv in range(NL + 1):
                    bank = psum[2 * par + lv // 4][:, (lv % 4) * P:(lv % 4 + 1) * P]
                    if lv < NL:
                        ins = mm(bank, hz[it % 2][rows(par), lv, part], hz[it % 2][rows(par), lv, part],
                                 start=True, stop=True)
                    else:
                        ins = mm(bank, a_f[rows(par), c, tok], a_q[rows(par), c, tok], start=True, stop=True)
                ins.then_inc(s["h_scr"], 1)

            def hgrn_out(q):
                it, j = q // 8, q % 8
                c, n, par = it // NHALF, (it % NHALF) * 4 + j // 2, j % 2
                pe.wait_ge(s["h_pm"], 2 * q + 2)
                if q >= 2:
                    pe.wait_ge(s["h_os"], q - 1)
                bank = psum[6 + par][rows(par), 0:P]
                for lv in range(NL + 1):
                    mm(bank, a_i[:, n, hd(2 * c + par)], h_pm[q % 2][:, lv], start=(lv == 0), stop=False)
                mm(bank, hS[rows(par), c, n], h_qe[rows(par), c, n * P:(n + 1) * P], start=False,
                   stop=True).then_inc(s["h_o"], 1)

            pe.wait_ge(s["f_out"], 4)
            pe.wait_ge(s["h_act"], 1)
            pe.wait_ge(s["h_Sv"], 1)
            pe.wait_ge(s["h_qe"], 1)
            hgrn_scores(0)
            for q in range(NIT * 8):
                if q + 1 < NIT * 8:
                    hgrn_scores(q + 1)
                hgrn_out(q)
            norm_pe(pe, mm, 0)

            pe.wait_ge(s["x_row"], 1)
            for i in range(NH * NHALF):
                if i >= 2:
                    pe.wait_ge(s["x_cb"], i - 1)
                h, hf = i // NHALF, i % NHALF
                mm(psum[4 + i % 2][:, :], ident[0:NH, h:h + 1].to_broadcast([NH, P]),
                   x_row[0:NH, hf * HALF:(hf + 1) * HALF], start=True, stop=True).then_inc(s["x_cbp"], 1)
            pe.wait_ge(s["x_cb"], NH * NHALF)
            pe.wait_ge(s["n_rms"], 1)
            tr = [0]

            def fox_scores(w):
                h, i = w // NT, w % NT
                if w >= 2:
                    pe.wait_ge(s["x_ad"], w - 1)
                q = b_q[rows(h), h // 2, i * P:(i + 1) * P]
                for b in range(0, i * P, HALF):
                    m = min(HALF, i * P - b)
                    mm(psum[6 * (w % 2) + b // HALF][:, 0:m], q, b_k[rows(h), h // 2, b:b + m], start=True, stop=True)
                o = (i * P) % HALF
                bank = psum[6 * (w % 2) + i * P // HALF][:, o:o + P]
                mm(bank, q, b_k[rows(h), h // 2, i * P:(i + 1) * P], start=True, stop=False)
                mm(bank, ident[:, :], negmask[:, :], start=False, stop=True).then_inc(s["x_qk"], 1)

            def fox_transposes(w):
                blocks = w % NT + 1
                pe.wait_ge(s["x_dg"], w + 1)
                for b in range(0, blocks, 4):
                    if tr[0] >= 2:
                        pe.wait_ge(s["x_pt"], tr[0] - 1)
                    for t in range(b, min(b + 4, blocks)):
                        ins = mm(psum[4 + tr[0] % 2][:, (t - b) * P:(t - b + 1) * P], x_sc[w % 3][:, t * P:(t + 1) * P],
                                 x_dg[w % 2][:, :], start=True, stop=True)
                    ins.then_inc(s["x_tr"], 1)
                    tr[0] += 1

            def fox_values(w):
                h, i = w // NT, w % NT
                pe.wait_ge(s["x_pt"], fox_tr(w))
                if w >= 2:
                    pe.wait_ge(s["x_o"], w - 1)
                for t in range(i + 1):
                    ins = mm(psum[2 + w % 2][rows(h), 0:P], b_v[:, t, hd(h)], x_pT[w % 2][:, t], start=(t == 0),
                             stop=(t == i))
                ins.then_inc(s["x_pv"], 1)

            fox_scores(0)
            fox_scores(1)
            for w in range(NW + 1):
                if w in (10, 18):
                    pe.wait_ge(s["l_ge"], CT * NHALF * (w // 8))
                if w + 2 < NW:
                    fox_scores(w + 2)
                lru_pe(pe, mm, w)
                if w >= 1:
                    fox_values(w - 1)
                if w < NW:
                    fox_transposes(w)
            norm_pe(pe, mm, 1)

            pe.wait_ge(s["t_wo"], 16)
            pe.wait_ge(s["n_out"], 2 * CT)
            for u in range(2):
                for k in W_ORDER[:KT - CT]:
                    ins = mm(psum[2 + u][:, :], yT[:, slot(k), 0:P], wo[:, k, u * HALF:(u + 1) * HALF],
                             start=(k == W_ORDER[0]), stop=False)
            norm_pe(pe, mm, 2)
            pe_tail2(pe, mm, transposes)

        def pool_tail(pool):
            pool.wait_ge(s["h_act"], 1)
            pool.wait_ge(s["h_act"], 5)
            nc.gpsimd.tensor_tensor(h_qe, h_qe, a_q, ALU.mult).then_inc(s["h_qe"], 1)
            pool.wait_ge(s["h_act"], 3)
            for k in range(NIT * NL):
                it, lv = k // NL, k % NL
                c, hf = it // NHALF, it % NHALF
                pool.wait_ge(s["h_Ee"], k + 1)
                if it >= 2:
                    pool.wait_ge(s["h_scr"], 8 * (it - 1))
                part = slice(hf * HALF, (hf + 1) * HALF)
                e, z = block_halves(hE[k % 2], LEVELS[lv]), block_halves(hz[it % 2][:, lv], LEVELS[lv])
                kk, qq = block_halves(a_f[:, c, part], LEVELS[lv]), block_halves(a_q[:, c, part], LEVELS[lv])
                nc.gpsimd.tensor_tensor(z[:, :, 0], e[:, :, 0], kk[:, :, 0], ALU.mult).then_inc(s["h_z"], 1)
                nc.gpsimd.tensor_tensor(z[:, :, 1], e[:, :, 1], qq[:, :, 1], ALU.mult).then_inc(s["h_z"], 1)
            lru_pool(pool)
            pool_tail2(pool)
        OE = NT * D
        wo = view(o_g1, KT, D)
        W_ORDER = [k for k in range(KT) if k not in (4, 5)] + [4, 5]
        x2 = view(o_bc, NT, D)
        mq = view(o_w, KT, GW)
        mo = view(o_w + KT * GW, CT, D)
        NR = NG + NE
        wr = view(o_cx, KT, NR)
        br = view(o_cx + KT * NR, NR)
        fin_g = view(o_cx + (KT + 1) * NR, D)
        mqT = view(o_tmp, CT, T)
        m_p = [view(o_g1 + i * T, NH, ML) for i in range(2)]
        m_pT = [view(o_g1 + (2 + i) * T, NH * MT_, P) for i in range(2)]
        m_dg = view(o_g1 + 4 * T, NH, P)
        M_SC = [(5, 6), (2, 7)]
        m_oT = [view(o_g1 + 4 * T + (2 + i) * GW, CT, P) for i in range(2)]
        m_col = sb("m_col", [3, NT, NH])
        G2, G3 = MT_ + NT, MT_ + 2 * NT
        r0 = o_g1 + 6144 + 4
        rp = [r0]

        def rt(*shape):
            n = 1
            for d in shape:
                n *= d
            rp[0] += n
            assert rp[0] <= o_g2, rp[0]
            return view(rp[0] - n, *shape)
        TK = 2
        lg = rt(NT, NR)
        gpad, gmx, sel, smx = rt(NT, 8), rt(NT, 8), rt(NT, 8), rt(NT, 8)
        gix, six = rt(NT, 8).bitcast(u32), rt(NT, 8).bitcast(u32)
        gself, goh, pg = rt(NT), rt(NT, NG), rt(NT)
        gex = rt(NT, NG)
        eid = rt(TK, NT)
        wts = rt(TK, NT)
        rank = rt(TK, NT)
        slots = rt(TK, NT).bitcast(i32)
        tokid = rt(NT).bitcast(i32)
        io_i = rt(NE).bitcast(i32)
        io_f = rt(NE)
        totf = rt(NE)
        toti = rt(1).bitcast(i32)
        r1 = [o_g2 + 6144]
        oh = [view(r1[0] + i * NT * NE, NT, NE) for i in range(TK)]
        asum, apre, rtmp = [view(r1[0] + (TK + i) * NT * NE, NT, NE) for i in range(3)]
        gsum = view(r1[0] + 5 * NT * NE, NT * NG, EPG)
        idx_all = view(r1[0] + 6 * NT * NE, NE * (T // P)).bitcast(i32)
        EW = KT * 2 * FE + (FE // P) * D
        NB = 4
        wb_at = [o_g2, 0, EW, 2 * EW + 128]
        assert wb_at[3] >= o_g1 and wb_at[3] + EW <= r0 and EW == 6144
        w_gu = [view(o, KT, 2 * FE) for o in wb_at]
        w_dn = [view(o + KT * 2 * FE, FE // P, D) for o in wb_at]
        hg = [view(o_tmp + i * D, D) for i in range(2)]
        hgT = [view(o_tmp + (2 + i) * D, KT, P) for i in range(2)]
        ysb = [view(o_tmp + (4 + i) * D, D) for i in range(2)]
        sg = view(o_cx + (KT + 1) * NR + D, 2, FE)
        actv = view(o_tmp + 6 * D + 2 * FE, 2, FE)
        actT = [view(o_tmp + 6 * D + i * FE, FE // P, P) for i in range(2)]
        idxc = sb("idxc", [2], i32)
        PASSES = T // P
        yg = [view(i * D, D) for i in range(8)]
        slot_tok = nc.dram_tensor("slot_tok", (NE * T, 1), i32, kind="Internal").ap()
        xn_d = nc.dram_tensor("xn_d", (T, D), f32, kind="Internal").ap()
        y_d = nc.dram_tensor("y_d", (NE * T, D), f32, kind="Internal").ap()
        y_rows = y_d.rearrange("(p r e) d -> p e r d", r=P, e=NE)
        moe = ({n: s["e_" + n] for n in
                                 "wl0 wl1 wl2 wl3 ic g0 g1 tr ht gu sg ac at ats dn y st0 st1".split()})

        OVER = P

        def after(eng, sem, start, n):
            if isinstance(n, int) and n <= 0:
                return
            eng.wait_ge(sem, start + n)

        def each_expert(eng, step):
            for e in range(NB):
                step(e, e)
            with eng.Fori(1, NE // NB - 1) as i:
                for j in range(NB):
                    step(i * NB + j, j)
            for e in range(NE - NB, NE):
                step(e, e % NB)

        def gathers(e, b):
            return (e + 2 - b) * 8

        def weights(e, j):
            return (e + NB - j) * 8

        gu_d, dn_d = [t[0].rearrange("e (k p) n -> e p k n", p=P) for t in (a["w_e_gu"], a["w_e_dn"])]

        def load_expert(sp, q, e, j):
            sem = (q["wl0"], q["wl1"], q["wl2"], q["wl3"])[j]
            sp.dma_start(w_gu[j], gu_d[e]).then_inc(sem, 16)
            sp.dma_start(w_dn[j], dn_d[e]).then_inc(sem, 16)

        def sp_experts(sp, q, base, p):
            def step(e, j, more=True):
                sp.wait_ge(q["y"], 2 * base + 2 * (e + 1))
                sp.dma_start(y_rows[p, e], ysb[j % 2]).then_inc((q["st0"], q["st1"])[j % 2], 16)
                if more:
                    load_expert(sp, q, e + NB, j)
            for e in range(NB):
                step(e, e)
            with sp.Fori(1, NE // NB - 1) as i:
                for j in range(NB):
                    step(i * NB + j, j)
            for e in range(NE - NB, NE):
                step(e, e % NB, more=False)

        def pass_end(eng, q, base):
            eng.wait_ge(q["st0"], 8 * base + 8 * NE)
            eng.wait_ge(q["st1"], 8 * base + 8 * NE)

        def sp_tail(sp):
            sp.wait_ge(s["n_out"], CT)
            sp.dma_start(wo, a["w_out"][0].rearrange("(k p) n -> p k n", p=P)).then_inc(s["t_wo"], 16)
            sp.wait_ge(s["n_out"], 2 * CT)
            sp.wait_ge(s["l_pool"], 4)
            sp.dma_start(x2, x.rearrange("(m p) n -> p m n", p=P)).then_inc(s["t_x2"], 16)
            sp.dma_start(mo, a["w_mo"][0].rearrange("(k p) n -> p k n", p=P)).then_inc(s["t_mo"], 16)
            sp.wait_ge(s["n_out"], 3 * CT)
            sp.dma_start(mq, a["w_mq"][0].rearrange("(k p) n -> p k n", p=P)).then_inc(s["t_mq"], 16)
            sp.dma_start(wr[:, :, 0:NG], a["w_rg"][0].rearrange("(k p) n -> p k n", p=P)).then_inc(s["t_rw"], 16)
            sp.dma_start(wr[:, :, NG:NR], a["w_re"][0].rearrange("(k p) n -> p k n", p=P)).then_inc(s["t_rw"], 16)
            sp.dma_start(br[:, 0:NG], a["b_rg"][0:1, :].to_broadcast([P, NG])).then_inc(s["t_rw"], 16)
            sp.dma_start(br[:, NG:NR], a["b_re"][0:1, :].to_broadcast([P, NE])).then_inc(s["t_rw"], 16)
            sp.dma_start(fin_g, a["norm_final"].unsqueeze(0).to_broadcast([P, D])).then_inc(s["t_fg"], 16)
            first = lambda e: load_expert(sp, moe, e, e)
            sp.wait_ge(s["t_o_r"], 2 * NT)
            first(0)
            for m in range(NT):
                sp.wait_ge(s["xs_r"], G3 + m + 1)
                sp.dma_start(xn_d[m * P:(m + 1) * P, :], xs[m % 2]).then_inc(s["t_xn"], 16)
                sp.wait_ge(s["t_xn"], 16 * (m + 1))
                if m == 0:
                    sp.wait_ge(s["t_m_e"], 2 * NT)
                    first(3)
            sp.wait_ge(s["t_rl"], 1)
            first(1)
            first(2)
            sp_experts(sp, moe, 0, 0)
            with overflow(sp):
                with sp.Fori(0, PASSES - 1) as p:
                    pass_end(sp, moe, p * NE)
                    for e in range(NB):
                        load_expert(sp, moe, e, e)
                    sp_experts(sp, moe, (p + 1) * NE, p + 1)
                sp.wait_ge(moe["st0"], 8 * NE * PASSES)
                sp.wait_ge(moe["st1"], 8 * NE * PASSES)
            sp_tail3(sp)

        def overflow(eng):
            eng.wait_ge(s["t_r_dve"], 4)
            most = eng.value_load(toti[0:1, 0:1], min_val=0, max_val=T)
            return eng.If(most > OVER)

        def act_experts(act, q, base):
            def step(e, j):
                b = j % 2
                act.wait_ge(q["gu"], base + (e + 1))
                after(act, q["ac"], base, e - 1)
                nc.scalar.activation(sg[:, b], psum[2 + 4 * b][:, 0:FE], ACT.Silu).then_inc(q["sg"], 1)
                act.wait_ge(q["at"], base + (e + 1))
                nc.scalar.activation(actT[b], psum[3][:, 0:FE].rearrange("p (k t) -> p k t", t=P),
                                     ACT.Copy).then_inc(q["ats"], 1)
                act.wait_ge(q["dn"], base + (e + 1))
                after(act, (q["st0"], q["st1"])[b], 8 * base, gathers(e, b) - 16)
                nc.scalar.activation(ysb[b][:, 0:HALF], psum[4][:, :], ACT.Copy).then_inc(q["y"], 1)
            each_expert(act, step)

        def act_tail2(act, link, stats):
            for m in range(NT):
                stats(G2 + m, x2[:, m], lambda e, m=m: e.wait_ge(s["t_o_e"], 2 * (m + 1)))
            for u in range(CT * NHALF):
                act.wait_ge(s["t_q_r"], u + 1)
                nc.scalar.activation(mqT[:, u % CT, (u // CT) * HALF:(u // CT + 1) * HALF], psum[2 + u % 3][:, :],
                                     ACT.Copy).then_inc(s["t_q_e"], 1)
            act.wait_ge(s["t_o_r"], 2 * NT)

            def probs(m):
                act.wait_ge(s["t_m_mx"], m + 1)
                if m >= 2:
                    act.wait_ge(s["t_m_tr"], 2 * (m - 1))
                for h in range(NH):
                    k = (h % 2) * 2 + h // 2
                    ins = nc.scalar.activation(m_p[m % 2][:, h], psum[M_SC[m % 2][h % 2]][:, (h // 2) * ML:(h // 2 + 1) * ML],
                                               ACT.Exp, bias=m_col[:, 0, m, k:k + 1], scale=QK_SCALE,
                                               accum_out=m_col[:, 1, m, h:h + 1])
                    ins.then_inc(s["t_m_p"], 1) if h == NH - 1 else link(ins)

            def probsT(m):
                if m >= 2:
                    act.wait_ge(s["t_m_pv"], m - 1)
                for b in range(2):
                    act.wait_ge(s["t_m_tr"], 2 * m + b + 1)
                    nc.scalar.activation(m_pT[m % 2][:, 4 * b:4 * b + 4],
                                         psum[b][:, :].rearrange("p (a b) -> p a b", b=P), ACT.Copy).then_inc(s["t_m_pt"], 1)

            def outT(m):
                act.wait_ge(s["t_m_pv"], m + 1)
                if m >= 2:
                    act.wait_ge(s["t_m_w"], 2 * (m - 1))
                nc.scalar.activation(m_oT[m % 2], psum[4][:, 0:GW].rearrange("p (c t) -> p c t", c=CT),
                                     ACT.Copy).then_inc(s["t_m_ots"], 1)

            for it in range(NT + 1):
                if it >= 1:
                    probsT(it - 1)
                if it < NT:
                    probs(it)
                if it >= 1:
                    outT(it - 1)
            for m in range(NT):
                stats(G3 + m, x2[:, m], lambda e, m=m: e.wait_ge(s["t_m_e"], 2 * (m + 1)))
            act.wait_ge(s["t_r_dve"], 1)
            nc.scalar.activation(gex, gex, ACT.Exp).then_inc(s["t_r_ge"], 1)
            act.wait_ge(s["t_r_dve"], 2)
            nc.scalar.activation(wts[:, 1], wts[:, 1], ACT.Exp).then_inc(s["t_r_ge"], 1)
            act.wait_ge(s["t_r_dve"], 5)
            act_experts(act, moe, 0)
            with overflow(act):
                pass_end(act, moe, 0)
                with act.Fori(0, PASSES - 1) as p:
                    act_experts(act, moe, (p + 1) * NE)
                    pass_end(act, moe, (p + 1) * NE)
            act_tail3(act, link, stats)

        def dve_experts(dve, v, q, base):
            def tokens(e, b):
                for k in range(2):
                    dve.wait_ge(q["tr"], 2 * base + (2 * e + k + 1))
                    v.tensor_tensor(hgT[b][:, 4 * k:4 * k + 4], psum[k][:, :].rearrange("p (a t) -> p a t", a=4),
                                    bc(pcol[:, PC["ffn"] + 4 * k:PC["ffn"] + 4 * k + 4], 2, [P, 4, P]),
                                    ALU.mult).then_inc(q["ht"], 1)

            def step(e, j):
                b = j % 2
                dve.wait_ge(q["sg"], base + (e + 1))
                after(dve, q["at"], base, e - 1)
                v.tensor_tensor(actv[:, b], sg[:, b], psum[2 + 4 * b][:, FE:2 * FE], ALU.mult).then_inc(q["ac"], 1)
                if not (isinstance(e, int) and e >= NE - 2):
                    tokens(e + 2, b)
                dve.wait_ge(q["dn"], base + (e + 1))
                after(dve, (q["st0"], q["st1"])[b], 8 * base, gathers(e, b) - 16)
                v.tensor_copy(ysb[b][:, HALF:D], psum[5][:, :]).then_inc(q["y"], 1)
            tokens(0, 0)
            tokens(1, 1)
            each_expert(dve, step)

        def dve_tail2(dve, v, link, scale_rows, gains, inverse_rms):
            dve.wait_ge(s["t_x2"], 16)

            def add(m, hf, bank):
                part = x2[:, m, hf * HALF:(hf + 1) * HALF]
                return v.tensor_tensor(part, part, bank[:, :], ALU.add)

            for m in range(NT + 1):
                if m < NT:
                    for hf in range(2):
                        u = 2 * m + hf
                        dve.wait_ge(s["t_o_r"], u + 1)
                        add(m, hf, psum[2 + u % 3]).then_inc(s["t_o_e"], 1)
                if m >= 1:
                    g = G2 + m - 1
                    scale_rows(g, x2[:, m - 1])
                    gains(g, PC["mem"], hT, slice((m - 1) * P, m * P))

            def row_max(m):
                dve.wait_ge(s["t_m_sc"], m + 1)
                for par in range(2):
                    link(v.tensor_reduce(m_col[:, 0, m, 2 * par:2 * par + 2],
                                         psum[M_SC[m % 2][par]][:, :].rearrange("p (h k) -> p h k", h=2), AX.X, ALU.max))
                v.tensor_scalar(m_col[:, 0, m], m_col[:, 0, m], -QK_SCALE, None, ALU.mult).then_inc(s["t_m_mx"], 1)

            def add_out(m, hf):
                dve.wait_ge(s["t_m_w"], 2 * m + hf + 1)
                add(m, hf, psum[3]).then_inc(s["t_m_e"], 1)

            row_max(0)
            for it in range(NT + 2):
                if it >= 2:
                    add_out(it - 2, 0)
                if it + 1 < NT:
                    row_max(it + 1)
                if it >= 2:
                    add_out(it - 2, 1)
                if it < NT:
                    dve.wait_ge(s["t_m_p"], it + 1)
                    if it >= 1:
                        dve.wait_ge(s["t_m_tr"], 2 * it)
                    link(v.reciprocal(m_col[:, 2, it], m_col[:, 1, it]))
                    v.tensor_tensor(m_dg, bc(ident[:, :], 1, [P, NH, P]), bc(m_col[:, 2, it], 2, [P, NH, P]),
                                    ALU.mult).then_inc(s["t_m_dg"], 1)
            for m in range(NT + 1):
                if m < NT:
                    if m >= 2:
                        dve.wait_ge(s["t_xn"], 16 * (m - 1))
                    scale_rows(G3 + m, x2[:, m])
                if m >= 1:
                    gains(G3 + m - 1, PC["ffn"], hT, slice((m - 1) * P, m * P))

            dve.wait_ge(s["t_rw"], 64)
            dve.wait_ge(s["t_z_ix"], 2)
            link(v.tensor_copy(io_f, io_i))
            link(v.memset(gpad, -3e38))
            dve.wait_ge(s["t_rl"], 1)
            link(v.tensor_tensor(lg, psum[2][:, 0:NT * NR].rearrange("p (m r) -> p m r", m=NT),
                                 bc(br, 1, [P, NT, NR]), ALU.add))
            grp = lg[:, :, 0:NG]
            link(v.tensor_copy(gpad[:, :, 0:NG], grp))
            for m in range(NT):
                link(v.max(gmx[:, m], gpad[:, m]))
                link(v.max_index(gix[:, m], gmx[:, m], gpad[:, m]))
            v.tensor_tensor(gex, grp, gmx[:, :, 0:1].to_broadcast([P, NT, NG]), ALU.subtract).then_inc(s["t_r_dve"], 1)
            link(v.tensor_copy(gself, gix[:, :, 0]))
            link(v.tensor_tensor(goh, bc(io_f[:, 0:NG], 1, [P, NT, NG]), bc(gself, 2, [P, NT, NG]), ALU.is_equal))
            for m in range(NT):
                link(v.tensor_tensor(gsum[:, m * NG:(m + 1) * NG], lg[:, m, NG:NR].rearrange("p (g e) -> p g e", g=NG),
                                     bc(goh[:, m], 2, [P, NG, EPG]), ALU.mult))
            link(v.tensor_reduce(sel, gsum.rearrange("p (m g) e -> p m e g", g=NG), AX.X, ALU.add))
            for m in range(NT):
                link(v.max(smx[:, m], sel[:, m]))
                link(v.max_index(six[:, m], smx[:, m], sel[:, m]))
            v.tensor_tensor(wts[:, 1], smx[:, :, 1], smx[:, :, 0], ALU.subtract).then_inc(s["t_r_dve"], 1)
            for k in range(TK):
                link(v.tensor_copy(rank[:, k], six[:, :, k]))
                link(v.scalar_tensor_tensor(eid[:, k], gself, float(EPG), rank[:, k], ALU.mult, ALU.add))
                link(v.tensor_tensor(oh[k], bc(io_f, 1, [P, NT, NE]), bc(eid[:, k], 2, [P, NT, NE]), ALU.is_equal))
            link(v.tensor_tensor(asum, oh[0], oh[1], ALU.add))
            link(v.memset(apre[:, 0], 0.0))
            for m in range(1, NT):
                link(v.tensor_tensor(apre[:, m], apre[:, m - 1], asum[:, m - 1], ALU.add))
            v.tensor_copy(totf, apre[:, NT - 1]).then_inc(s["t_r_dve"], 1)
            dve.wait_ge(s["t_r_ge"], 2)
            link(v.tensor_reduce(pg, gex, AX.X, ALU.add))
            link(v.reciprocal(pg, pg))
            link(v.tensor_scalar(wts[:, 0], wts[:, 1], 1.0, None, ALU.add))
            link(v.reciprocal(wts[:, 0], wts[:, 0]))
            link(v.tensor_tensor(wts[:, 0], wts[:, 0], pg, ALU.mult))
            link(v.tensor_tensor(wts[:, 1], wts[:, 1], wts[:, 0], ALU.mult))
            dve.wait_ge(s["t_r_rk"], 1)
            for k in range(TK):
                link(v.tensor_tensor(rtmp, oh[k], psum[3][:, 0:NT * NE].rearrange("p (m e) -> p m e", m=NT), ALU.mult))
                link(v.tensor_reduce(rank[:, k], rtmp, AX.X, ALU.add))
                link(v.scalar_tensor_tensor(rank[:, k], rank[:, k], float(NE), eid[:, k], ALU.mult, ALU.add))
            link(v.tensor_reduce(totf[:, 0:1], psum[3][:, NT * NE:(NT + 1) * NE], AX.X, ALU.max))
            v.tensor_copy(toti[:, 0:1], totf[:, 0:1]).then_inc(s["t_r_dve"], 1)
            v.tensor_copy(slots, rank).then_inc(s["t_r_dve"], 1)
            dve_experts(dve, v, moe, 0)
            with overflow(dve):
                pass_end(dve, moe, 0)
                with dve.Fori(0, PASSES - 1) as p:
                    dve_experts(dve, v, moe, (p + 1) * NE)
                    pass_end(dve, moe, (p + 1) * NE)
            dve_tail3(dve, v, link, inverse_rms)

        def pe_experts(pe, mm, q, base):
            def tr(e, b):
                pe.wait_ge((q["g0"], q["g1"])[b], 8 * base + gathers(e, b))
                for k in range(2):
                    after(pe, q["ht"], 2 * base, 2 * e + (k - 1))
                    for t in range(4):
                        c = (4 * k + t) * P
                        ins = nc.tensor.transpose(psum[k][:, t * P:(t + 1) * P], hg[b][:, c:c + P], ident[:, :])
                    ins.then_inc(q["tr"], 1)

            def gate_up(e, j):
                b = j % 2
                pe.wait_ge((q["wl0"], q["wl1"], q["wl2"], q["wl3"])[j], 8 * base + weights(e, j))
                pe.wait_ge(q["ht"], 2 * base + 2 * (e + 1))
                after(pe, q["ac"], base, e - 1)
                for k in range(KT):
                    ins = mm(psum[2 + 4 * b][:, :], hgT[b][:, k], w_gu[j][:, k], start=(k == 0), stop=(k == KT - 1))
                ins.then_inc(q["gu"], 1)

            def act_tr(e, j):
                b = j % 2
                pe.wait_ge(q["ac"], base + (e + 1))
                after(pe, q["ats"], base, e)
                for k in range(FE // P):
                    ins = nc.tensor.transpose(psum[3][:, k * P:(k + 1) * P], actv[:, b, k * P:(k + 1) * P], ident[:, :])
                ins.then_inc(q["at"], 1)

            def down(e, j):
                b = j % 2
                pe.wait_ge(q["ats"], base + (e + 1))
                after(pe, q["y"], 2 * base, 2 * e)
                for hf in range(2):
                    for k in range(FE // P):
                        ins = mm(psum[4 + hf][:, :], actT[b][:, k], w_dn[j][:, k, hf * HALF:(hf + 1) * HALF],
                                 start=(k == 0), stop=(k == FE // P - 1))
                ins.then_inc(q["dn"], 1)

            def step(e, j):
                first, last = (isinstance(e, int) and e == x for x in (0, NE - 1))
                gate_up(e, j)
                if not first:
                    act_tr(e - 1, (j - 1) % NB)
                if not last:
                    tr(e + 1, (j + 1) % 2)
                if not first:
                    down(e - 1, (j - 1) % NB)

            tr(0, 0)
            each_expert(pe, step)
            act_tr(NE - 1, NB - 1)
            down(NE - 1, NB - 1)

        def pe_tail2(pe, mm, transposes):
            rows = lambda h: slice(HD * (h % 2), HD * (h % 2) + HD)
            pe.wait_ge(s["n_out"], 3 * CT)
            pe.wait_ge(s["t_wo"], 16)

            for m in range(NT + 1):
                if m < NT:
                    for hf in range(2):
                        u = 2 * m + hf
                        if u >= 3:
                            pe.wait_ge(s["t_o_e"], u - 2)
                        for k in W_ORDER[KT - CT:] if u < 2 else W_ORDER:
                            ins = mm(psum[2 + u % 3][:, :], yT[:, slot(k), m * P:(m + 1) * P],
                                     wo[:, k, hf * HALF:(hf + 1) * HALF], start=(u >= 2 and k == W_ORDER[0]),
                                     stop=(k == W_ORDER[-1]))
                        ins.then_inc(s["t_o_r"], 1)
                if m >= 1:
                    transposes(G2 + m - 1)
            pe.wait_ge(s["t_o_e"], 2 * NT)
            pe.wait_ge(s["t_mq"], 16)
            for u in range(CT * NHALF):
                c, hf = u % CT, u // CT
                pe.wait_ge(s["ht_r"], 2 * (G2 + 4 * hf + 4))
                if u >= 3:
                    pe.wait_ge(s["t_q_e"], u - 2)
                for k in range(KT):
                    ins = mm(psum[2 + u % 3][:, :], mq[:, k, c * P:(c + 1) * P], hT[:, k, hf * HALF:(hf + 1) * HALF],
                             start=(k == 0), stop=(k == KT - 1))
                ins.then_inc(s["t_q_r"], 1)
            pe.wait_ge(s["t_q_e"], CT * NHALF)
            pe.wait_ge(s["t_mo"], 16)

            def scores(m):
                if m >= 2:
                    pe.wait_ge(s["t_m_p"], m - 1)
                for h in range(NH):
                    ins = mm(psum[M_SC[m % 2][h % 2]][:, (h // 2) * ML:(h // 2 + 1) * ML],
                             mqT[rows(h), h // 2, m * P:(m + 1) * P], memk[rows(h), h // 2, :], start=True, stop=True)
                ins.then_inc(s["t_m_sc"], 1)

            def normed_transposes(m):
                pe.wait_ge(s["t_m_dg"], m + 1)
                for b in range(2):
                    if m >= 1:
                        pe.wait_ge(s["t_m_pt"], 2 * (m - 1) + b + 1)
                    for t in range(4):
                        h, k = (4 * b + t) // MT_, (4 * b + t) % MT_
                        ins = mm(psum[b][:, t * P:(t + 1) * P], m_p[m % 2][:, h, k * P:(k + 1) * P], m_dg[:, h],
                                 start=True, stop=True)
                    ins.then_inc(s["t_m_tr"], 1)

            def values(m):
                pe.wait_ge(s["t_m_pt"], 2 * (m + 1))
                if m >= 1:
                    pe.wait_ge(s["t_m_ots"], m)
                for h in range(NH):
                    for k in range(MT_):
                        ins = mm(psum[4][rows(h), (h // 2) * P:(h // 2 + 1) * P], memv[:, k, h * HD:(h + 1) * HD],
                                 m_pT[m % 2][:, h * MT_ + k], start=(k == 0), stop=(k == MT_ - 1))
                ins.then_inc(s["t_m_pv"], 1)

            def out_product(m, hf):
                pe.wait_ge(s["t_m_ots"], m + 1)
                if 2 * m + hf >= 1:
                    pe.wait_ge(s["t_m_e"], 2 * m + hf)
                for c in range(CT):
                    ins = mm(psum[3][:, :], m_oT[m % 2][:, c], mo[:, c, hf * HALF:(hf + 1) * HALF],
                             start=(c == 0), stop=(c == CT - 1))
                ins.then_inc(s["t_m_w"], 1)

            scores(0)
            for it in range(NT + 2):
                if it >= 2:
                    out_product(it - 2, 0)
                if it + 1 < NT:
                    scores(it + 1)
                if 1 <= it <= NT:
                    values(it - 1)
                if it >= 2:
                    out_product(it - 2, 1)
                if it < NT:
                    normed_transposes(it)
            pe.wait_ge(s["t_rw"], 64)
            for m in range(NT + 1):
                if m < NT:
                    transposes(G3 + m)
                if m >= 1:
                    pe.wait_ge(s["ht_r"], 2 * (G3 + m))
                    for k in range(KT):
                        ins = mm(psum[2][:, (m - 1) * NR:m * NR], hT[:, k, (m - 1) * P:m * P], wr[:, k],
                                 start=(k == 0), stop=(k == KT - 1))
            ins.then_inc(s["t_rl"], 1)
            pe.wait_ge(s["t_r_dve"], 3)
            pe.wait_ge(s["t_m_e"], 2 * NT)
            flat = lambda t: t.rearrange("p m e -> p (m e)")
            mm(psum[3][:, 0:NT * NE], triu_s[:, :], flat(asum), start=True, stop=False)
            mm(psum[3][:, 0:NT * NE], ones[:, :], flat(apre), start=False, stop=True)
            tot = psum[3][:, NT * NE:(NT + 1) * NE]
            mm(tot, ones[:, :], apre[:, NT - 1], start=True, stop=False)
            mm(tot, ones[:, :], asum[:, NT - 1], start=False, stop=True).then_inc(s["t_r_rk"], 1)
            pe.wait_ge(s["t_r_dve"], 5)
            pe_experts(pe, mm, moe, 0)
            with overflow(pe):
                pass_end(pe, moe, 0)
                with pe.Fori(0, PASSES - 1) as p:
                    pe_experts(pe, mm, moe, (p + 1) * NE)
                    pass_end(pe, moe, (p + 1) * NE)

        def pool_experts(pool, q, base, p):
            def step(e, j):
                b = j % 2
                after(pool, q["tr"], 2 * base, 2 * (e - 1))
                after(pool, (q["g0"], q["g1"])[b], 8 * base, gathers(e, b) - 16)
                nc.gpsimd.tensor_copy(idxc[:, b:b + 1], idx_all[:, bass.ds(p * NE + e, 1)]).then_inc(q["ic"], 1)
                pool.drain()
                pool.indirect_dma_start(hg[b], None, xn_d, bass.IndirectOffsetOnAxis(ap=idxc[:, b:b + 1], axis=0)
                                        ).then_inc((q["g0"], q["g1"])[b], 16)
            each_expert(pool, step)

        def pool_tail2(pool):
            pool.wait_ge(s["t_o_r"], 2 * NT)
            nc.gpsimd.iota(tokid, [[P, NT]], base=0, channel_multiplier=1).then_inc(s["t_z_ix"], 1)
            nc.gpsimd.iota(io_i, [[1, NE]], base=0, channel_multiplier=0).then_inc(s["t_z_ix"], 1)
            nc.gpsimd.memset(idx_all, 0).then_inc(s["t_z_ix"], 1)
            pool.wait_ge(s["t_z_ix"], 3)
            pool.dma_start(slot_tok.rearrange("(r q) o -> r (q o)", r=P), idx_all).then_inc(s["t_sl"], 16)
            pool.wait_ge(s["t_sl"], 16)
            pool.wait_ge(s["t_r_dve"], 5)
            for k in range(TK):
                for m in range(NT):
                    pool.indirect_dma_start(slot_tok, bass.IndirectOffsetOnAxis(ap=slots[:, k, m:m + 1], axis=0),
                                            tokid[:, m:m + 1], None).then_inc(s["t_sl"], 16)
            pool.wait_ge(s["t_sl"], 16 + 16 * TK * NT)
            pool.dma_start(idx_all.rearrange("r (p e) -> r p e", e=NE),
                           slot_tok.rearrange("(p r e) o -> r p (e o)", r=P, e=NE)).then_inc(s["t_sl"], 16)
            pool.wait_ge(s["t_sl"], 32 + 16 * TK * NT)
            pool.wait_ge(s["t_xn"], 16 * NT)
            pool_experts(pool, moe, 0, 0)
            with overflow(pool):
                pass_end(pool, moe, 0)
                with pool.Fori(0, PASSES - 1) as p:
                    pool_experts(pool, moe, (p + 1) * NE, p + 1)
                    pass_end(pool, moe, (p + 1) * NE)
                gather_outputs(pool, y_d)
            with pool.Else():
                gather_outputs(pool, y_d[0:NE * P, :])

        def gather_outputs(pool, rows):
            pool.wait_ge(moe["st0"], 8 * NE)
            pool.wait_ge(moe["st1"], 8 * NE)
            for m in range(NT):
                if m >= 4:
                    pool.wait_ge(s["f_c"], m - 3)
                for k in range(TK):
                    pool.indirect_dma_start(yg[2 * (m % 4) + k], None, rows,
                                            bass.IndirectOffsetOnAxis(ap=slots[:, k, m:m + 1], axis=0)
                                            ).then_inc((s["f_g0"], s["f_g1"], s["f_g2"], s["f_g3"])[m % 4], 16)

        G4 = G3 + NT

        def dve_tail3(dve, v, link, inverse_rms):
            dve.wait_ge(s["t_fg"], 16)
            for m in range(NT + 1):
                if m < NT:
                    dve.wait_ge((s["f_g0"], s["f_g1"], s["f_g2"], s["f_g3"])[m % 4], 32 * (m // 4 + 1))
                    for k in range(TK):
                        ins = v.scalar_tensor_tensor(x2[:, m], yg[2 * (m % 4) + k], wts[:, k, m:m + 1], x2[:, m],
                                                     ALU.mult, ALU.add)
                        link(ins) if k == 0 else ins.then_inc(s["f_c"], 1)
                if m >= 1:
                    q = m - 1
                    inverse_rms(G4 + q)
                    if q >= 2:
                        dve.wait_ge((s["f_ot0"], s["f_ot1"])[q % 2], 16 * (q // 2))
                    v.scalar_tensor_tensor(xs[q % 2], x2[:, q], rms[:, (G4 + q) % 4:(G4 + q) % 4 + 1], fin_g,
                                           ALU.mult, ALU.mult).then_inc(s["xs_r"], 1)

        def act_tail3(act, link, stats):
            for m in range(NT):
                stats(G4 + m, x2[:, m], lambda e, m=m: e.wait_ge(s["f_c"], m + 1))

        def sp_tail3(sp):
            for m in range(NT):
                sp.wait_ge(s["xs_r"], G4 + m + 1)
                sp.dma_start(out[m * P:(m + 1) * P, :], xs[m % 2]).then_inc((s["f_ot0"], s["f_ot1"])[m % 2], 16)
            sp.wait_ge(s["f_ot0"], 16 * (NT // 2))
            sp.wait_ge(s["f_ot1"], 16 * (NT // 2))
        @block.sync
        def _(sp):
            def x_tile(g):
                if g >= 2:
                    sp.wait_ge(s["xs_r"], g - 1)
                src = mem[g * P:(g + 1) * P, :] if g < MT_ else x[(g - MT_) * P:(g - MT_ + 1) * P, :]
                sp.dma_start(xin[g % 2], src).then_inc(s["x_in0"] if g % 2 == 0 else s["x_in1"], 16)

            def w_chunk(c):
                if c >= 2:
                    sp.wait_ge(s["unit_r"], END_OF[c - 2])
                src, c0, width, _p = CHUNKS[c]
                sp.dma_start(wbuf[c % 2][:, :, 0:width],
                             src[:, c0:c0 + width].rearrange("(k p) n -> p k n", p=P)).then_inc(
                                 s["w_ld0"] if c % 2 == 0 else s["w_ld1"], 16)

            x_tile(0)
            x_tile(1)
            w_chunk(0)
            w_chunk(1)
            for g in range(2, MT_ + NT):
                x_tile(g)
            for c in range(2, len(CHUNKS)):
                w_chunk(c)
            sp_tail(sp)

        @block.gpsimd
        def _(pool):
            nc.gpsimd.iota(iota_f[:], [[1, P]], base=0, channel_multiplier=0).then_inc(s["consts_i"], 1)
            nc.gpsimd.iota(iota_p[:], [[0, P]], base=0, channel_multiplier=1).then_inc(s["consts_i"], 1)
            pool.wait_ge(s["consts_v"], 2)
            for g, w in enumerate((a["lru_wa"][0], a["lru_wx"][0])):
                for h in range(NH):
                    r = slice(HD * (h % 2), HD * (h % 2) + HD)
                    pool.dma_start(lru_w[r, g * CT + h // 2, r], w[h]).then_inc(s["l_w"], 16)
            k = 0
            for n in range(NT):
                for lv in range(1, NL):
                    if lv == 1:
                        pool.wait_ge(s["g_MTs"], n + 1)
                    if k >= 2:
                        pool.wait_ge(s["g_T1"], k - 1)
                    nc.gpsimd.tensor_tensor(MTh[k % 2], gMT, bc(levT[:, lv], 1, [P, NH, P]),
                                            ALU.mult).then_inc(s["g_MTh"], 1)
                    k += 1
            pool_tail(pool)

        @block.scalar
        def _(act):
            link = chain(act, s["a_chain"])
            act.dma_start(prow[0:8, :], a["norm_mix"][0].rearrange("(r c) -> r c", c=P)).then_inc(s["params_in"], 16)
            act.dma_start(prow[8:16, :], a["norm_mem"][0].rearrange("(r c) -> r c", c=P)).then_inc(s["params_in"], 16)
            act.dma_start(prow[16:24, :], a["norm_memkv"][0].rearrange("(r c) -> r c", c=P)).then_inc(s["params_in"], 16)
            act.dma_start(prow[24:32, :], a["norm_ffn"][0].rearrange("(r c) -> r c", c=P)).then_inc(s["params_in"], 16)
            act.dma_start(prow[32:40, :], a["mix_gain"][0].rearrange("(r c) -> r c", c=P)).then_inc(s["params_in"], 16)
            act.dma_start(prow[40:48, :], a["lru_conv_w"][0].rearrange("t (r c) -> (t r) c", c=P)).then_inc(s["params_in"], 16)
            for i, v in enumerate((a["lru_conv_b"], a["lru_ba"], a["lru_bx"], a["lru_lam"])):
                act.dma_start(prow[48 + 2 * i:50 + 2 * i, :],
                              v[0].rearrange("(r c) -> r c", c=P)).then_inc(s["params_in"], 16)
            act.dma_start(prow[56:80, :], a["gdn_conv_w"][0].rearrange("t (r c) -> (t r) c", c=P)).then_inc(s["params_in"], 16)
            act.dma_start(fox_b[0:NH, :], a["fox_fb"].rearrange("a h -> h a")).then_inc(s["prm_in"], 16)
            act.dma_start(alog[:, :], a["gdn_a_log"][0:1, :].to_broadcast([P, NH])).then_inc(s["prm_in"], 16)
            act.dma_start(dtb[:, :], a["gdn_dt_bias"][0:1, :].to_broadcast([P, NH])).then_inc(s["prm_in"], 16)
            act.wait_ge(s["consts_v"], 1)

            def stats(g, src, wait):
                wait(act)
                if g >= 4:
                    act.wait_ge(s["xs_r"], g - 3)
                link(nc.scalar.activation(junk, src, ACT.Square, accum_out=ss[:, g % 4:g % 4 + 1]))
                nc.scalar.activation(rms[:, g % 4:g % 4 + 1], ss[:, g % 4:g % 4 + 1], ACT.Sqrt,
                                     bias=epsc[:, 0:1], scale=1.0 / D).then_inc(s["rms_r"], 1)

            def x_wait(g):
                return lambda e: e.wait_ge(s["x_in0"] if g % 2 == 0 else s["x_in1"], 16 * (g // 2 + 1))

            def evacuate(u):
                act.wait_ge(s["unit_r"], u + 1)
                to = UNITS[u][5]
                for i, (cols, dst) in enumerate(to):
                    rows = UNITS[u][3]
                    ins = nc.scalar.activation(dst, psum[PROJ_BANKS[u % 3]][0:rows, cols], ACT.Copy)
                    if i == len(to) - 1:
                        ins.then_inc(s["unit_e"], 1)
                    else:
                        link(ins)

            for g in range(MT_):
                stats(g, xin[g % 2], x_wait(g))
            for g in range(MT_, MT_ + NT):
                stats(g, xin[g % 2], x_wait(g))
                if g - MT_ < END_OF[1]:
                    evacuate(g - MT_)
            for u in range(END_OF[1], END_OF[5]):
                evacuate(u)

            for j in range(6):
                act.wait_ge(s["d_cvd"], j + 1)
                nc.scalar.activation(d_cv[:, j], d_cv[:, j], ACT.Silu).then_inc(s["d_sil"], 1)
            for j0 in (0, 2):
                for j in (j0, j0 + 1):
                    act.wait_ge(s["d_sil"], j + 3)
                    if j >= 2:
                        act.wait_ge(s["d_ssp"], 2 * (j - 1))
                    nc.scalar.activation(l2sq[j % 2], d_cv[:, 2 + j], ACT.Square).then_inc(s["d_sq"], 1)
                for j in (j0, j0 + 1):
                    for h in range(NHALF):
                        act.wait_ge(s["d_ssp"], 2 * j + h + 1)
                        if j >= 2:
                            act.wait_ge(s["d_l2"], j - 1)
                        link(nc.scalar.activation(l2rs[j % 2][:, h * HALF:(h + 1) * HALF],
                                                  psum[L2_BANKS[j % 2][h]][:, :], ACT.Ln, bias=epsc[:, 0:1]))
                for j in (j0, j0 + 1):
                    nc.scalar.activation(l2rs[j % 2], l2rs[j % 2], ACT.Exp, scale=-0.5).then_inc(s["d_el"], 1)
                evacuate(PRE[j0 // 2])

            act.wait_ge(s["prm_in"], 48)
            link(nc.scalar.activation(sm_e, dba[:, :, 0:NH], ACT.Exp, scale=-1.0))
            link(nc.scalar.activation(nexp[:, 0], alog[:, :], ACT.Exp))
            link(nc.scalar.activation(l_col[:, 0:CT], pcol[:, PC["lam"]:PC["lam"] + CT], ACT.Abs))
            link(nc.scalar.activation(l_col[:, 0:CT], l_col[:, 0:CT], ACT.Exp, scale=-1.0))
            nc.scalar.activation(l_col[:, 0:CT], l_col[:, 0:CT], ACT.Ln, bias=1.0).then_inc(s["l_sp"], 1)
            act.wait_ge(s["g_beta"], 1)
            link(nc.scalar.activation(Gc, sm_t, ACT.Abs))
            link(nc.scalar.activation(Gc, Gc, ACT.Exp, scale=-1.0))
            nc.scalar.activation(Gl, Gc, ACT.Ln, bias=1.0).then_inc(s["g_el"], 1)
            evacuate(PRE[2])
            act.wait_ge(s["g_Gv"], 1)
            link(nc.scalar.activation(eG, Gc, ACT.Exp))
            link(nc.scalar.activation(kds, kds, ACT.Exp))
            nc.scalar.activation(gle, Gl, ACT.Exp).then_inc(s["g_el"], 1)
            evacuate(PRE[3])

            def emptied(n, slot):
                for u, k in FILL[n, slot]:
                    if k == KT - 1:
                        evacuate(u)

            for n in range(NT):
                emptied(n, "head")
                act.wait_ge(s["g_D"], n + 1)
                if n >= 1:
                    act.wait_ge(s["g_qd"], n)
                nc.scalar.activation(eR, psum[5][:, :], ACT.Exp).then_inc(s["g_eR"], 1)
                act.wait_ge(s["g_mm"], 2 * n + 2)
                nc.scalar.activation(gam, gam, ACT.Exp, scale=-1.0).then_inc(s["g_ex"], 1)
                nc.scalar.activation(gamT, gamT, ACT.Exp).then_inc(s["g_ex"], 1)
                emptied(n, "decay")
                act.wait_ge(s["g_MT"], n + 1)
                if n >= 1:
                    act.wait_ge(s["g_MTh"], (NL - 1) * n)
                nc.scalar.activation(gMT, psum[5][:, :], ACT.Copy).then_inc(s["g_MTs"], 1)
                emptied(n, "rows")
                for lv in range(1, NL):
                    k = (NL - 1) * n + lv
                    act.wait_ge(s["g_T1"], k)
                    if k >= 2:
                        act.wait_ge(s["g_XY"], k - 1)
                    nc.scalar.activation(gT1, psum[1][:, :], ACT.Copy).then_inc(s["g_T1s"], 1)
                    emptied(n, ("half", lv))
                    emptied(n, ("joined", lv))
                    if n == NT - 1:
                        hgrn_prepare_act(act, link, lv)
                act.wait_ge(s["g_wk"], n + 1)
                if n >= 1:
                    act.wait_ge(s["g_vn"], n)
                nc.scalar.activation(wkT, psum[6][:, 0:CT * P], ACT.Copy, scale=-1.0).then_inc(s["g_wks"], 1)
                emptied(n, "new")
                emptied(n, "out")
                act.wait_ge(s["g_o"], n + 1)
                for par in range(2):
                    ins = nc.scalar.activation(d_o[:, :, n * P + par * HD:n * P + (par + 1) * HD],
                                               psum[7 - par][:, 0:GW // 2].rearrange("p (c d) -> p c d", c=CT),
                                               ACT.Copy)
                    link(ins) if par == 0 else ins.then_inc(s["g_os"], 1)
                emptied(n, "state")

            def finish_act(f, o, gate, ready):
                ready(act)
                nc.scalar.activation(fin_sq, o, ACT.Square).then_inc(s["f_sq"], 1)
                act.wait_ge(s["f_ss"], f + 1)
                nc.scalar.activation(fin_ss[:, :], fin_ss[:, :], ACT.Sqrt, bias=epsc[:, 0:1],
                                     scale=1.0 / HD).then_inc(s["f_rs"], 1)
                if gate is not None:
                    nc.scalar.activation(gate, gate, ACT.Silu).then_inc(s["f_sil"], 1)

            finish_act(0, d_o, d_z, lambda e: e.wait_ge(s["g_os"], NT))
            act_tail(act, link, stats)

        @block.vector
        def _(dve):
            v = nc.vector
            link = chain(dve, s["v_chain"])
            dve.wait_ge(s["consts_i"], 2)
            link(v.memset(epsc[:, :], EPS))
            v.tensor_tensor(xor_i[:, :], iota_f[:, :], iota_p[:, :], ALU.bitwise_xor).then_inc(s["consts_v"], 1)
            link(v.tensor_copy(fidx[:, :], iota_f[:, :]))
            link(v.tensor_copy(pidx[:, :], iota_p[:, :]))
            dve.wait_ge(s["consts_v"], 1)
            link(v.tensor_copy(xor_f[:, :], xor_i[:, :]))
            link(v.tensor_tensor(ident[:, :], fidx[:, :], pidx[:, :], ALU.is_equal))
            link(v.tensor_tensor(triu[:, :], fidx[:, :], pidx[:, :], ALU.is_ge))
            link(v.tensor_tensor(triu_s[:, :], fidx[:, :], pidx[:, :], ALU.is_gt))
            link(v.tensor_tensor(tril_s[:, :], fidx[:, :], pidx[:, :], ALU.is_lt))
            link(v.tensor_scalar(negmask[:, :], triu_s[:, :], -1e30, None, ALU.mult))
            link(v.memset(ones[:, :], 1.0))
            link(v.tensor_scalar(tmp_mask[:, :], pidx[:, :], float(HD), None, ALU.is_ge))
            link(v.scalar_tensor_tensor(head_ones[:, :], fidx[:, :], float(HD), tmp_mask[:, :],
                                        ALU.is_ge, ALU.is_equal))
            for lv, h in enumerate(LEVELS):
                link(v.scalar_tensor_tensor(tmp_mask[:, :], xor_f[:, :], float(h), triu_s[:, :], ALU.is_ge, ALU.mult))
                link(v.scalar_tensor_tensor(levT[:, lv], xor_f[:, :], float(2 * h), tmp_mask[:, :],
                                            ALU.is_lt, ALU.mult))
            link(v.tensor_copy(levT[:, NL], ident[:, :]))
            link(v.scalar_tensor_tensor(lev1[:, :], xor_f[:, :], 2.0, tril_s[:, :], ALU.is_lt, ALU.mult))
            link(v.memset(d_raw[:, :, 0:PAD], 0.0))
            link(v.memset(c_x[:, :, 0:PAD], 0.0))
            link(v.memset(lru_w[:, :, :], 0.0))
            v.memset(gS[:, :, :], 0.0).then_inc(s["consts_v"], 1)
            dve.wait_ge(s["pcol_t"], 1)
            link(v.tensor_copy(pcol[:, :], psum[7][:, 0:80]))

            def inverse_rms(g):
                dve.wait_ge(s["rms_r"], g + 1)
                link(v.reciprocal(rms[:, g % 4:g % 4 + 1], rms[:, g % 4:g % 4 + 1]))

            def scale_rows(g, src):
                if g >= 2:
                    dve.wait_ge(s["tr_r"], 2 * (g - 1))
                inverse_rms(g)
                v.tensor_scalar(xs[g % 2], src, rms[:, g % 4:g % 4 + 1], None, ALU.mult).then_inc(s["xs_r"], 1)

            def gains(g, gain, dst, cols):
                for b in range(2):
                    dve.wait_ge(s["tr_r"], 2 * g + b + 1)
                    v.tensor_tensor(dst[:, 4 * b:4 * b + 4, cols], psum[b][:, :].rearrange("p (k t) -> p k t", k=4),
                                    bc(pcol[:, gain + 4 * b:gain + 4 * b + 4], 2, [P, 4, P]),
                                    ALU.mult).then_inc(s["ht_r"], 1)

            for lo, hi in ((0, MT_), (MT_, MT_ + NT)):
                for g in range(lo, hi + 1):
                    if g < hi:
                        scale_rows(g, xin[g % 2])
                    q = g - 1
                    if q >= lo and lo == 0:
                        gains(q, PC["memkv"], memT, slice(q * P, (q + 1) * P))
                    elif q >= lo:
                        gains(q, PC["mix"], hT, slice((q - MT_) * P, (q - MT_ + 1) * P))

            for j in range(6):
                if j % 2 == 0:
                    dve.wait_ge(s["unit_e"], END_OF[4 - j // 2])
                grp, ct = 2 - j // 2, j % 2
                w = lambda t: pcol[:, PC["gconv"] + 6 * t + 2 * grp + ct:PC["gconv"] + 6 * t + 2 * grp + ct + 1]
                link(v.tensor_scalar(d_cv[:, j], d_raw[:, j, 0:T], w(0), None, ALU.mult))
                for t in range(1, TAPS):
                    ins = v.scalar_tensor_tensor(d_cv[:, j], d_raw[:, j, t:t + T], w(t), d_cv[:, j], ALU.mult, ALU.add)
                    if t < TAPS - 1:
                        link(ins)
                    else:
                        ins.then_inc(s["d_cvd"], 1)
            for j in range(4):
                dve.wait_ge(s["d_el"], j + 1)
                v.scalar_tensor_tensor(d_cv[:, 2 + j], d_cv[:, 2 + j], 1.0 if j < 2 else QK_SCALE, l2rs[j % 2],
                                       ALU.mult, ALU.mult).then_inc(s["d_l2"], 1)
            dve.wait_ge(s["unit_e"], END_OF[5])
            dve.wait_ge(s["prm_in"], 48)
            v.tensor_tensor(sm_t, dba[:, :, NH:2 * NH], bc(dtb[:, :], 1, [P, NT, NH]), ALU.add).then_inc(s["g_beta"], 1)
            dve.wait_ge(s["g_el"], 1)
            link(v.tensor_scalar(sm_e, sm_e, 1.0, None, ALU.add))
            link(v.reciprocal(beta, sm_e))
            link(v.scalar_tensor_tensor(sm_t, sm_t, 0.0, Gl, ALU.max, ALU.add))
            v.scalar_tensor_tensor(gg, sm_t, -1.0, bc(nexp[:, 0], 1, [P, NT, NH]), ALU.mult,
                                   ALU.mult).then_inc(s["g_beta"], 1)
            dve.wait_ge(s["g_Gp"], 1)
            gp = psum[5]
            link(v.tensor_copy(Gc, gp[:, 0:NHT].rearrange("p (n h) -> p n h", h=NH)))
            link(v.tensor_copy(Gl, gp[:, NHT:2 * NHT].rearrange("p (n h) -> p n h", h=NH)))
            v.tensor_tensor(kds, Gl, Gc, ALU.subtract).then_inc(s["g_Gv"], 1)
            dve.wait_ge(s["g_el"], 2)
            link(v.tensor_tensor(beG, beta, eG, ALU.mult))
            link(v.tensor_copy(glS[0:HD, :, :], gle[0:HD, :, 0:NH:2]))
            v.tensor_copy(glS[HD:P, :, :], gle[HD:P, :, 1:NH:2]).then_inc(s["g_cols"], 1)
            dve.wait_ge(s["g_cols"], 1)
            dve.wait_ge(s["l_sp"], 1)
            link(v.tensor_scalar(l_col[:, 2:4], pcol[:, PC["lam"]:PC["lam"] + CT], -1.0, 0.0, ALU.mult, ALU.max))
            link(v.tensor_tensor(l_col[:, 0:2], l_col[:, 0:2], l_col[:, 2:4], ALU.add))
            link(v.tensor_scalar(l_col[:, 2:4], l_col[:, 0:2], -LRU_C, None, ALU.mult))
            v.tensor_scalar(l_col[:, 4:6], l_col[:, 0:2], LRU_C, None, ALU.mult).then_inc(s["l_sp"], 1)

            for n in range(NT):
                tok = slice(n * P, (n + 1) * P)
                col = lambda c, w: bc(c[:, n], 2, [P, NH, w])
                b5, b6, b7 = [psum[i][:, :].rearrange("p (h t) -> p h t", h=NH) for i in (5, 6, 7)]
                dve.wait_ge(s["g_R"], n + 1)
                v.tensor_tensor(gD, b5, col(Gc, P), ALU.subtract).then_inc(s["g_D"], 1)
                dve.wait_ge(s["g_D"], n + 1)
                v.tensor_scalar(gam, gD, 0.0, None, ALU.max).then_inc(s["g_mm"], 1)
                v.tensor_scalar(gamT, gD, 0.0, None, ALU.min).then_inc(s["g_mm"], 1)
                dve.wait_ge(s["g_KV"], n + 1)
                b0 = psum[0][:, :].rearrange("p (w h d) -> p w h d", w=2, h=NH)
                link(v.tensor_tensor(kvb[:, :, 0:HD], b0[:, 1], col(beta, HD), ALU.mult))
                link(v.tensor_tensor(kvb[:, :, HD:P], b0[:, 0], col(beG, HD), ALU.mult))
                v.tensor_tensor(kdec, b0[:, 0], col(kds, HD), ALU.mult).then_inc(s["g_kv"], 1)
                dve.wait_ge(s["g_ex"], 2 * n + 2)
                link(v.tensor_tensor(gam, gam, bc(tril_s[:, :], 1, [P, NH, P]), ALU.mult))
                link(v.tensor_tensor(gam, gam, col(beta, P), ALU.mult))
                dve.wait_ge(s["g_KK"], n + 1)
                link(v.tensor_tensor(gM[:, 0:NH:2], b6[:, 0:2], gam[:, 0:NH:2], ALU.mult))
                v.tensor_tensor(gM[:, 1:NH:2], b7[:, 0:2], gam[:, 1:NH:2], ALU.mult).then_inc(s["g_M"], 1)
                dve.wait_ge(s["g_M"], n + 1)
                link(v.tensor_tensor(gX, gM, bc(lev1[:, :], 1, [P, NH, P]), ALU.mult))
                link(v.tensor_tensor(gX, bc(ident[:, :], 1, [P, NH, P]), gX, ALU.subtract))
                link(v.tensor_tensor(gamT, gamT, bc(triu[:, :], 1, [P, NH, P]), ALU.mult))
                dve.wait_ge(s["g_MTs"], n + 1)
                link(v.tensor_tensor(gY, gMT, bc(levT[:, 0], 1, [P, NH, P]), ALU.mult))
                v.tensor_tensor(gY, bc(ident[:, :], 1, [P, NH, P]), gY, ALU.subtract).then_inc(s["g_upd"], 1)
                link(v.tensor_tensor(gAT[:, 0:NH:2], b6[:, 2:4], gamT[:, 0:NH:2], ALU.mult))
                v.tensor_tensor(gAT[:, 1:NH:2], b7[:, 2:4], gamT[:, 1:NH:2], ALU.mult).then_inc(s["g_AT"], 1)
                dve.wait_ge(s["g_eR"], n + 1)
                for h in range(NH):
                    r = slice(HD * (h % 2), HD * (h % 2) + HD)
                    ins = v.tensor_tensor(qd[r, h // 2], d_cv[r, 4 + h // 2, tok], eR[r, h], ALU.mult)
                    ins.then_inc(s["g_qd"], 1) if h == NH - 1 else link(ins)
                for lv in range(1, NL):
                    k = (NL - 1) * n + lv
                    dve.wait_ge(s["g_upd"], NL * n + lv)
                    dve.wait_ge(s["g_XY"], k)
                    if lv < NL - 1:
                        link(v.tensor_tensor(gX, gX, b7, ALU.subtract))
                    v.tensor_tensor(gY, gY, b5, ALU.subtract).then_inc(s["g_upd"], 1)
                    if n == NT - 1:
                        hgrn_prepare_dve(dve, v, link, lv)
                dve.wait_ge(s["g_vn"], n + 1)
                for par in range(2):
                    ins = v.tensor_copy(vnew[:, par:NH:2, :],
                                        psum[1 - par][:, 0:GW // 2].rearrange("p (h d) -> p h d", d=HD))
                    link(ins) if par == 0 else ins.then_inc(s["g_vns"], 1)
                dve.wait_ge(s["g_dS"], n + 1)
                link(v.tensor_tensor(gS[:, :, :], gS[:, :, :], bc(glS[:, n], 2, [P, CT, HD]), ALU.mult))
                v.tensor_tensor(gS[:, :, :], gS[:, :, :], psum[5][:, 0:CT * HD].rearrange("p (c d) -> p c d", c=CT),
                                ALU.add).then_inc(s["g_S"], 1)

            def finish_dve(f, o, gate, c0):
                heads = lambda t: t.rearrange("p c (g d) -> p (c g) d", d=HD)
                dve.wait_ge(s["f_sq"], f + 1)
                v.tensor_reduce(fin_ss[:, :], heads(fin_sq), AX.X, ALU.add).then_inc(s["f_ss"], 1)
                dve.wait_ge(s["f_rs"], f + 1)
                link(v.reciprocal(fin_ss[:, :], fin_ss[:, :]))
                G = NT * 2
                for c in range(CT):
                    oh = o[:, c].rearrange("p (g d) -> p g d", d=HD)
                    ins = v.tensor_tensor(oh, oh, bc(fin_ss[:, c * G:(c + 1) * G], 2, [P, G, HD]), ALU.mult)
                    if gate is None:
                        ins.then_inc(s["f_y"], 1)
                        continue
                    link(ins)
                    if c == 0:
                        dve.wait_ge(s["f_sil"], f + 1)
                    ot = o[:, c].rearrange("p (n q) -> p n q", q=P)
                    v.tensor_tensor(ot, ot, gate[:, :, c * P:(c + 1) * P], ALU.mult).then_inc(s["f_y"], 1)
                fox_logits_dve(dve, v, link)
                for k in range(2):
                    hgrn_level(dve, v, link, k)
                for c in range(CT):
                    for hf in range(2):
                        i = (f * CT + c) * 2 + hf
                        dve.wait_ge(s["f_tr"], i + 1)
                        v.tensor_scalar(yT[:, slot(c0 + c), hf * HALF:(hf + 1) * HALF], psum[i % 2][:, :],
                                        pcol[:, PC["gain"] + c0 + c:PC["gain"] + c0 + c + 1], None,
                                        ALU.mult).then_inc(s["f_out"], 1)

            dve.wait_ge(s["h_act"], 4)
            v.tensor_tensor(h_lf, h_lf, a_f, ALU.mult).then_inc(s["h_dve"], 1)
            finish_dve(0, d_o, d_z, 6)
            dve_tail(dve, v, link, scale_rows, gains, inverse_rms)

        @block.tensor
        def _(pe):
            mm = nc.tensor.matmul
            pe.wait_ge(s["consts_v"], 2)
            pe.wait_ge(s["params_in"], 16 * 11)
            nc.tensor.transpose(psum[7][:, 0:80], prow[0:80, :], ident[0:80, 0:80]).then_inc(s["pcol_t"], 1)

            def transposes(g):
                pe.wait_ge(s["xs_r"], g + 1)
                for b in range(2):
                    if g >= 1:
                        pe.wait_ge(s["ht_r"], 2 * (g - 1) + b + 1)
                    for k in range(4):
                        c = (4 * b + k) * P
                        ins = nc.tensor.transpose(psum[b][:, k * P:(k + 1) * P], xs[g % 2][:, c:c + P], ident[:, :])
                    ins.then_inc(s["tr_r"], 1)

            def unit(u, ks=range(KT)):
                c, lhs, rhs, rows, n, _to = UNITS[u]
                for k in ks:
                    if k == 0 and (u == 0 or UNITS[u - 1][0] != c):
                        pe.wait_ge(s["w_ld0"] if c % 2 == 0 else s["w_ld1"], 16 * (c // 2 + 1))
                    if k == 0 and u >= 3:
                        pe.wait_ge(s["unit_e"], u - 2)
                    ins = mm(psum[PROJ_BANKS[u % 3]][0:rows, 0:n], lhs(k), rhs(k), start=(k == 0), stop=(k == KT - 1))
                    if k == KT - 1:
                        ins.then_inc(s["unit_r"], 1)

            for g in range(MT_):
                transposes(g)
            pe.wait_ge(s["ht_r"], 2 * MT_)
            for g in range(MT_, MT_ + NT):
                if g - MT_ < END_OF[1]:
                    unit(g - MT_)
                transposes(g)
            pe.wait_ge(s["ht_r"], 2 * (MT_ + NT))
            for u in range(END_OF[1], END_OF[5]):
                unit(u)
            for j in range(4):
                pe.wait_ge(s["d_sq"], j + 1)
                if j >= 2:
                    pe.wait_ge(s["d_el"], j - 1)
                for h in range(NHALF):
                    mm(psum[L2_BANKS[j % 2][h]][:, :], head_ones[:, :], l2sq[j % 2][:, h * HALF:(h + 1) * HALF],
                       start=True, stop=True).then_inc(s["d_ssp"], 1)
                if j % 2 == 1:
                    unit(PRE[j // 2])
            unit(PRE[2])
            pe.wait_ge(s["g_beta"], 2)
            pe.wait_ge(s["d_el"], 4)
            mm(psum[5][:, 0:NHT], triu[:, :], gg.rearrange("p n h -> p (n h)"), start=True, stop=True)
            mm(psum[5][:, NHT:2 * NHT], ones[:, :], gg.rearrange("p n h -> p (n h)"), start=True,
               stop=True).then_inc(s["g_Gp"], 1)
            unit(PRE[3])
            pe.wait_ge(s["d_l2"], 4)
            pe.wait_ge(s["g_cols"], 1)

            def fill(n, slot):
                for u, k in FILL[n, slot]:
                    unit(u, [k])

            for n in range(NT):
                tok = slice(n * P, (n + 1) * P)
                rows = lambda h: slice(HD * (h % 2), HD * (h % 2) + HD)
                hp = lambda h: slice(h * P, (h + 1) * P)
                hd = lambda h: slice(h * HD, (h + 1) * HD)
                if n >= 1:
                    pe.wait_ge(s["g_S"], n)
                for h in range(NH):
                    ins = mm(psum[5][:, hp(h)], gg[:, n, h:h + 1].to_broadcast([P, P]), triu[:, :],
                             start=True, stop=True)
                ins.then_inc(s["g_R"], 1)
                fill(n, "head")
                if n >= 1:
                    pe.wait_ge(s["g_os"], n)
                for h in range(NH):
                    bank = psum[6 + h % 2]
                    mm(bank[:, hp(h // 2)], d_cv[rows(h), 2 + h // 2, tok], d_cv[rows(h), 2 + h // 2, tok],
                       start=True, stop=True)
                    ins = mm(bank[:, hp(2 + h // 2)], d_cv[rows(h), 2 + h // 2, tok], d_cv[rows(h), 4 + h // 2, tok],
                             start=True, stop=True)
                ins.then_inc(s["g_KK"], 1)
                if n >= 1:
                    pe.wait_ge(s["g_vns"], n)
                for c in range(4):
                    j = 2 + c if c < 2 else c - 2
                    ins = nc.tensor.transpose(psum[0][:, hp(c)], d_cv[:, j, tok], ident[:, :])
                ins.then_inc(s["g_KV"], 1)
                fill(n, "decay")
                pe.wait_ge(s["g_M"], n + 1)
                pe.wait_ge(s["g_eR"], n + 1)
                pe.wait_ge(s["g_D"], n + 1)
                for h in range(NH):
                    ins = nc.tensor.transpose(psum[5][:, hp(h)], gM[:, h], ident[:, :])
                ins.then_inc(s["g_MT"], 1)
                fill(n, "rows")
                for lv in range(1, NL):
                    k = (NL - 1) * n + lv
                    pe.wait_ge(s["g_MTh"], k)
                    pe.wait_ge(s["g_upd"], NL * n + lv)
                    for h in range(NH):
                        ins = mm(psum[1][:, hp(h)], MTh[(k - 1) % 2][:, h], gX[:, h], start=True, stop=True)
                    ins.then_inc(s["g_T1"], 1)
                    fill(n, ("half", lv))
                    if n == NT - 1 and lv == 1:
                        fox_logits_pe(pe)
                    pe.wait_ge(s["g_T1s"], k)
                    if lv == 1:
                        pe.wait_ge(s["g_MTs"], n + 1)
                        pe.wait_ge(s["g_AT"], n + 1)
                    if lv < NL - 1:
                        for h in range(NH):
                            mm(psum[7][:, hp(h)], gY[:, h], gT1[:, h], start=True, stop=True)
                    for h in range(NH):
                        ins = mm(psum[5][:, hp(h)], gT1[:, h], gY[:, h], start=True, stop=True)
                    ins.then_inc(s["g_XY"], 1)
                    fill(n, ("joined", lv))
                pe.wait_ge(s["g_upd"], NL * n + NL)
                pe.wait_ge(s["g_kv"], n + 1)
                for h in range(NH):
                    ins = mm(psum[6][rows(h), (h // 2) * P:(h // 2 + 1) * P], kvb[:, h, HD:P], gY[:, h],
                             start=True, stop=True)
                ins.then_inc(s["g_wk"], 1)
                fill(n, "new")
                pe.wait_ge(s["g_wks"], n + 1)
                pe.wait_ge(s["g_S"], n) if n >= 1 else None
                for h in range(NH):
                    bank = psum[1 - h % 2]
                    mm(bank[:, hd(h // 2)], gY[:, h], kvb[:, h, 0:HD], start=True, stop=False)
                    ins = mm(bank[:, hd(h // 2)], wkT[rows(h), h // 2], gS[rows(h), h // 2], start=False, stop=True)
                ins.then_inc(s["g_vn"], 1)
                fill(n, "out")
                pe.wait_ge(s["g_vns"], n + 1)
                pe.wait_ge(s["g_qd"], n + 1)
                for h in range(NH):
                    bank = psum[7 - h % 2]
                    mm(bank[:, hd(h // 2)], qd[rows(h), h // 2], gS[rows(h), h // 2], start=True, stop=False)
                    ins = mm(bank[:, hd(h // 2)], gAT[:, h], vnew[:, h], start=False, stop=True)
                ins.then_inc(s["g_o"], 1)
                for h in range(NH):
                    ins = mm(psum[5][rows(h), (h // 2) * HD:(h // 2 + 1) * HD], kdec[:, h], vnew[:, h],
                             start=True, stop=True)
                ins.then_inc(s["g_dS"], 1)
                fill(n, "state")

            def finish_pe(f, o):
                pe.wait_ge(s["f_y"], CT * (f + 1))
                for c in range(CT):
                    for hf in range(2):
                        i = (f * CT + c) * 2 + hf
                        if i >= 2:
                            pe.wait_ge(s["f_out"], i - 1)
                        for t in range(4):
                            n = 4 * hf + t
                            ins = nc.tensor.transpose(psum[i % 2][:, t * P:(t + 1) * P], o[:, c, n * P:(n + 1) * P],
                                                      ident[:, :])
                        ins.then_inc(s["f_tr"], 1)

            hgrn_states_pe(pe, mm)
            finish_pe(0, d_o)
            pe_tail(pe, mm, transposes)


_INS = ["x", "mem", "norm_mix", "w_in", "hgrn_lb", "fox_fb", "lru_conv_w", "lru_conv_b", "lru_wa", "lru_ba", "lru_wx",
        "lru_bx", "lru_lam", "gdn_conv_w", "gdn_a_log", "gdn_dt_bias", "mix_gain", "w_out", "norm_mem", "norm_memkv",
        "w_mq", "w_mkv", "w_mo", "norm_ffn", "w_rg", "b_rg", "w_re", "b_re", "w_e_gu", "w_e_dn", "norm_final"]


def kernel(**inputs):
    import numpy as np
    import concourse.bacc as bacc
    from concourse.bass_utils import run_bass_kernel_spmd

    nc = bacc.Bacc("TRN2", target_bir_lowering=False, num_devices=1)
    arrays, aps = {}, {}
    for name in _INS:
        v = np.ascontiguousarray(inputs[name])
        arrays[f"in_{name}"] = v
        aps[name] = nc.dram_tensor(f"in_{name}", v.shape, mybir.dt.from_np(v.dtype), kind="ExternalInput").ap()
    T, D = inputs["x"].shape[1:]
    out = nc.dram_tensor("out_0", (T, D), mybir.dt.float32, kind="ExternalOutput").ap()
    hybrid_trunk(nc, aps, out)
    r = run_bass_kernel_spmd(nc, [arrays], core_ids=[0])
    return r.results[0]["out_0"].reshape(1, T, D)
```
